# Optimizing a Trainium2 kernel written in Bass

```python
import math
import jax
import jax.numpy as jnp
from jax import lax
import numpy as np
import jax, jax.numpy as jnp

D_MODEL = 1024
BATCH = 1
SEQ = 1024
DEPTH = 1

GRID_W = 64
CTX_LEN = 256
EPS = 1e-6
DA_HEADS = 4
DA_D = 64
DA_DV = 2 * DA_D
ROPE_AXIS_DIM = DA_D // 2
ROPE_THETA = 10000.0
Q_BLOCK = 128
GDN_HEADS = 4
GDN_DK = 128
GDN_DV = 128
CONV_K = 3
CHUNK = 64
N_EXPERTS = 16
EXPERT_FF = 1024
CAP_FACTOR = 2
DA_QK = DA_HEADS * 2 * DA_D
DA_V = DA_HEADS * DA_DV
GDN_QK = GDN_HEADS * GDN_DK
GDN_V = GDN_HEADS * GDN_DV
GDN_QKV = 2 * GDN_QK + GDN_V
GDN_AB = 2 * 2 * GDN_HEADS
D_MIX = DA_V + GDN_V
IN_SPLIT_POINTS = (DA_QK, 2 * DA_QK, 2 * DA_QK + DA_V, 2 * DA_QK + DA_V + GDN_QKV, 2 * DA_QK + DA_V + GDN_QKV + GDN_V)
IN_COLS = 2 * DA_QK + DA_V + GDN_QKV + GDN_V + GDN_AB


def rms_norm(x, g):
    xf = x.astype(jnp.float32)
    y = xf * lax.rsqrt(jnp.mean(xf * xf, axis=-1, keepdims=True) + EPS)
    return (y * g.astype(jnp.float32)).astype(x.dtype)

def modulate(x, g, shift, scale):
    return rms_norm(x, g) * (1.0 + scale) + shift

def l2_normalize(t):
    tf = t.astype(jnp.float32)
    return (tf * lax.rsqrt(jnp.sum(tf * tf, axis=-1, keepdims=True) + EPS)).astype(t.dtype)

def rope_axis(x, ang):
    cos = jnp.cos(ang).astype(x.dtype)[:, None, None, :]
    sin = jnp.sin(ang).astype(x.dtype)[:, None, None, :]
    x1, x2 = jnp.split(x, 2, axis=-1)
    return jnp.concatenate([x1 * cos - x2 * sin, x2 * cos + x1 * sin], axis=-1)

def rope_2d(x, ang_row, ang_col):
    xr, xc = jnp.split(x, 2, axis=-1)
    return jnp.concatenate([rope_axis(xr, ang_row), rope_axis(xc, ang_col)], axis=-1)

def diff_attn(q, k, v, lam):
    B, L = q.shape[:2]
    nblk = L // Q_BLOCK
    qb = jnp.moveaxis((q * DA_D ** -0.5).reshape(B, nblk, Q_BLOCK, DA_HEADS, 2, DA_D), 1, 0)

    def block(qi):
        s = jnp.einsum('bqhid,bkhid->bhiqk', qi, k).astype(jnp.float32)
        p = jax.nn.softmax(s, axis=-1)
        a = (p[:, :, 0] - lam * p[:, :, 1]).astype(v.dtype)
        return jnp.einsum('bhqk,bkhe->bqhe', a, v)

    o = lax.map(block, qb)
    return jnp.moveaxis(o, 0, 1).reshape(B, L, DA_HEADS, DA_DV)

def short_conv(x, w):
    L = x.shape[1]
    p = CONV_K // 2
    xp = jnp.pad(x, ((0, 0), (p, p), (0, 0)))
    return jax.nn.silu(sum(xp[:, i:i + L] * w[i] for i in range(CONV_K)))

def gdn_inputs(qkv, ab, conv_w, a_log, dt_bias):
    B, L = qkv.shape[:2]
    q, k, v = jnp.split(short_conv(qkv, conv_w), [GDN_QK, 2 * GDN_QK], axis=-1)
    q = l2_normalize(q.reshape(B, L, GDN_HEADS, GDN_DK)) * GDN_DK ** -0.5
    k = l2_normalize(k.reshape(B, L, GDN_HEADS, GDN_DK))
    v = v.reshape(B, L, GDN_HEADS, GDN_DV)
    ab = ab.reshape(B, L, 2, 2, GDN_HEADS).astype(jnp.float32)
    g = -jnp.exp(a_log.astype(jnp.float32)) * jax.nn.softplus(ab[:, :, 0] + dt_bias.astype(jnp.float32))
    beta = jax.nn.sigmoid(ab[:, :, 1])
    return q, k, v, g, beta

def gdn_chunked(q, k, v, g, beta, s0, need_out):
    B, L, H, dk = k.shape
    dv = v.shape[-1]
    n = L // CHUNK
    f32 = jnp.float32

    def chunks(t):
        t = t.astype(f32).reshape(B, n, CHUNK, *t.shape[2:])
        return jnp.moveaxis(t, (1, 3), (0, 2))

    kc, vc, gc, bc = chunks(k), chunks(v), chunks(g), chunks(beta)
    Gc = jnp.cumsum(gc, axis=-1)
    diff = Gc[..., :, None] - Gc[..., None, :]
    idx = jnp.arange(CHUNK)
    strict = idx[:, None] > idx[None, :]
    dec_strict = jnp.where(strict, jnp.exp(jnp.where(strict, diff, 0.0)), 0.0)
    a_mat = jnp.eye(CHUNK, dtype=f32) + bc[..., None] * jnp.einsum('nbhid,nbhjd->nbhij', kc, kc) * dec_strict
    rhs = jnp.concatenate([(bc * jnp.exp(Gc))[..., None] * kc, bc[..., None] * vc], axis=-1)
    sol = lax.linalg.triangular_solve(a_mat, rhs, left_side=True, lower=True, unit_diagonal=True)
    w, ub = sol[..., :dk], sol[..., dk:]
    kd = kc * jnp.exp(Gc[..., -1:] - Gc)[..., None]
    g_last = jnp.exp(Gc[..., -1])[..., None, None]

    if need_out:
        qc = chunks(q)
        incl = idx[:, None] >= idx[None, :]
        dec_incl = jnp.where(incl, jnp.exp(jnp.where(incl, diff, 0.0)), 0.0)
        qd = qc * jnp.exp(Gc)[..., None]
        aqk = jnp.einsum('nbhid,nbhjd->nbhij', qc, kc) * dec_incl

        def step(s, xs):
            w_n, ub_n, kd_n, gl_n, qd_n, aqk_n = xs
            u = ub_n - jnp.einsum('bhcd,bhde->bhce', w_n, s)
            o = jnp.einsum('bhcd,bhde->bhce', qd_n, s) + jnp.einsum('bhij,bhje->bhie', aqk_n, u)
            return gl_n * s + jnp.einsum('bhcd,bhce->bhde', kd_n, u), o

        s_fin, o = lax.scan(step, s0, (w, ub, kd, g_last, qd, aqk))
        o = jnp.moveaxis(o, (0, 2), (1, 3)).reshape(B, L, H, dv).astype(v.dtype)
        return o, s_fin

    def step_state(s, xs):
        w_n, ub_n, kd_n, gl_n = xs
        u = ub_n - jnp.einsum('bhcd,bhde->bhce', w_n, s)
        return gl_n * s + jnp.einsum('bhcd,bhce->bhde', kd_n, u), None

    s_fin, _ = lax.scan(step_state, s0, (w, ub, kd, g_last))
    return None, s_fin

def bidirectional_gdn(lat, ctx_in, need_ctx_out):
    ql, kl, vl, gl, bl = lat
    qc, kc, vc, gc, bc = ctx_in
    B = ql.shape[0]
    o_lat, o_ctx = None, None
    for d in range(2):
        rev = (lambda t: jnp.flip(t, axis=1)) if d == 1 else (lambda t: t)
        s0 = jnp.zeros((B, GDN_HEADS, GDN_DK, GDN_DV), jnp.float32)
        oc, s_ctx = gdn_chunked(rev(qc), rev(kc), rev(vc), rev(gc[:, :, d]), rev(bc[:, :, d]), s0, need_ctx_out)
        ol, _ = gdn_chunked(rev(ql), rev(kl), rev(vl), rev(gl[:, :, d]), rev(bl[:, :, d]), s_ctx, True)
        o_lat = rev(ol) if o_lat is None else o_lat + rev(ol)
        if need_ctx_out:
            o_ctx = rev(oc) if o_ctx is None else o_ctx + rev(oc)
    return o_lat, o_ctx

def gdn_output(o, gate, gdn_norm_g):
    B, L = o.shape[:2]
    y = rms_norm(o, gdn_norm_g) * jax.nn.silu(gate.reshape(B, L, GDN_HEADS, GDN_DV))
    return y.reshape(B, L, GDN_V)

def expert_choice_ffn(h, w_router, w_gate, w_up, w_down):
    def route_set(t):
        n = t.shape[0]
        cap = CAP_FACTOR * n // N_EXPERTS
        aff = jax.nn.softmax((t @ w_router).astype(jnp.float32), axis=-1)
        gate, idx = lax.top_k(aff.T, cap)
        xe = t[idx]
        hid = jax.nn.silu(jnp.einsum('ecd,edf->ecf', xe, w_gate)) * jnp.einsum('ecd,edf->ecf', xe, w_up)
        ye = jnp.einsum('ecf,efd->ecd', hid, w_down) * gate[..., None].astype(t.dtype)
        return jnp.zeros_like(t).at[idx.reshape(-1)].add(ye.reshape(-1, t.shape[-1]))

    return jax.vmap(route_set)(h)

def hybrid_layer(x, xc, c, c_ctx, ang_row, ang_col, lam_init, last,
                 w_mod, b_mod, norm1_g, w_in, conv_w, a_log, dt_bias, gdn_norm_g,
                 lam_q1, lam_k1, lam_q2, lam_k2, da_subln_g, w_out, norm2_g,
                 w_router, w_gate, w_up, w_down):
    B, L, _ = x.shape
    Lc = xc.shape[1]
    sh1, sc1, gt1, sh2, sc2, gt2 = jnp.split((jax.nn.silu(c) @ w_mod + b_mod)[:, None, :], 6, axis=-1)
    sh1c, sc1c, gt1c, sh2c, sc2c, gt2c = jnp.split(jax.nn.silu(c_ctx) @ w_mod + b_mod, 6, axis=-1)

    p = modulate(x, norm1_g, sh1, sc1) @ w_in
    pc = modulate(xc, norm1_g, sh1c, sc1c) @ w_in
    q, k, v, qkv, gate, ab = jnp.split(p, IN_SPLIT_POINTS, axis=-1)
    qc, kc, vc, qkvc, gatec, abc = jnp.split(pc, IN_SPLIT_POINTS, axis=-1)

    lam = (jnp.exp(jnp.sum(lam_q1 * lam_k1, dtype=jnp.float32))
           - jnp.exp(jnp.sum(lam_q2 * lam_k2, dtype=jnp.float32)) + lam_init)
    k_c = kc.reshape(B, Lc, DA_HEADS, 2, DA_D)
    v_c = vc.reshape(B, Lc, DA_HEADS, DA_DV)
    q_l = rope_2d(q.reshape(B, L, DA_HEADS, 2, DA_D), ang_row, ang_col)
    k_l = rope_2d(k.reshape(B, L, DA_HEADS, 2, DA_D), ang_row, ang_col)
    o_da = diff_attn(q_l, jnp.concatenate([k_c, k_l], axis=1),
                     jnp.concatenate([v_c, v.reshape(B, L, DA_HEADS, DA_DV)], axis=1), lam)
    o_da = (rms_norm(o_da, da_subln_g) * (1.0 - lam_init)).reshape(B, L, DA_V)

    o_gdn_l, o_gdn_c = bidirectional_gdn(gdn_inputs(qkv, ab, conv_w, a_log, dt_bias),
                                         gdn_inputs(qkvc, abc, conv_w, a_log, dt_bias), not last)
    o_gdn = gdn_output(o_gdn_l, gate, gdn_norm_g)

    x_new = x + gt1 * (jnp.concatenate([o_da, o_gdn], axis=-1) @ w_out)
    x_new = x_new + gt2 * expert_choice_ffn(modulate(x_new, norm2_g, sh2, sc2), w_router, w_gate, w_up, w_down)

    if not last:
        o_da_c = diff_attn(qc.reshape(B, Lc, DA_HEADS, 2, DA_D), k_c, v_c, lam)
        o_da_c = (rms_norm(o_da_c, da_subln_g) * (1.0 - lam_init)).reshape(B, Lc, DA_V)
        xc = xc + gt1c * (jnp.concatenate([o_da_c, gdn_output(o_gdn_c, gatec, gdn_norm_g)], axis=-1) @ w_out)
        xc = xc + gt2c * expert_choice_ffn(modulate(xc, norm2_g, sh2c, sc2c), w_router, w_gate, w_up, w_down)
    return x_new, xc

def first_inputs(seed: int = 0) -> dict:
    key = jax.random.key(seed)
    ks = jax.random.split(key, 24)
    D = D_MODEL
    f32 = jnp.float32

    def nrm(k, shape, s):
        return jax.random.normal(k, shape, f32) * s

    dt = jnp.exp(jax.random.uniform(ks[10], (DEPTH, 2, GDN_HEADS), f32, math.log(1e-3), math.log(1e-1)))
    return {
        'x': nrm(ks[0], (BATCH, SEQ, D), 1.0),
        'c': nrm(ks[1], (BATCH, D), 1.0),
        'ctx': nrm(ks[2], (BATCH, CTX_LEN, D), 1.0),
        'c_ctx': nrm(ks[3], (D,), 1.0),
        'w_mod': nrm(ks[4], (DEPTH, D, 6 * D), 0.5 * D ** -0.5),
        'b_mod': nrm(ks[5], (DEPTH, 6 * D), 0.01),
        'norm1_g': 1.0 + nrm(ks[6], (DEPTH, D), 0.05),
        'w_in': nrm(ks[7], (DEPTH, D, IN_COLS), D ** -0.5),
        'conv_w': nrm(ks[8], (DEPTH, CONV_K, GDN_QKV), CONV_K ** -0.5),
        'a_log': jnp.log(jax.random.uniform(ks[9], (DEPTH, 2, GDN_HEADS), f32, 1.0, 16.0)),
        'dt_bias': dt + jnp.log(-jnp.expm1(-dt)),
        'gdn_norm_g': 1.0 + nrm(ks[11], (DEPTH, GDN_DV), 0.05),
        'lam_q1': nrm(ks[12], (DEPTH, DA_D), 0.1),
        'lam_k1': nrm(ks[13], (DEPTH, DA_D), 0.1),
        'lam_q2': nrm(ks[14], (DEPTH, DA_D), 0.1),
        'lam_k2': nrm(ks[15], (DEPTH, DA_D), 0.1),
        'da_subln_g': 1.0 + nrm(ks[16], (DEPTH, DA_DV), 0.05),
        'w_out': nrm(ks[17], (DEPTH, D_MIX, D), D_MIX ** -0.5),
        'norm2_g': 1.0 + nrm(ks[18], (DEPTH, D), 0.05),
        'w_router': nrm(ks[19], (DEPTH, D, N_EXPERTS), D ** -0.5),
        'w_gate': nrm(ks[20], (DEPTH, N_EXPERTS, D, EXPERT_FF), D ** -0.5),
        'w_up': nrm(ks[21], (DEPTH, N_EXPERTS, D, EXPERT_FF), D ** -0.5),
        'w_down': nrm(ks[22], (DEPTH, N_EXPERTS, EXPERT_FF, D), EXPERT_FF ** -0.5),
        'final_g': 1.0 + nrm(ks[23], (D,), 0.05),
    }

def first_block(x, c, ctx, c_ctx, w_mod, b_mod, norm1_g, w_in, conv_w, a_log, dt_bias, gdn_norm_g,
              lam_q1, lam_k1, lam_q2, lam_k2, da_subln_g, w_out, norm2_g,
              w_router, w_gate, w_up, w_down, final_g):
    f32 = jnp.float32
    L = x.shape[1]
    ROWS = L // GRID_W
    rows = jnp.repeat(jnp.arange(ROWS, dtype=f32), GRID_W)
    cols = jnp.tile(jnp.arange(GRID_W, dtype=f32), ROWS)
    inv_freq = jnp.power(ROPE_THETA, -jnp.arange(0, ROPE_AXIS_DIM, 2, dtype=f32) / ROPE_AXIS_DIM)
    ang_row = rows[:, None] * inv_freq[None, :]
    ang_col = cols[:, None] * inv_freq[None, :]

    xc = ctx
    for layer in range(DEPTH):
        lam_init = 0.8 - 0.6 * math.exp(-0.3 * layer)
        x, xc = hybrid_layer(x, xc, c, c_ctx, ang_row, ang_col, lam_init, layer == DEPTH - 1,
                             w_mod[layer], b_mod[layer], norm1_g[layer], w_in[layer], conv_w[layer],
                             a_log[layer], dt_bias[layer], gdn_norm_g[layer],
                             lam_q1[layer], lam_k1[layer], lam_q2[layer], lam_k2[layer], da_subln_g[layer],
                             w_out[layer], norm2_g[layer], w_router[layer], w_gate[layer], w_up[layer], w_down[layer])
    return rms_norm(x, final_g)


SSM_WIDTH = D_MODEL // 2
SSM_GROUP = 16
SSM_GROUPS = SSM_WIDTH // SSM_GROUP
SSM_STATE = 64
N_HEADS = 8
HEAD_DIM = 64
ATTN_WIDTH = N_HEADS * HEAD_DIM
KV_DIM = HEAD_DIM
IDX_HEADS = 4
IDX_DIM = 64
INDEX_TOPK = 256
N_BRANCH = 2
D_FF = -(-8 * D_MODEL // (3 * 256)) * 256
RMS_EPS = 1e-6
DT_MIN = 1e-3
DT_MAX = 1e-1

IN_SIZES = (SSM_WIDTH, ATTN_WIDTH, KV_DIM, KV_DIM, IDX_HEADS * IDX_DIM, IDX_DIM, IDX_HEADS, N_BRANCH * D_MODEL)
IN_COLS_2 = sum(IN_SIZES)
IN_SPLITS = tuple(int(s) for s in np.cumsum(IN_SIZES)[:-1])


def _rms(x, g, eps=RMS_EPS):
    xf = x.astype(jnp.float32)
    y = xf * lax.rsqrt(jnp.mean(xf * xf, axis=-1, keepdims=True) + eps)
    return (y * g.astype(jnp.float32)).astype(x.dtype)

def _complex_combine(e1, e2):
    a1r, a1i, b1r, b1i = e1
    a2r, a2i, b2r, b2i = e2
    return (a2r * a1r - a2i * a1i,
            a2r * a1i + a2i * a1r,
            a2r * b1r - a2i * b1i + b2r,
            a2r * b1i + a2i * b1r + b2i)

def _s5_branch(u, A_re, A_im, log_dt, B_re, B_im, C_re, C_im, D_skip, w_glu, b_glu):
    bsz, L, _ = u.shape
    uf = u.astype(jnp.float32).reshape(bsz, L, SSM_GROUPS, SSM_GROUP)
    ar = A_re.astype(jnp.float32)
    ai = A_im.astype(jnp.float32)
    dt = jnp.exp(log_dt.astype(jnp.float32))[:, None]
    mag = jnp.exp(ar * dt)
    abar_r = mag * jnp.cos(ai * dt)
    abar_i = mag * jnp.sin(ai * dt)
    den = ar * ar + ai * ai
    nr = abar_r - 1.0
    coef_r = (nr * ar + abar_i * ai) / den
    coef_i = (abar_i * ar - nr * ai) / den
    bu_r = jnp.einsum('gnp,blgp->blgn', B_re.astype(jnp.float32), uf)
    bu_i = jnp.einsum('gnp,blgp->blgn', B_im.astype(jnp.float32), uf)
    b_r = coef_r * bu_r - coef_i * bu_i
    b_i = coef_r * bu_i + coef_i * bu_r
    a_r = jnp.broadcast_to(abar_r, (1, L, SSM_GROUPS, SSM_STATE))
    a_i = jnp.broadcast_to(abar_i, (1, L, SSM_GROUPS, SSM_STATE))
    _, _, s_r, s_i = lax.associative_scan(_complex_combine, (a_r, a_i, b_r, b_i), axis=1)
    y = (jnp.einsum('gpn,blgn->blgp', C_re.astype(jnp.float32), s_r)
         - jnp.einsum('gpn,blgn->blgp', C_im.astype(jnp.float32), s_i)
         + D_skip.astype(jnp.float32).reshape(SSM_GROUPS, SSM_GROUP) * uf)
    y = jax.nn.gelu(y.reshape(bsz, L, SSM_WIDTH))
    y = y * jax.nn.sigmoid(y @ w_glu.astype(jnp.float32) + b_glu.astype(jnp.float32))
    return y.astype(u.dtype)

def _dsa_branch(q, k, v, qi, ki, wi):
    bsz, L = q.shape[0], q.shape[1]
    k_sel = min(INDEX_TOPK, L // 4)
    nb = L // Q_BLOCK
    q_blk = q.reshape(bsz, nb, Q_BLOCK, N_HEADS, HEAD_DIM).transpose(1, 0, 2, 3, 4)
    qi_blk = qi.reshape(bsz, nb, Q_BLOCK, IDX_HEADS, IDX_DIM).transpose(1, 0, 2, 3, 4)
    wi_blk = wi.reshape(bsz, nb, Q_BLOCK, IDX_HEADS).transpose(1, 0, 2, 3)
    starts = jnp.arange(nb, dtype=jnp.int32) * Q_BLOCK
    kif = ki.astype(jnp.float32)
    key_pos = jnp.arange(L, dtype=jnp.int32)
    w_scale = (IDX_HEADS ** -0.5) * (IDX_DIM ** -0.5)
    a_scale = HEAD_DIM ** -0.5
    gather = jax.vmap(lambda kk, ii: kk[ii])

    def block(args):
        qb, qib, wib, start = args
        pos_q = start + jnp.arange(Q_BLOCK, dtype=jnp.int32)
        visible = key_pos[None, :] <= pos_q[:, None]
        rel = jax.nn.relu(jnp.einsum('bqhd,bsd->bqhs', qib.astype(jnp.float32), kif))
        iscore = jnp.einsum('bqhs,bqh->bqs', rel, wib.astype(jnp.float32) * w_scale)
        iscore = jnp.where(visible[None], iscore, -jnp.inf)
        _, idx = lax.top_k(iscore, k_sel)
        valid = idx <= pos_q[None, :, None]
        kg = gather(k, idx).astype(jnp.float32)
        vg = gather(v, idx).astype(jnp.float32)
        logits = jnp.einsum('bqhd,bqkd->bhqk', qb.astype(jnp.float32), kg) * a_scale
        logits = jnp.where(valid[:, None], logits, -jnp.inf)
        p = jax.nn.softmax(logits, axis=-1)
        o = jnp.einsum('bhqk,bqkd->bqhd', p, vg)
        return o.astype(q.dtype)

    out = lax.map(block, (q_blk, qi_blk, wi_blk, starts))
    return out.transpose(1, 0, 2, 3, 4).reshape(bsz, L, ATTN_WIDTH)

def second_inputs(seed: int = 0) -> dict:
    key = jax.random.key(seed)
    ks = jax.random.split(key, 24)
    f32 = jnp.float32
    nrm = lambda k, shape, s: jax.random.normal(k, shape, f32) * s
    gain = lambda k, shape: 1.0 + 0.02 * jax.random.normal(k, shape, f32)
    Ld = DEPTH
    G, N, P = SSM_GROUPS, SSM_STATE, SSM_GROUP
    a_im = jnp.broadcast_to(math.pi * jnp.arange(N, dtype=f32), (Ld, G, N)) + 0.01 * jax.random.normal(ks[4], (Ld, G, N), f32)
    log_dt = jax.random.uniform(ks[5], (Ld, G), f32, math.log(DT_MIN), math.log(DT_MAX))
    return {
        "x": jax.random.normal(ks[0], (BATCH, SEQ, D_MODEL), f32),
        "norm1_g": gain(ks[1], (Ld, D_MODEL)),
        "w_in": nrm(ks[2], (Ld, D_MODEL, IN_COLS_2), D_MODEL ** -0.5),
        "A_re": -0.5 + 0.01 * jax.random.normal(ks[3], (Ld, G, N), f32),
        "A_im": a_im,
        "log_dt": log_dt,
        "B_re": nrm(ks[6], (Ld, G, N, P), (2 * P) ** -0.5),
        "B_im": nrm(ks[7], (Ld, G, N, P), (2 * P) ** -0.5),
        "C_re": nrm(ks[8], (Ld, G, P, N), (2 * N) ** -0.5),
        "C_im": nrm(ks[9], (Ld, G, P, N), (2 * N) ** -0.5),
        "D_skip": nrm(ks[10], (Ld, SSM_WIDTH), 1.0),
        "w_glu": nrm(ks[11], (Ld, SSM_WIDTH, SSM_WIDTH), SSM_WIDTH ** -0.5),
        "b_glu": nrm(ks[12], (Ld, SSM_WIDTH), 0.01),
        "q_norm_g": gain(ks[13], (Ld, HEAD_DIM)),
        "k_norm_g": gain(ks[14], (Ld, KV_DIM)),
        "idx_k_norm_g": gain(ks[15], (Ld, IDX_DIM)),
        "w_proj_ssm": nrm(ks[16], (Ld, SSM_WIDTH, D_MODEL), SSM_WIDTH ** -0.5),
        "w_proj_attn": nrm(ks[17], (Ld, ATTN_WIDTH, D_MODEL), ATTN_WIDTH ** -0.5),
        "w_out": nrm(ks[18], (Ld, D_MODEL, D_MODEL), D_MODEL ** -0.5),
        "norm2_g": gain(ks[19], (Ld, D_MODEL)),
        "w_ffn_gate": nrm(ks[20], (Ld, D_MODEL, D_FF), D_MODEL ** -0.5),
        "w_ffn_up": nrm(ks[21], (Ld, D_MODEL, D_FF), D_MODEL ** -0.5),
        "w_ffn_down": nrm(ks[22], (Ld, D_FF, D_MODEL), D_FF ** -0.5),
    }

def second_block(x, norm1_g, w_in, A_re, A_im, log_dt, B_re, B_im, C_re, C_im, D_skip, w_glu, b_glu,
              q_norm_g, k_norm_g, idx_k_norm_g, w_proj_ssm, w_proj_attn, w_out,
              norm2_g, w_ffn_gate, w_ffn_up, w_ffn_down):
    bsz, L, _ = x.shape
    for l in range(DEPTH):
        h = _rms(x, norm1_g[l])
        proj = h @ w_in[l]
        u, q, k, v, qi, ki, wi, gates = jnp.split(proj, IN_SPLITS, axis=-1)
        y_ssm = _s5_branch(u, A_re[l], A_im[l], log_dt[l], B_re[l], B_im[l], C_re[l], C_im[l],
                           D_skip[l], w_glu[l], b_glu[l])
        q = _rms(q.reshape(bsz, L, N_HEADS, HEAD_DIM), q_norm_g[l])
        k = _rms(k, k_norm_g[l])
        ki = _rms(ki, idx_k_norm_g[l])
        qi = qi.reshape(bsz, L, IDX_HEADS, IDX_DIM)
        y_att = _dsa_branch(q, k, v, qi, ki, wi)
        g_ssm, g_att = jnp.split(gates, N_BRANCH, axis=-1)
        merged = (jax.nn.sigmoid(g_ssm) * (y_ssm @ w_proj_ssm[l])
                  + jax.nn.sigmoid(g_att) * (y_att @ w_proj_attn[l]))
        x = x + merged @ w_out[l]
        h2 = _rms(x, norm2_g[l])
        x = x + (jax.nn.silu(h2 @ w_ffn_gate[l]) * (h2 @ w_ffn_up[l])) @ w_ffn_down[l]
    return x


def setup_inputs(seed=0):
    out = dict(first_inputs(seed))
    for name, value in second_inputs(seed + 1).items():
        if name != "x":
            out[name + "_2"] = value
    return out


def reference(
    x, c, ctx, c_ctx, w_mod, b_mod, norm1_g, w_in, conv_w, a_log, dt_bias, gdn_norm_g, lam_q1,
    lam_k1, lam_q2, lam_k2, da_subln_g, w_out, norm2_g, w_router, w_gate, w_up, w_down, final_g,
    norm1_g_2, w_in_2, A_re_2, A_im_2, log_dt_2, B_re_2, B_im_2, C_re_2, C_im_2, D_skip_2,
    w_glu_2, b_glu_2, q_norm_g_2, k_norm_g_2, idx_k_norm_g_2, w_proj_ssm_2, w_proj_attn_2,
    w_out_2, norm2_g_2, w_ffn_gate_2, w_ffn_up_2, w_ffn_down_2,
):
    x = first_block(
        x, c, ctx, c_ctx, w_mod, b_mod, norm1_g, w_in, conv_w, a_log, dt_bias, gdn_norm_g,
        lam_q1, lam_k1, lam_q2, lam_k2, da_subln_g, w_out, norm2_g, w_router, w_gate, w_up,
        w_down, final_g,
    )
    return second_block(
        x, norm1_g_2, w_in_2, A_re_2, A_im_2, log_dt_2, B_re_2, B_im_2, C_re_2, C_im_2,
        D_skip_2, w_glu_2, b_glu_2, q_norm_g_2, k_norm_g_2, idx_k_norm_g_2, w_proj_ssm_2,
        w_proj_attn_2, w_out_2, norm2_g_2, w_ffn_gate_2, w_ffn_up_2, w_ffn_down_2,
    )


_drawn_inputs = setup_inputs


def setup_inputs(seed=0):
    import zlib

    import numpy as np

    out = dict(_drawn_inputs(seed))
    spreads = {}
    factors = {'b_mod': 3.756,
     'norm1_g': 3.579,
     'gdn_norm_g': 4.614,
     'lam_q1': 6.201,
     'lam_k1': 2.882,
     'lam_q2': 8.0,
     'lam_k2': 5.76,
     'da_subln_g': 4.333,
     'norm2_g': 4.183,
     'norm1_g_2': 5.786,
     'A_re_2': 64.0,
     'A_im_2': 33.184,
     'log_dt_2': 35.656,
     'B_re_2': 47.48,
     'B_im_2': 47.736,
     'C_re_2': 45.928,
     'C_im_2': 47.12,
     'b_glu_2': 48.995,
     'q_norm_g_2': 8.0,
     'k_norm_g_2': 8.0,
     'idx_k_norm_g_2': 8.0,
     'norm2_g_2': 3.576}
    for name, (base, spread) in spreads.items():
        noise = np.random.default_rng([zlib.crc32(name.encode()), seed]).standard_normal(out[name].shape)
        drawn = base * np.exp(spread * noise) if base else spread * noise
        out[name] = jnp.asarray(drawn.astype(out[name].dtype))
    for name, factor in factors.items():
        out[name] = (out[name] * factor).astype(out[name].dtype)
    return out
```

```python
from contextlib import ExitStack

import numpy as np

import concourse.bass as bass
from concourse import mybir

F32 = mybir.dt.float32
U32 = mybir.dt.uint32
I32 = mybir.dt.int32
ALU = mybir.AluOpType
ACT = mybir.ActivationFunctionType
AX = mybir.AxisListType.X

P = 128
D = 1024
KD = D // P
L = 1024
LC = 256
LA = LC + L
TC, TL, TA = LC // P, L // P, LA // P
EPS = 1e-6
BIG = 1e30
DAH, DAD, DAV = 4, 64, 128
GH, GD = 4, 128
NE, CAP, FF = 16, 128, 1024
SG, SP, SN = 32, 16, 64
CH = 8
NCH = L // CH
HEADS, HD = 8, 64
IH = 4
TOPK = 256
DFF = 2816
TOKEN_RANGES = ((0, 256), (256, 512), (768, 512))


def constant_tables():
    i = np.arange(P)
    col, row = i[None, :], i[:, None]
    parts = {"ident": (row == col).astype(np.float32), "ones": np.ones((P, P), np.float32)}
    parts["cum0"] = (row <= col).astype(np.float32)
    parts["cum1"] = (row >= col).astype(np.float32)
    big = np.float32(-BIG)
    parts["strict0"] = np.where(col < row, 0, big)
    parts["strict1"] = np.where(col > row, 0, big)
    parts["incl0"] = np.where(row <= col, 0, big)
    parts["incl1"] = np.where(row >= col, 0, big)
    for lv in range(7):
        s = 1 << lv
        same = (row // (2 * s)) == (col // (2 * s))
        low = same & ((row // s) % 2 == 1) & ((col // s) % 2 == 0)
        parts[f"level0_{lv}"] = low.astype(np.float32)
        parts[f"level1_{lv}"] = low.T.astype(np.float32)
    d = i % 64
    axis, within = d // 32, d % 32
    inv = 10000.0 ** (-(2.0 * (within % 16)) / 32.0)
    t = np.arange(L)
    pos = np.where(axis[:, None] == 0, t[None, :] // 64, t[None, :] % 64)
    ang = pos.astype(np.float32) * inv.astype(np.float32)[:, None]
    swap = np.zeros((P, P), np.float32)
    for m in range(P):
        first = (m % 32) < 16
        swap[m + 16 if first else m - 16, m] = -1.0 if first else 1.0
    parts["swap"] = swap
    parts["eps"] = np.full((P, 1), EPS, np.float32)
    parts["causal"] = np.where(col <= row, 0, big)
    rope = {"cos": np.cos(ang), "sin": np.sin(ang)}
    names, at, arrays = {}, 0, []
    for name, a in parts.items():
        names[name] = (at, a.shape[1])
        at += a.shape[1]
        arrays.append(a.astype(np.float32))
    return (np.concatenate(arrays, 1), names,
            np.concatenate([rope["cos"], rope["sin"]], 1).astype(np.float32))


class Arena:

    def __init__(self, tensor, words):
        self.tensor, self.words, self.used = tensor, words, {}

    def take(self, name, *shape, high=False):
        n = int(np.prod(shape))
        if high:
            at = self.words - n
            for a, b in sorted(self.used.values(), reverse=True):
                if b <= at:
                    break
                at = min(at, a - n)
        else:
            at = 0
            for a, b in sorted(self.used.values()):
                if at + n <= a:
                    break
                at = max(at, b)
        assert at >= 0 and at + n <= self.words, f"{name}: {at + n} of {self.words} words"
        assert name not in self.used, name
        self.used[name] = (at, at + n)
        v = self.tensor[:, at:at + n]
        if len(shape) > 1:
            axes = [f"a{i}" for i in range(len(shape))]
            v = v.rearrange(f"p ({' '.join(axes)}) -> p {' '.join(axes)}", **dict(zip(axes[:-1], shape)))
        return v

    def give(self, *names):
        for name in names:
            del self.used[name]


class Steps:

    def __init__(self, eng, sem, base=0):
        self.eng, self.sem, self.n = eng, sem, base

    def __call__(self, ins):
        self.n += 1
        ins.then_inc(self.sem, 1)
        self.eng.wait_ge(self.sem, self.n)


class Env:
    pass


def broadcast_rows(ap, n=P):
    return ap.partition_broadcast(n)


def row_of(vec):
    return vec.rearrange("(a n) -> a n", a=1)


def stage_modulation(e):
    nc, A = e.nc, e.arena
    cc = A.take("cc", 2, KD)
    e.silu_c = A.take("silu_c", KD, 2)
    w = A.take("w_ring", 3, KD, 512)
    bm = A.take("b_mod1", 2 * KD)
    g1 = A.take("norm1", KD)
    w_mod = e.in_["w_mod"][0].rearrange("(k p) n -> p k n", p=P)
    s_in, s_w = e.sem("mod_in"), [e.sem(f"mod_w{i}") for i in range(3)]
    s_silu, s_mm, s_own = e.sem("mod_silu"), e.sem("mod_mm"), e.sem("mod_own")
    with nc.Block() as block:
        @block.sync
        def _(sp):
            sp.dma_start(e.consts, e.in_["tables"]).then_inc(s_in, 16)
            with nc.allow_non_contiguous_dma("vectors by channel"):
                sp.dma_start(cc[:, 0, :], e.in_["c"].rearrange("a (k p) -> p (a k)", p=P)).then_inc(s_in, 16)
                sp.dma_start(cc[:, 1, :], e.in_["c_ctx"].rearrange("(k p) -> p k", p=P)).then_inc(s_in, 16)
                sp.dma_start(bm, e.in_["b_mod"][0, 0:2 * D].rearrange("(k p) -> p k", p=P)).then_inc(s_in, 16)
                sp.dma_start(g1, e.in_["norm1_g"][0].rearrange("(k p) -> p k", p=P)).then_inc(s_in, 16)
            for c in range(4):
                if c >= 3:
                    sp.wait_ge(s_mm, c - 2)
                sp.dma_start(w[:, c % 3], w_mod[:, :, c * 512:(c + 1) * 512]).then_inc(s_w[c % 3], 16)

        @block.scalar
        def _(act):
            act.wait_ge(s_in, 80)
            nc.scalar.activation(e.silu_c.rearrange("p k v -> p v k"), cc, ACT.Silu).then_inc(s_silu, 1)

        @block.tensor
        def _(pe):
            pe.wait_ge(s_silu, 1)
            for c in range(4):
                pe.wait_ge(s_w[c % 3], 16 * (c // 3 + 1))
                for j in range(4):
                    for k in range(KD):
                        last = nc.tensor.matmul(e.ps[:, 0, 2 * (4 * c + j):2 * (4 * c + j) + 2],
                                                w[:, c % 3, k, j * P:(j + 1) * P], e.silu_c[:, k, :],
                                                start=(k == 0), stop=(k == KD - 1))
                last.then_inc(s_mm, 1)

        @block.vector
        def _(dve):
            step = Steps(dve, s_own)
            dve.wait_ge(s_in, 80)
            dve.wait_ge(s_mm, 4)
            out = e.ps[:, 0, 0:4 * KD].rearrange("p (m v) -> p m v", v=2)
            step(nc.vector.tensor_tensor(e.shift1, out[:, 0:KD], bm[:, 0:KD].unsqueeze(2).broadcast_to([P, KD, 2]), ALU.add))
            step(nc.vector.tensor_tensor(e.scale1, out[:, KD:], bm[:, KD:].unsqueeze(2).broadcast_to([P, KD, 2]), ALU.add))
            step(nc.vector.tensor_scalar(e.scale1, e.scale1, 1.0, None, ALU.add))
            step(nc.vector.tensor_tensor(e.scale1, e.scale1, g1.unsqueeze(2).broadcast_to([P, KD, 2]), ALU.mult))
    A.give("cc", "w_ring", "b_mod1", "norm1")


def stage_norm1(e):
    nc, A = e.nc, e.arena
    xa = A.take("xa", TA, D)
    junk = A.take("junk", D)
    ss = A.take("ss", TA)
    s_x = [e.sem(f"n1_x{i}") for i in range(TA)]
    s_sq, s_rs, s_rt, s_xn, s_tr, s_ev, s_own = (e.sem(f"n1_{n}") for n in ("sq", "rs", "rt", "xn", "tr", "ev", "own"))
    s_ev2 = e.sem("n1_ev2")
    with nc.Block() as block:
        @block.sync
        def _(sp):
            for t in range(TA):
                src = e.in_["ctx"][0, t * P:(t + 1) * P, :] if t < TC else e.in_["x"][0, (t - TC) * P:(t - TC + 1) * P, :]
                sp.dma_start(xa[:, t], src).then_inc(s_x[t], 16)

        @block.scalar
        def _(act):
            for t in range(TA):
                act.wait_ge(s_x[t], 16)
                if t:
                    act.wait_ge(s_sq, t)
                nc.scalar.activation(junk, xa[:, t], ACT.Square, accum_out=ss[:, t:t + 1]).then_inc(s_sq, 1)
            act.wait_ge(s_rs, 1)
            nc.scalar.activation(ss, ss, ACT.Sqrt).then_inc(s_rt, 1)
            for t in range(TA):
                v = 1 if t < TC else 0
                act.wait_ge(s_tr, 2 * t + 1)
                for k in range(4):
                    ins = nc.scalar.activation(e.hT[:, k, t * P:(t + 1) * P], e.ps[:, (2 * t) % 8, k * P:(k + 1) * P],
                                               ACT.Identity, bias=e.shift1[:, k, v:v + 1], scale=e.scale1[:, k, v:v + 1])
                ins.then_inc(s_ev, 1)

        @block.vector
        def _(dve):
            step = Steps(dve, s_own)
            dve.wait_ge(s_sq, TA)
            step(nc.vector.tensor_scalar(ss, ss, 1.0 / D, EPS, ALU.mult, ALU.add))
            nc.vector.reciprocal(ss, ss).then_inc(s_rs, 1)
            dve.wait_ge(s_rt, 1)
            for t in range(TA):
                nc.vector.tensor_scalar(xa[:, t], xa[:, t], ss[:, t:t + 1], None, ALU.mult).then_inc(s_xn, 1)
            for t in range(TA):
                v = 1 if t < TC else 0
                dve.wait_ge(s_tr, 2 * t + 2)
                for k in range(4, 8):
                    ins = nc.vector.tensor_scalar(e.hT[:, k, t * P:(t + 1) * P], e.ps[:, (2 * t + 1) % 8, (k - 4) * P:(k - 3) * P],
                                                  e.scale1[:, k, v:v + 1], e.shift1[:, k, v:v + 1], ALU.mult, ALU.add)
                ins.then_inc(s_ev2, 1)

        @block.tensor
        def _(pe):
            for t in range(TA):
                pe.wait_ge(s_xn, t + 1)
                for half, s in ((0, s_ev), (1, s_ev2)):
                    if t >= 4:
                        pe.wait_ge(s, t - 3)
                    for k in range(4):
                        last = nc.tensor.transpose(e.ps[:, (2 * t + half) % 8, k * P:(k + 1) * P],
                                                   xa[:, t, (4 * half + k) * P:(4 * half + k + 1) * P], e.ident)
                    last.then_inc(s_tr, 1)
    A.give("xa", "junk", "ss")


def stage_da_project(e):
    nc, A = e.nc, e.arena
    e.qT = A.take("qT", DAH, L)
    e.kT = A.take("kT", DAH, LA)
    e.v = A.take("v", TA, DAH * DAV)
    w = A.take("w_ring", 2, KD, 512)
    rope = A.take("rope", 2, L)
    raw = A.take("raw", 3, 512)
    tmp = A.take("rope_tmp", 2, 512)
    w_in = e.in_["w_in"][0].rearrange("(k p) n -> p k n", p=P)
    tasks = []
    for m in range(DAH):
        tasks += [("q", 0, m, s, n) for s, n in TOKEN_RANGES[1:]]
    for m in range(DAH):
        tasks += [("k", 1, m, s, n) for s, n in TOKEN_RANGES]
    tasks += [("v", 2, t, t * P, P) for t in range(TA)]
    first = {c: min(i for i, t in enumerate(tasks) if t[1] == c) for c in range(3)}
    last_of = {c: max(i for i, t in enumerate(tasks) if t[1] == c) for c in range(3)}
    roped = [i for i, t in enumerate(tasks) if t[0] in "qk" and t[3] >= LC]
    s_w = [e.sem(f"da_w{i}") for i in range(2)]
    s_rope, s_mm, s_raw, s_swap, s_done, s_own = (e.sem(f"dap_{n}") for n in ("rope", "mm", "raw", "swap", "done", "own"))
    with nc.Block() as block:
        @block.sync
        def _(sp):
            for c in range(3):
                if c >= 2:
                    sp.wait_ge(s_mm, last_of[c - 2] + 1)
                sp.dma_start(w[:, c % 2], w_in[:, :, c * 512:(c + 1) * 512]).then_inc(s_w[c % 2], 16)
                if c == 0:
                    sp.dma_start(rope, e.in_["rope"].rearrange("p (a n) -> p a n", a=2)).then_inc(s_rope, 16)

        @block.tensor
        def _(pe):
            def swap(r):
                pe.wait_ge(s_raw, roped[r] + 1)
                if r >= 2:
                    pe.wait_ge(s_done, r - 1)
                nc.tensor.matmul(e.ps[:, 4 + r % 2, :], e.const("swap"), raw[:, r % 3], start=True, stop=True).then_inc(s_swap, 1)

            done = 0
            for i, (kind, c, m, s, n) in enumerate(tasks):
                if i == first[c]:
                    pe.wait_ge(s_w[c % 2], 16 * (c // 2 + 1))
                if i >= 4:
                    pe.wait_ge(s_raw, i - 3)
                for k in range(KD):
                    if kind == "v":
                        ins = nc.tensor.matmul(e.ps[:, i % 4, :], e.hT[:, k, s:s + n], w[:, c % 2, k, :],
                                               start=(k == 0), stop=(k == KD - 1))
                    else:
                        ins = nc.tensor.matmul(e.ps[:, i % 4, 0:n], w[:, c % 2, k, m * P:(m + 1) * P], e.hT[:, k, s:s + n],
                                               start=(k == 0), stop=(k == KD - 1))
                ins.then_inc(s_mm, 1)
                while done < len(roped) and roped[done] < i:
                    swap(done)
                    done += 1
            while done < len(roped):
                swap(done)
                done += 1

        @block.scalar
        def _(act):
            for i, (kind, c, m, s, n) in enumerate(tasks):
                act.wait_ge(s_mm, i + 1)
                if i in roped:
                    r = roped.index(i)
                    if r >= 3:
                        act.wait_ge(s_done, r - 2)
                    dst = raw[:, r % 3]
                elif kind == "k":
                    dst = e.kT[:, m, s:s + n]
                else:
                    dst = e.v[:, m, :]
                nc.scalar.activation(dst, e.ps[:, i % 4, 0:n if kind != "v" else 512], ACT.Copy).then_inc(s_raw, 1)

        @block.vector
        def _(dve):
            step = Steps(dve, s_own)
            dve.wait_ge(s_rope, 16)
            for r, i in enumerate(roped):
                kind, c, m, s, n = tasks[i]
                o = s - LC
                dst = e.qT[:, m, o:o + n] if kind == "q" else e.kT[:, m, s:s + n]
                dve.wait_ge(s_raw, i + 1)
                nc.vector.tensor_tensor(tmp[:, 0], raw[:, r % 3], rope[:, 0, o:o + n], ALU.mult).then_inc(s_own, 1)
                dve.wait_ge(s_swap, r + 1)
                nc.vector.tensor_tensor(tmp[:, 1], e.ps[:, 4 + r % 2, :], rope[:, 1, o:o + n], ALU.mult).then_inc(s_own, 1)
                dve.wait_ge(s_own, 2 * r + 2)
                nc.vector.tensor_tensor(dst, tmp[:, 0], tmp[:, 1], ALU.add).then_inc(s_done, 1)
                dve.wait_ge(s_done, r + 1)
    A.give("w_ring", "rope", "raw", "rope_tmp")


def stage_da(e):
    nc, A = e.nc, e.arena
    pr = A.take("probs", 4, LA)
    aT = A.take("aT", 2, TA, P)
    on = A.take("o_norm", 2, P)
    mx = A.take("mx", 2, 8)
    sm = A.take("sm", 2, 8)
    lamv = A.take("lamv", 4, DAD)
    lam = A.take("lam", 8)
    sub = A.take("subln", 1)
    steps = [(t, h) for t in range(TL) for h in range(DAH)]
    n_steps = len(steps)
    COLS = ((0, 512), (512, 512), (1024, 256))
    s_in, s_own, s_lam, s_lam2, s_qk, s_mx, s_exp, s_comb, s_tr, s_aT, s_pv, s_on, s_fin, s_sq, s_rt, s_oT, s_var, s_e2 = (
        e.sem(f"da_{n}") for n in ("in", "own", "lam", "lam2", "qk", "mx", "exp", "comb", "tr", "aT", "pv", "on", "fin", "sq", "rt", "oT", "var", "e2"))
    SC = DAD ** -0.5
    with nc.Block() as block:
        @block.sync
        def _(sp):
            for j, name in enumerate(("lam_q1", "lam_k1", "lam_q2", "lam_k2")):
                sp.dma_start(lamv[:, j], broadcast_rows(e.in_[name][0])).then_inc(s_in, 16)
            with nc.allow_non_contiguous_dma("a vector by channel"):
                sp.dma_start(sub, e.in_["da_subln_g"][0].rearrange("(p a) -> p a", a=1)).then_inc(s_in, 16)

        @block.tensor
        def _(pe):
            def scores(i):
                t, h = steps[i]
                for m in range(2):
                    u = 2 * i + m
                    if u >= 2:
                        pe.wait_ge(s_exp, u - 1)
                    for j, (c, n) in enumerate(COLS):
                        ins = nc.tensor.matmul(e.ps[:, 3 * m + j, 0:n], e.qT[64 * m:64 * m + 64, h, t * P:(t + 1) * P],
                                               e.kT[64 * m:64 * m + 64, h, c:c + n], start=True, stop=True)
                    ins.then_inc(s_qk, 1)

            def weigh(i):
                t, h = steps[i]
                pe.wait_ge(s_comb, i + 1)
                for g in range(3):
                    u = 3 * i + g
                    if u >= 1:
                        pe.wait_ge(s_aT, u)
                    for j in range(4 * g, min(4 * g + 4, TA)):
                        ins = nc.tensor.transpose(e.ps[:, 6, (j % 4) * P:(j % 4 + 1) * P], pr[:, 2 * (i % 2), j * P:(j + 1) * P], e.ident)
                    ins.then_inc(s_tr, 1)
                if i >= 1:
                    pe.wait_ge(s_fin, i)
                pe.wait_ge(s_aT, 3 * i + 3)
                for j in range(TA):
                    ins = nc.tensor.matmul(e.ps[:, 7, 0:P], aT[:, i % 2, j, :], e.v[:, j, h * P:(h + 1) * P],
                                           start=(j == 0), stop=(j == TA - 1))
                ins.then_inc(s_pv, 1)
                pe.wait_ge(s_on, i + 1)
                nc.tensor.transpose(e.ps[:, 7, P:2 * P], on[:, i % 2, :], e.ident).then_inc(s_oT, 1)

            for i in range(n_steps):
                scores(i)
                if i >= 1:
                    weigh(i - 1)
            weigh(n_steps - 1)

        @block.scalar
        def _(act):
            act.wait_ge(s_lam, 2)
            nc.scalar.activation(lam[:, 2:4], lam[:, 0:2], ACT.Exp).then_inc(s_lam2, 1)

            def copies(i):
                for g in range(3):
                    n = min(4, TA - 4 * g)
                    act.wait_ge(s_tr, 3 * i + g + 1)
                    if g == 0 and i >= 2:
                        act.wait_ge(s_pv, i - 1)
                    nc.scalar.activation(aT[:, i % 2, 4 * g:4 * g + n, :], e.ps[:, 6, 0:n * P].rearrange("p (a b) -> p a b", b=P),
                                         ACT.Copy).then_inc(s_aT, 1)

            def norm(i):
                act.wait_ge(s_pv, i + 1)
                nc.scalar.activation(on[:, i % 2, :], e.ps[:, 7, 0:P], ACT.Square, accum_out=sm[:, i % 2, 4:5]).then_inc(s_sq, 1)
                act.wait_ge(s_var, i + 1)
                nc.scalar.activation(sm[:, i % 2, 6:7], sm[:, i % 2, 5:6], ACT.Ln).then_inc(s_e2, 1)
                act.wait_ge(s_e2, i + 1)
                nc.scalar.activation(sm[:, i % 2, 7:8], sm[:, i % 2, 6:7], ACT.Exp, scale=-0.5).then_inc(s_rt, 1)

            for i in range(n_steps + 1):
                if i < n_steps:
                    for m in range(2):
                        u = 2 * i + m
                        act.wait_ge(s_mx, u + 1)
                        if i >= 2 and m == 0:
                            act.wait_ge(s_tr, 3 * (i - 1))
                        ins = nc.scalar.activation(pr[:, 2 * (i % 2) + m, :], e.ps[:, 3 * m:3 * m + 3, :].rearrange("p a b -> p (a b)")[:, 0:LA],
                                                   ACT.Exp, bias=mx[:, i % 2, 4 + m:5 + m], scale=SC, accum_out=sm[:, i % 2, m:m + 1])
                        ins.then_inc(s_exp, 1)
                if i >= 1:
                    copies(i - 1)
                    norm(i - 1)

        @block.vector
        def _(dve):
            step = Steps(dve, s_own)
            dve.wait_ge(s_in, 80)
            for j in range(2):
                step(nc.vector.tensor_tensor(lamv[:, 2 * j], lamv[:, 2 * j], lamv[:, 2 * j + 1], ALU.mult))
                nc.vector.tensor_reduce(lam[:, j:j + 1], lamv[:, 2 * j], AX, ALU.add).then_inc(s_lam, 1)
            dve.wait_ge(s_lam2, 1)
            step(nc.vector.tensor_tensor(lam[:, 4:5], lam[:, 3:4], lam[:, 2:3], ALU.subtract))
            step(nc.vector.tensor_scalar(lam[:, 4:5], lam[:, 4:5], -0.2, None, ALU.add))
            step(nc.vector.tensor_scalar(sub, sub, 0.8, None, ALU.mult))

            def finish(i):
                t, h = steps[i]
                b = i % 2
                dve.wait_ge(s_sq, i + 1)
                nc.vector.tensor_scalar(sm[:, b, 5:6], sm[:, b, 4:5], 1.0 / DAV, EPS, ALU.mult, ALU.add).then_inc(s_var, 1)
                dve.wait_ge(s_rt, i + 1)
                nc.vector.tensor_scalar(on[:, b, :], e.ps[:, 7, 0:P], sm[:, b, 7:8], None, ALU.mult).then_inc(s_on, 1)
                dve.wait_ge(s_oT, i + 1)
                nc.vector.tensor_scalar(e.catA[:, h, t * P:(t + 1) * P], e.ps[:, 7, P:2 * P], sub[:, 0:1], None, ALU.mult).then_inc(s_fin, 1)

            for i in range(n_steps + 1):
                if i < n_steps:
                    b = i % 2
                    for m in range(2):
                        dve.wait_ge(s_qk, 2 * i + m + 1)
                        step(nc.vector.tensor_reduce(mx[:, b, m:m + 1], e.ps[:, 3 * m:3 * m + 3, :].rearrange("p a b -> p (a b)")[:, 0:LA], AX, ALU.max))
                        nc.vector.tensor_scalar(mx[:, b, 4 + m:5 + m], mx[:, b, m:m + 1], -SC, None, ALU.mult).then_inc(s_mx, 1)
                    dve.wait_ge(s_exp, 2 * i + 2)
                    step(nc.vector.reciprocal(sm[:, b, 2:4], sm[:, b, 0:2]))
                    step(nc.vector.tensor_scalar(sm[:, b, 3:4], sm[:, b, 3:4], lam[:, 4:5], None, ALU.mult))
                    step(nc.vector.tensor_scalar(pr[:, 2 * b, :], pr[:, 2 * b, :], sm[:, b, 2:3], None, ALU.mult))
                    nc.vector.scalar_tensor_tensor(out=pr[:, 2 * b, :], in0=pr[:, 2 * b + 1, :], scalar=sm[:, b, 3:4],
                                                   in1=pr[:, 2 * b, :], op0=ALU.mult, op1=ALU.add).then_inc(s_comb, 1)
                if i >= 1:
                    finish(i - 1)
    A.give("probs", "aT", "o_norm", "mx", "sm", "lamv", "lam", "subln", "qT", "kT", "v")


def stage_gdn_project(e):
    nc, A = e.nc, e.arena
    NB = 3 * GH
    e.gqT = A.take("gqT", GH, LA)
    e.gkT = A.take("gkT", GH, LA)
    e.gvt = A.take("gvt", TA, GH * GD)
    e.gkt = A.take("gkt", TA, GH * GD)
    e.g = A.take("g", TA, 8)
    e.beta = A.take("beta", TA, 8)
    e.gate_dram = nc.dram_tensor("gate_scratch", (L, GH * GD), F32).ap()
    vT = A.take("vT", 2, LA)
    w = A.take("w_ring", 2, KD, 256)
    xc = A.take("conv_in", 2, LA + 4)
    cw = A.take("conv_w", 3, NB)
    rw = A.take("ab_rows", 2, 8)
    abt = A.take("ab", TA, 16)
    gs = A.take("gate_out", 2, 256)
    sq = A.take("sq", 512)
    inv = A.take("inv", 2, 512)
    w_in = e.in_["w_in"][0].rearrange("(k p) n -> p k n", p=P)
    V = lambda b, sh: (xc[:, b, sh:sh + LC], xc[:, b, LC + 2 + sh:LC + 2 + sh + L])
    s_w = [e.sem(f"gp_w{i}") for i in range(2)]
    names = ("in", "taps", "mm", "raw", "conv", "silu", "own", "sq", "ss", "ln", "inv", "nrm", "tr", "tok",
             "ab", "gate", "store", "actown", "pad")
    s_in, s_taps, s_mm, s_raw, s_conv, s_silu, s_own, s_sq, s_ss, s_ln, s_inv, s_nrm, s_tr, s_tok, s_ab, s_gate, s_store, s_ao, s_pad = (
        e.sem(f"gp_{n}") for n in names)
    s_st = [e.sw_sem(f"gp_st{i}") for i in range(2)]
    chunks = [(1536 + 256 * c, 256) for c in range(8)] + [(3584, 16)]
    ranges = TOKEN_RANGES
    qkv = [(m, r) for m in range(NB) for r in range(3)]
    NQ = len(qkv)
    gate = [(c, t) for c in range(2) for t in range(TL)]
    NG = len(gate)
    norms = [(m, r) for m in range(2 * GH) for r in range(3)]
    dst_of = lambda m: (e.gqT, e.gkT)[m // GH][:, m % GH] if m < 2 * GH else vT[:, m % 2]
    with nc.Block() as block:
        @block.sync
        def _(sp):
            with nc.allow_non_contiguous_dma("vectors by channel"):
                for i in range(3):
                    sp.dma_start(cw[:, i], e.in_["conv_w"][0, i].rearrange("(m p) -> p m", p=P)).then_inc(s_in, 16)
            sp.dma_start(rw[:, 0], broadcast_rows(e.in_["a_log"][0].rearrange("a b -> (a b)"))).then_inc(s_in, 16)
            sp.dma_start(rw[:, 1], broadcast_rows(e.in_["dt_bias"][0].rearrange("a b -> (a b)"))).then_inc(s_in, 16)
            for c, (at, n) in enumerate(chunks):
                if c >= 2:
                    d = c - 2
                    sp.wait_ge(s_mm, 6 * (d + 1) if d < 6 else NQ + TL * (d - 5))
                sp.dma_start(w[:, c % 2, :, 0:n], w_in[:, :, at:at + n]).then_inc(s_w[c % 2], 16)

        @block.gpsimd
        def _(pool):
            for i, (c, t) in enumerate(gate):
                pool.wait_ge(s_raw, NQ + i + 1)
                pool.dma_start(e.gate_dram[t * P:(t + 1) * P, c * 256:(c + 1) * 256], gs[:, i % 2, 0:256]).then_inc(s_st[i % 2], 16)
            for i in range(2):
                pool.wait_ge(s_st[i], 16 * NG // 2)

        @block.tensor
        def _(pe):
            def loaded(c):
                pe.wait_ge(s_w[c % 2], 16 * (c // 2 + 1))

            def v_tokens(m):
                pe.wait_ge(s_silu, m + 1)
                h = m - 2 * GH
                for g in range(3):
                    u = 3 * h + g
                    if u >= 2:
                        pe.wait_ge(s_tok, u - 1)
                    for j in range(4 * g, min(4 * g + 4, TA)):
                        ins = nc.tensor.transpose(e.ps[:, 4 + u % 2, (j % 4) * P:(j % 4 + 1) * P], vT[:, m % 2, j * P:(j + 1) * P], e.ident)
                    ins.then_inc(s_tr, 1)

            for i, (m, r) in enumerate(qkv):
                if m % 2 == 0 and r == 0:
                    loaded(m // 2)
                if i >= 4:
                    pe.wait_ge(s_raw, i - 3)
                s, n = ranges[r]
                for k in range(KD):
                    ins = nc.tensor.matmul(e.ps[:, i % 4, 0:n], w[:, (m // 2) % 2, k, (m % 2) * P:(m % 2 + 1) * P],
                                           e.hT[:, k, s:s + n], start=(k == 0), stop=(k == KD - 1))
                ins.then_inc(s_mm, 1)
                if r == 2 and m - 1 >= 2 * GH:
                    v_tokens(m - 1)
            for i, (c, t) in enumerate(gate):
                if t == 0:
                    loaded(6 + c)
                n = NQ + i
                pe.wait_ge(s_raw, n - 3)
                for k in range(KD):
                    ins = nc.tensor.matmul(e.ps[:, n % 4, 0:256], e.hT[:, k, LC + t * P:LC + (t + 1) * P], w[:, (6 + c) % 2, k, :],
                                           start=(k == 0), stop=(k == KD - 1))
                ins.then_inc(s_mm, 1)
                if i == 1:
                    v_tokens(NB - 1)
            loaded(8)
            for t in range(TA):
                for k in range(KD):
                    ins = nc.tensor.matmul(e.ps[:, 6, 16 * t:16 * t + 16], e.hT[:, k, t * P:(t + 1) * P], w[:, 0, k, 0:16],
                                           start=(k == 0), stop=(k == KD - 1))
            ins.then_inc(s_ab, 1)
            pe.wait_ge(s_raw, NQ + NG)
            for i, (m, r) in enumerate(norms):
                s, n = ranges[r]
                pe.wait_ge(s_sq, i + 1)
                if i >= 2:
                    pe.wait_ge(s_ln, i - 1)
                nc.tensor.matmul(e.ps[:, (i % 2), 0:n], e.const("ones"), sq[:, 0:n], start=True, stop=True).then_inc(s_ss, 1)
            for t in range(TA):
                pe.wait_ge(s_nrm, len(norms))
                if t >= 2:
                    pe.wait_ge(s_tok, 3 * GH + t - 1)
                else:
                    pe.wait_ge(s_tok, 3 * GH)
                for h in range(GH):
                    ins = nc.tensor.transpose(e.ps[:, 4 + t % 2, h * P:(h + 1) * P], e.gkT[:, h, t * P:(t + 1) * P], e.ident)
                ins.then_inc(s_tr, 1)

        @block.scalar
        def _(act):
            def silu(m):
                act.wait_ge(s_conv, m + 1)
                if m >= 2 * GH + 2:
                    act.wait_ge(s_tr, 3 * (m - 2 * GH - 1))
                d = dst_of(m)
                nc.scalar.activation(d, d, ACT.Silu).then_inc(s_silu, 1)

            act.wait_ge(s_pad, 1)
            for i, (m, r) in enumerate(qkv):
                s, n = ranges[r]
                act.wait_ge(s_mm, i + 1)
                if m >= 2 and r == 0:
                    act.wait_ge(s_conv, m - 1)
                at = 1 + s if r == 0 else 3 + s
                nc.scalar.activation(xc[:, m % 2, at:at + n], e.ps[:, i % 4, 0:n], ACT.Copy).then_inc(s_raw, 1)
                if r == 2 and m >= 1:
                    silu(m - 1)
            silu(NB - 1)
            for i, (c, t) in enumerate(gate):
                act.wait_ge(s_mm, NQ + i + 1)
                if i >= 2:
                    act.wait_ge(s_st[i % 2], 16 * (i // 2))
                nc.scalar.activation(gs[:, i % 2, 0:256], e.ps[:, (NQ + i) % 4, 0:256], ACT.Silu).then_inc(s_raw, 1)
            act.wait_ge(s_own, 1)
            nc.scalar.activation(e.beta, abt[:, :, 8:16], ACT.Sigmoid).then_inc(s_ao, 1)
            nc.scalar.activation(rw[:, 0], rw[:, 0], ACT.Exp).then_inc(s_ao, 1)
            act.wait_ge(s_own, 4)
            nc.scalar.activation(abt[:, :, 8:16], abt[:, :, 8:16], ACT.Exp).then_inc(s_ao, 1)
            act.wait_ge(s_ao, 3)
            nc.scalar.activation(abt[:, :, 8:16], abt[:, :, 8:16], ACT.Ln, bias=e.const("ones")[:, 0:1]).then_inc(s_ao, 1)
            act.wait_ge(s_silu, NB)
            for i, (m, r) in enumerate(norms):
                s, n = ranges[r]
                if i:
                    act.wait_ge(s_ss, i)
                nc.scalar.activation(sq[:, 0:n], dst_of(m)[:, s:s + n], ACT.Square).then_inc(s_sq, 1)
                act.wait_ge(s_ss, i + 1)
                if i >= 2:
                    act.wait_ge(s_nrm, i - 1)
                nc.scalar.activation(inv[:, i % 2, 0:n], e.ps[:, i % 2, 0:n], ACT.Sqrt, bias=e.eps[:, 0:1]).then_inc(s_ln, 1)

        @block.vector
        def _(dve):
            step = Steps(dve, s_own)
            nc.vector.memset(xc, 0.0).then_inc(s_pad, 1)
            dve.wait_ge(s_in, 80)

            def v_out(m):
                h = m - 2 * GH
                for g in range(3):
                    n = min(4, TA - 4 * g)
                    dve.wait_ge(s_tr, 3 * h + g + 1)
                    nc.vector.tensor_copy(e.gvt[:, 4 * g:4 * g + n, h * GD:(h + 1) * GD],
                                          e.ps[:, 4 + (3 * h + g) % 2, 0:n * P].rearrange("p (a b) -> p a b", b=P)).then_inc(s_tok, 1)

            cs = 0
            for m in range(NB):
                dve.wait_ge(s_raw, 3 * m + 3)
                d = dst_of(m)
                if m >= 2 * GH + 2:
                    dve.wait_ge(s_tr, 3 * (m - 2 * GH - 1))
                D2 = (d[:, 0:LC], d[:, LC:LA])
                for a in range(2):
                    nc.vector.tensor_scalar(D2[a], V(m % 2, 0)[a], cw[:, 0, m:m + 1], None, ALU.mult).then_inc(s_taps, 1)
                dve.wait_ge(s_taps, 2 * (2 * m + 1))
                for a in range(2):
                    nc.vector.scalar_tensor_tensor(out=D2[a], in0=V(m % 2, 1)[a], scalar=cw[:, 1, m:m + 1], in1=D2[a],
                                                   op0=ALU.mult, op1=ALU.add).then_inc(s_taps, 1)
                dve.wait_ge(s_taps, 2 * (2 * m + 2))
                for a in range(2):
                    ins = nc.vector.scalar_tensor_tensor(out=D2[a], in0=V(m % 2, 2)[a], scalar=cw[:, 2, m:m + 1], in1=D2[a],
                                                         op0=ALU.mult, op1=ALU.add)
                ins.then_inc(s_conv, 1)
                if m - 1 >= 2 * GH:
                    v_out(m - 1)
            v_out(NB - 1)
            dve.wait_ge(s_ab, 1)
            step(nc.vector.tensor_copy(abt, e.ps[:, 6, 0:16 * TA].rearrange("p (t c) -> p t c", c=16)))
            z = abt[:, :, 0:8]
            dve.wait_ge(s_ao, 2)
            step(nc.vector.tensor_tensor(z, z, rw[:, 1].unsqueeze(1).broadcast_to([P, TA, 8]), ALU.add))
            step(nc.vector.tensor_scalar(abt[:, :, 8:16], z, -1.0, None, ALU.mult))
            step(nc.vector.tensor_tensor(abt[:, :, 8:16], abt[:, :, 8:16], z, ALU.min))
            dve.wait_ge(s_ao, 4)
            step(nc.vector.tensor_scalar(z, z, 0.0, None, ALU.max))
            step(nc.vector.tensor_tensor(z, z, abt[:, :, 8:16], ALU.add))
            step(nc.vector.tensor_scalar(rw[:, 0], rw[:, 0], -1.0, None, ALU.mult))
            step(nc.vector.tensor_tensor(e.g, z, rw[:, 0].unsqueeze(1).broadcast_to([P, TA, 8]), ALU.mult))
            for i, (m, r) in enumerate(norms):
                s, n = ranges[r]
                dve.wait_ge(s_ln, i + 1)
                step(nc.vector.reciprocal(inv[:, i % 2, 0:n], inv[:, i % 2, 0:n]))
                d = dst_of(m)[:, s:s + n]
                nc.vector.scalar_tensor_tensor(out=d, in0=d, scalar=GD ** -0.5 if m < GH else 1.0, in1=inv[:, i % 2, 0:n],
                                               op0=ALU.mult, op1=ALU.mult).then_inc(s_nrm, 1)
            for t in range(TA):
                dve.wait_ge(s_tr, 3 * GH + t + 1)
                nc.vector.tensor_copy(e.gkt[:, t], e.ps[:, 4 + t % 2, :]).then_inc(s_tok, 1)
    A.give("vT", "w_ring", "conv_in", "conv_w", "ab_rows", "ab", "gate_out", "sq", "inv", "hT")


def stage_gdn(e):
    nc, A, ps = e.nc, e.arena, e.ps
    H4 = GH * P
    e.og = A.take("og", TL, H4)
    F = {n: A.take("f_" + n, 2, H4) for n in ("D", "Dt", "eG", "N", "X", "Y", "T1", "C", "aqk", "kb", "vb", "kd", "qd", "wT", "u")}
    S = A.take("state", 2, H4)
    small = A.take("g_small", 2, 7, GH)
    b4 = lambda m: m.unsqueeze(1).broadcast_to([P, GH, P])
    h4 = lambda v: v.rearrange("p (h n) -> p h n", h=GH)
    col = lambda v: v.unsqueeze(2).broadcast_to([P, GH, P])
    hs = [slice(h * P, (h + 1) * P) for h in range(GH)]
    chunk = [[s for s in range(TA)], [TC - 1 - s if s < TC else TA - 1 - (s - TC) for s in range(TA)]]
    both = lambda name: [e.sem(f"gd_{name}{d}") for d in range(2)]
    LV = 6
    cum_mm, kk_mm, kq_mm, c0t_mm, t1_mm, y_mm, x_mm, w_mm, u_mm, o_mm, ku_mm = (
        both(n) for n in ("cum", "kk", "kq", "c0t", "t1m", "ym", "xm", "wm", "um", "om", "kum"))
    d_exp, dt_exp, sm_exp, eg_exp, t1_in, w_in_, u_in = (both(n) for n in ("dexp", "dtexp", "smexp", "egexp", "t1", "w", "u"))
    sm_in, d_arg, dt_arg, c_in, xy_in, prods, state, o_read, own = (
        both(n) for n in ("sm", "darg", "dtarg", "c", "xy", "prod", "state", "oread", "own"))
    with nc.Block() as block:
        @block.tensor
        def _(pe):
            for s in range(TA):
                lat = s >= TC
                for d in range(2):
                    c, B, g0 = chunk[d][s], 4 * d, 4 * d
                    tok = slice(c * P, (c + 1) * P)
                    cum = e.const(f"cum{d}")
                    pe.wait_ge(state[d], s + 1)
                    if s > TC:
                        pe.wait_ge(o_read[d], s - TC)
                    for h in range(GH):
                        nc.tensor.matmul(ps[:, B, hs[h]], e.g[:, c, g0 + h:g0 + h + 1].broadcast_to([P, P]), cum, start=True, stop=True)
                    nc.tensor.matmul(ps[:, B + 1, 0:GH], cum, e.g[:, c, g0:g0 + 4], start=True, stop=True)
                    nc.tensor.matmul(ps[:, B + 1, GH:2 * GH], e.const("ones"), e.g[:, c, g0:g0 + 4], start=True, stop=True).then_inc(cum_mm[d], 1)
                    for h in range(GH):
                        ins = nc.tensor.matmul(ps[:, B + 2, hs[h]], e.gkT[:, h, tok], e.gkT[:, h, tok], start=True, stop=True)
                    ins.then_inc(kk_mm[d], 1)
                    if lat:
                        for h in range(GH):
                            ins = nc.tensor.matmul(ps[:, B + 3, hs[h]], e.gkT[:, h, tok], e.gqT[:, h, tok], start=True, stop=True)
                        ins.then_inc(kq_mm[d], 1)
                for d in range(2):
                    B, C = 4 * d, F["C"][:, d]
                    pe.wait_ge(c_in[d], 7 * s + 1)
                    for h in range(GH):
                        ins = nc.tensor.matmul(ps[:, B + 1, hs[h]], C[:, hs[h]], e.ident, start=True, stop=True)
                    ins.then_inc(c0t_mm[d], 1)
                for lv in range(1, LV + 1):
                    for d in range(2):
                        B, C, Y = 4 * d, F["C"][:, d], F["Y"][:, d]
                        pe.wait_ge(c_in[d], 7 * s + lv + 1)
                        pe.wait_ge(xy_in[d], 7 * s + lv)
                        if lv == 1:
                            pe.wait_ge(eg_exp[d], s + 1)
                        for h in range(GH):
                            ins = nc.tensor.matmul(ps[:, B, hs[h]], C[:, hs[h]], Y[:, hs[h]], start=True, stop=True)
                        ins.then_inc(t1_mm[d], 1)
                    for d in range(2):
                        B, X, T1 = 4 * d, F["X"][:, d], F["T1"][:, d]
                        pe.wait_ge(t1_in[d], LV * s + lv)
                        for h in range(GH):
                            ins = nc.tensor.matmul(ps[:, B + 1, hs[h]], X[:, hs[h]], T1[:, hs[h]], start=True, stop=True)
                        ins.then_inc(y_mm[d], 1)
                        if lv < LV:
                            for h in range(GH):
                                ins = nc.tensor.matmul(ps[:, B + 2, hs[h]], T1[:, hs[h]], X[:, hs[h]], start=True, stop=True)
                            ins.then_inc(x_mm[d], 1)
                for d in range(2):
                    B, Y = 4 * d, F["Y"][:, d]
                    pe.wait_ge(prods[d], s + 1)
                    pe.wait_ge(xy_in[d], 7 * s + 7)
                    for h in range(GH):
                        ins = nc.tensor.matmul(ps[:, B + 2, hs[h]], F["kb"][:, d, hs[h]], Y[:, hs[h]], start=True, stop=True)
                    ins.then_inc(w_mm[d], 1)
                for d in range(2):
                    B, Y = 4 * d, F["Y"][:, d]
                    pe.wait_ge(w_in_[d], s + 1)
                    for h in range(GH):
                        nc.tensor.matmul(ps[:, B, hs[h]], Y[:, hs[h]], F["vb"][:, d, hs[h]], start=True, stop=False)
                        ins = nc.tensor.matmul(ps[:, B, hs[h]], F["wT"][:, d, hs[h]], S[:, d, hs[h]], start=False, stop=True)
                    ins.then_inc(u_mm[d], 1)
                for d in range(2):
                    B = 4 * d
                    pe.wait_ge(u_in[d], s + 1)
                    if lat:
                        for h in range(GH):
                            nc.tensor.matmul(ps[:, B + 3, hs[h]], F["qd"][:, d, hs[h]], S[:, d, hs[h]], start=True, stop=False)
                            ins = nc.tensor.matmul(ps[:, B + 3, hs[h]], F["aqk"][:, d, hs[h]], F["u"][:, d, hs[h]], start=False, stop=True)
                        ins.then_inc(o_mm[d], 1)
                    for h in range(GH):
                        ins = nc.tensor.matmul(ps[:, B + 1, hs[h]], F["kd"][:, d, hs[h]], F["u"][:, d, hs[h]], start=True, stop=True)
                    ins.then_inc(ku_mm[d], 1)

        @block.scalar
        def _(act):
            for s in range(TA):
                lat = s >= TC
                for d in range(2):
                    B = 4 * d
                    act.wait_ge(sm_in[d], s + 1)
                    nc.scalar.activation(small[:, d, 3:6], small[:, d, 0:3], ACT.Exp).then_inc(sm_exp[d], 1)
                    act.wait_ge(d_arg[d], s + 1)
                    nc.scalar.activation(F["D"][:, d], F["D"][:, d], ACT.Exp).then_inc(d_exp[d], 1)
                    act.wait_ge(dt_arg[d], s + 1)
                    if lat:
                        nc.scalar.activation(F["Dt"][:, d], F["Dt"][:, d], ACT.Exp).then_inc(dt_exp[d], 1)
                    nc.scalar.activation(F["eG"][:, d], ps[:, B, :], ACT.Exp).then_inc(eg_exp[d], 1)
                for lv in range(1, LV + 1):
                    for d in range(2):
                        act.wait_ge(t1_mm[d], LV * s + lv)
                        nc.scalar.activation(F["T1"][:, d], ps[:, 4 * d, :], ACT.Copy).then_inc(t1_in[d], 1)
                for d in range(2):
                    act.wait_ge(w_mm[d], s + 1)
                    nc.scalar.activation(F["wT"][:, d], ps[:, 4 * d + 2, :], ACT.Copy, scale=-1.0).then_inc(w_in_[d], 1)
                for d in range(2):
                    act.wait_ge(u_mm[d], s + 1)
                    nc.scalar.activation(F["u"][:, d], ps[:, 4 * d, :], ACT.Copy).then_inc(u_in[d], 1)

        @block.vector
        def _(dve):
            seen = [False] * TL
            step = [Steps(dve, own[d]) for d in range(2)]
            for d in range(2):
                nc.vector.memset(S[:, d], 0.0).then_inc(state[d], 1)
            TT = nc.vector.tensor_tensor
            for s in range(TA):
                lat = s >= TC
                for d in range(2):
                    B, sm, st = 4 * d, small[:, d], step[d]
                    D, Dt = F["D"][:, d], F["Dt"][:, d]
                    dve.wait_ge(cum_mm[d], s + 1)
                    st(nc.vector.tensor_copy(sm[:, 0:3:2], ps[:, B + 1, 0:2 * GH].rearrange("p (a h) -> p a h", a=2)))
                    TT(sm[:, 1], sm[:, 2], sm[:, 0], ALU.subtract).then_inc(sm_in[d], 1)
                    st(TT(h4(D), b4(e.const(f"strict{d}")), col(sm[:, 0]), ALU.add))
                    TT(D, D, ps[:, B, :], ALU.subtract).then_inc(d_arg[d], 1)
                    if lat:
                        st(TT(h4(Dt), b4(e.const(f"incl{d}")), col(sm[:, 0]), ALU.subtract))
                        TT(Dt, Dt, ps[:, B, :], ALU.add).then_inc(dt_arg[d], 1)
                    else:
                        dve.wait_ge(d_arg[d], s + 1)
                        dve.sem_inc(dt_arg[d], 1)
                for d in range(2):
                    B, sm, st, c = 4 * d, small[:, d], step[d], chunk[d][s]
                    bt = e.beta[:, c, 4 * d:4 * d + 4]
                    N, C, X, Y = (F[n][:, d] for n in ("N", "C", "X", "Y"))
                    dve.wait_ge(d_exp[d], s + 1)
                    dve.wait_ge(kk_mm[d], s + 1)
                    st(TT(N, F["D"][:, d], ps[:, B + 2, :], ALU.mult))
                    st(TT(h4(N), h4(N), col(bt), ALU.mult))
                    TT(h4(C), h4(N), b4(e.const(f"level{d}_0")), ALU.mult).then_inc(c_in[d], 1)
                    dve.wait_ge(c_in[d], 7 * s + 1)
                    st(TT(h4(X), b4(e.ident), h4(C), ALU.subtract))
                for d in range(2):
                    B, st = 4 * d, step[d]
                    N, C, X, Y = (F[n][:, d] for n in ("N", "C", "X", "Y"))
                    dve.wait_ge(c0t_mm[d], s + 1)
                    TT(h4(C), h4(N), b4(e.const(f"level{d}_1")), ALU.mult).then_inc(c_in[d], 1)
                    TT(h4(Y), b4(e.ident), ps[:, B + 1, :].rearrange("p (h n) -> p h n", h=GH), ALU.subtract).then_inc(xy_in[d], 1)
                for d in range(2):
                    B, sm, st, c = 4 * d, small[:, d], step[d], chunk[d][s]
                    bt = e.beta[:, c, 4 * d:4 * d + 4]
                    dve.wait_ge(sm_exp[d], s + 1)
                    st(TT(sm[:, 6], sm[:, 3], bt, ALU.mult))
                    TT(h4(F["kb"][:, d]), h4(e.gkt[:, c]), col(sm[:, 6]), ALU.mult)
                    TT(h4(F["vb"][:, d]), h4(e.gvt[:, c]), col(bt), ALU.mult)
                    if lat:
                        dve.wait_ge(dt_exp[d], s - TC + 1)
                        dve.wait_ge(kq_mm[d], s - TC + 1)
                        TT(F["aqk"][:, d], F["Dt"][:, d], ps[:, B + 3, :], ALU.mult)
                        dve.wait_ge(eg_exp[d], s + 1)
                        TT(h4(F["qd"][:, d]), e.gqT[:, :, c * P:(c + 1) * P], h4(F["eG"][:, d]), ALU.mult)
                    TT(h4(F["kd"][:, d]), h4(e.gkt[:, c]), col(sm[:, 4]), ALU.mult).then_inc(prods[d], 1)
                for lv in range(1, LV + 1):
                    if lv < LV:
                        for d in range(2):
                            dve.wait_ge(t1_mm[d], LV * s + lv)
                            TT(h4(F["C"][:, d]), h4(F["N"][:, d]), b4(e.const(f"level{d}_{lv + 1}")), ALU.mult).then_inc(c_in[d], 1)
                    for d in range(2):
                        B, X, Y = 4 * d, F["X"][:, d], F["Y"][:, d]
                        dve.wait_ge(y_mm[d], LV * s + lv)
                        if lv < LV:
                            TT(Y, Y, ps[:, B + 1, :], ALU.subtract).then_inc(own[d], 1)
                            step[d].n += 1
                            dve.wait_ge(x_mm[d], (LV - 1) * s + lv)
                            TT(X, X, ps[:, B + 2, :], ALU.subtract).then_inc(xy_in[d], 1)
                        else:
                            TT(Y, Y, ps[:, B + 1, :], ALU.subtract).then_inc(xy_in[d], 1)
                for d in range(2):
                    B, sm, st, c = 4 * d, small[:, d], step[d], chunk[d][s]
                    if lat:
                        j = c - TC
                        dve.wait_ge(o_mm[d], s - TC + 1)
                        if seen[j]:
                            TT(e.og[:, j], e.og[:, j], ps[:, B + 3, :], ALU.add).then_inc(o_read[d], 1)
                        else:
                            nc.vector.tensor_copy(e.og[:, j], ps[:, B + 3, :]).then_inc(o_read[d], 1)
                        seen[j] = True
                    dve.wait_ge(ku_mm[d], s + 1)
                    st(TT(h4(S[:, d]), h4(S[:, d]), col(sm[:, 5]), ALU.mult))
                    TT(S[:, d], S[:, d], ps[:, B + 1, :], ALU.add).then_inc(state[d], 1)
    A.give(*("f_" + n for n in F), "state", "g_small", "gqT", "gkT", "gvt", "gkt", "g", "beta")


def stage_gdn_out(e):
    nc, A = e.nc, e.arena
    e.catB = A.take("catB", GH, L)
    gate = A.take("gate", TL, GH * GD)
    gn = A.take("gdn_norm", GD)
    sq = A.take("gsq", 2, GH * GD)
    ss = A.take("gss", TL, GH)
    s_in, s_sq, s_ss, s_rt, s_own, s_y, s_tr, s_ev = (e.sem(f"go_{n}") for n in ("in", "sq", "ss", "rt", "own", "y", "tr", "ev"))
    h4 = lambda v: v.rearrange("p (h n) -> p h n", h=GH)
    with nc.Block() as block:
        @block.sync
        def _(sp):
            sp.dma_start(gate, e.gate_dram.rearrange("(t p) n -> p t n", p=P)).then_inc(s_in, 16)
            sp.dma_start(gn, broadcast_rows(e.in_["gdn_norm_g"][0])).then_inc(s_in, 16)

        @block.scalar
        def _(act):
            for t in range(TL):
                if t >= 2:
                    act.wait_ge(s_ss, t - 1)
                nc.scalar.activation(sq[:, t % 2], e.og[:, t], ACT.Square).then_inc(s_sq, 1)
            act.wait_ge(s_own, 1)
            nc.scalar.activation(ss, ss, ACT.Sqrt).then_inc(s_rt, 1)
            for t in range(TL):
                act.wait_ge(s_tr, t + 1)
                nc.scalar.activation(e.catB[:, :, t * P:(t + 1) * P], h4(e.ps[:, t % 4, :]), ACT.Copy).then_inc(s_ev, 1)

        @block.vector
        def _(dve):
            step = Steps(dve, s_own)
            for t in range(TL):
                dve.wait_ge(s_sq, t + 1)
                nc.vector.tensor_reduce(ss[:, t], h4(sq[:, t % 2]), AX, ALU.add).then_inc(s_ss, 1)
            dve.wait_ge(s_ss, TL)
            step(nc.vector.tensor_scalar(ss, ss, 1.0 / GD, EPS, ALU.mult, ALU.add))
            dve.wait_ge(s_rt, 1)
            step(nc.vector.reciprocal(ss, ss))
            dve.wait_ge(s_in, 32)
            for t in range(TL):
                step(nc.vector.tensor_tensor(h4(gate[:, t]), h4(gate[:, t]), ss[:, t].unsqueeze(2).broadcast_to([P, GH, GD]), ALU.mult))
                step(nc.vector.tensor_tensor(h4(gate[:, t]), h4(gate[:, t]), gn.unsqueeze(1).broadcast_to([P, GH, GD]), ALU.mult))
                nc.vector.tensor_tensor(e.og[:, t], e.og[:, t], gate[:, t], ALU.mult).then_inc(s_y, 1)

        @block.tensor
        def _(pe):
            for t in range(TL):
                pe.wait_ge(s_y, t + 1)
                if t >= 4:
                    pe.wait_ge(s_ev, t - 3)
                for h in range(GH):
                    ins = nc.tensor.transpose(e.ps[:, t % 4, h * P:(h + 1) * P], e.og[:, t, h * P:(h + 1) * P], e.ident)
                ins.then_inc(s_tr, 1)
    A.give("gate", "gdn_norm", "gsq", "gss", "og")


def stage_rows(e):
    nc, A = e.nc, e.arena
    e.rows = A.take("rows", 4, D)
    w = A.take("w_ring", 3, KD, 512)
    bm = A.take("b_row", 2, 512)
    g2 = A.take("norm2", D)
    w_mod = e.in_["w_mod"][0].rearrange("(k p) n -> p k n", p=P)
    s_w, s_b = [e.sem(f"mr_w{i}") for i in range(3)], [e.sem(f"mr_b{i}") for i in range(2)]
    s_in, s_mm, s_row, s_own = (e.sem(f"mr_{n}") for n in ("in", "mm", "row", "own"))
    NC = 8
    with nc.Block() as block:
        @block.sync
        def _(sp):
            for c in range(NC):
                if c >= 3:
                    sp.wait_ge(s_mm, c - 2)
                at = 2 * D + c * 512
                sp.dma_start(w[:, c % 3], w_mod[:, :, at:at + 512]).then_inc(s_w[c % 3], 16)
                if c >= 2:
                    sp.wait_ge(s_row, c - 1)
                sp.dma_start(bm[:, c % 2], broadcast_rows(e.in_["b_mod"][0, at:at + 512])).then_inc(s_b[c % 2], 16)
            sp.dma_start(g2, broadcast_rows(e.in_["norm2_g"][0])).then_inc(s_in, 16)

        @block.tensor
        def _(pe):
            for c in range(NC):
                pe.wait_ge(s_w[c % 3], 16 * (c // 3 + 1))
                if c >= 4:
                    pe.wait_ge(s_row, c - 3)
                for k in range(KD):
                    ins = nc.tensor.matmul(e.ps[:, c % 4, :], e.silu_c[:, k, 0:1].broadcast_to([P, P]), w[:, c % 3, k, :],
                                           start=(k == 0), stop=(k == KD - 1))
                ins.then_inc(s_mm, 1)

        @block.vector
        def _(dve):
            step = Steps(dve, s_own)
            for c in range(NC):
                dve.wait_ge(s_b[c % 2], 16 * (c // 2 + 1))
                dve.wait_ge(s_mm, c + 1)
                nc.vector.tensor_tensor(e.rows[:, c // 2, (c % 2) * 512:(c % 2 + 1) * 512], e.ps[:, c % 4, :], bm[:, c % 2], ALU.add).then_inc(s_row, 1)
            dve.wait_ge(s_row, NC)
            dve.wait_ge(s_in, 16)
            step(nc.vector.scalar_tensor_tensor(out=e.rows[:, 2], in0=e.rows[:, 2], scalar=1.0, in1=g2, op0=ALU.add, op1=ALU.mult))
    A.give("w_ring", "b_row", "norm2", "silu_c")


def stage_out_router(e):
    nc, A, ps = e.nc, e.arena, e.ps
    e.affT = A.take("affT", L)
    e.gateT = A.take("gateT", NE)
    e.idxT = A.take("idxT", NE)
    x1 = A.take("x1", TL, D)
    w = A.take("w_o", KD, D)
    xr = A.take("x_ring", 2, D)
    wr = A.take("w_r", KD, NE)
    h2 = A.take("h2", 2, D)
    h2T = A.take("h2T", 2, KD, P)
    junk = A.take("junk", D)
    ss = A.take("ss", TL)
    sm = A.take("r_small", 2, 4)
    pr = A.take("r_probs", 2, NE)
    e.x_dram = nc.dram_tensor("x_scratch", (L, D), F32).ap()
    e.h_dram = nc.dram_tensor("h_scratch", (L, D), F32).ap()
    s_x, s_hst = [e.sem(f"or_xin{i}") for i in range(2)], [e.sw_sem(f"or_hst{i}") for i in range(2)]
    s_w, s_mm, s_x1, s_x1a, s_sq, s_var, s_rt, s_own, s_h2, s_tr, s_hT, s_lg, s_mx, s_ex, s_pr, s_at, s_aff = (
        e.sem(f"or_{n}") for n in ("w", "mm", "x1", "x1a", "sq", "var", "rt", "own", "h2", "tr", "hT", "lg", "mx", "ex", "pr", "at", "aff"))
    s_xst = e.sw_sem("or_xst")
    cat = lambda k: e.catA[:, k] if k < 4 else e.catB[:, k - 4]
    with nc.Block() as block:
        @block.sync
        def _(sp):
            sp.dma_start(w, e.in_["w_out"][0].rearrange("(k p) n -> p k n", p=P)).then_inc(s_w, 16)
            sp.dma_start(wr, e.in_["w_router"][0].rearrange("(k p) n -> p k n", p=P)).then_inc(s_w, 16)
            for t in range(TL):
                if t >= 2:
                    sp.wait_ge(s_x1, t - 1)
                sp.dma_start(xr[:, t % 2], e.in_["x"][0, t * P:(t + 1) * P, :]).then_inc(s_x[t % 2], 16)

        @block.gpsimd
        def _(pool):
            for t in range(TL):
                pool.wait_ge(s_x1, t + 1)
                pool.dma_start(e.x_dram[t * P:(t + 1) * P, :], x1[:, t]).then_inc(s_xst, 16)
            for t in range(TL):
                pool.wait_ge(s_h2, t + 1)
                pool.dma_start(e.h_dram[t * P:(t + 1) * P, :], h2[:, t % 2]).then_inc(s_hst[t % 2], 16)
            pool.wait_ge(s_xst, 16 * TL)
            for i in range(2):
                pool.wait_ge(s_hst[i], 16 * TL // 2)

        @block.tensor
        def _(pe):
            pe.wait_ge(s_w, 32)
            for t in range(TL):
                if t >= 2:
                    pe.wait_ge(s_x1a, t - 1)
                for j in range(2):
                    for k in range(KD):
                        ins = nc.tensor.matmul(ps[:, 2 * (t % 2) + j, :], cat(k)[:, t * P:(t + 1) * P], w[:, k, j * 512:(j + 1) * 512],
                                               start=(k == 0), stop=(k == KD - 1))
                ins.then_inc(s_mm, 1)
            for t in range(TL):
                pe.wait_ge(s_h2, t + 1)
                if t >= 1:
                    pe.wait_ge(s_hT, t)
                for k in range(KD):
                    ins = nc.tensor.transpose(ps[:, 4 + k // 4, (k % 4) * P:(k % 4 + 1) * P], h2[:, t % 2, k * P:(k + 1) * P], e.ident)
                ins.then_inc(s_tr, 1)
                pe.wait_ge(s_hT, t + 1)
                if t >= 1:
                    pe.wait_ge(s_pr, t)
                for k in range(KD):
                    ins = nc.tensor.matmul(ps[:, 6, 0:NE], h2T[:, t % 2, k], wr[:, k], start=(k == 0), stop=(k == KD - 1))
                ins.then_inc(s_lg, 1)
                pe.wait_ge(s_pr, t + 1)
                if t >= 1:
                    pe.wait_ge(s_aff, t)
                nc.tensor.transpose(ps[0:NE, 7, 0:P], pr[:, t % 2], e.ident).then_inc(s_at, 1)

        @block.scalar
        def _(act):
            for t in range(TL):
                act.wait_ge(s_x1, t + 1)
                if t:
                    act.wait_ge(s_sq, t)
                nc.scalar.activation(junk, x1[:, t], ACT.Square, accum_out=ss[:, t:t + 1]).then_inc(s_sq, 1)
            act.wait_ge(s_var, 1)
            nc.scalar.activation(ss, ss, ACT.Sqrt).then_inc(s_rt, 1)
            for t in range(TL):
                act.wait_ge(s_tr, t + 1)
                if t >= 2:
                    act.wait_ge(s_lg, t - 1)
                nc.scalar.activation(h2T[:, t % 2], ps[:, 4:6, :].rearrange("p a (b c) -> p (a b) c", c=P), ACT.Copy).then_inc(s_hT, 1)
                act.wait_ge(s_mx, t + 1)
                nc.scalar.activation(pr[:, t % 2], ps[:, 6, 0:NE], ACT.Exp, bias=sm[:, t % 2, 1:2], accum_out=sm[:, t % 2, 2:3]).then_inc(s_ex, 1)

        @block.vector
        def _(dve):
            step = Steps(dve, s_own)
            for t in range(TL):
                dve.wait_ge(s_mm, t + 1)
                v = x1[:, t].rearrange("p (a n) -> p a n", a=2)
                nc.vector.tensor_tensor(v, ps[:, 2 * (t % 2):2 * (t % 2) + 2, :], e.rows[:, 0].rearrange("p (a n) -> p a n", a=2), ALU.mult).then_inc(s_x1a, 1)
                dve.wait_ge(s_x1a, t + 1)
                dve.wait_ge(s_x[t % 2], 16 * (t // 2 + 1))
                nc.vector.tensor_tensor(x1[:, t], x1[:, t], xr[:, t % 2], ALU.add).then_inc(s_x1, 1)
            dve.wait_ge(s_sq, TL)
            step(nc.vector.tensor_scalar(ss, ss, 1.0 / D, EPS, ALU.mult, ALU.add))
            nc.vector.reciprocal(ss, ss).then_inc(s_var, 1)
            dve.wait_ge(s_rt, 1)
            for t in range(TL):
                b = t % 2
                if t >= 2:
                    dve.wait_ge(s_hst[b], 16 * (t // 2))
                    dve.wait_ge(s_tr, t - 1)
                step(nc.vector.scalar_tensor_tensor(out=h2[:, b], in0=x1[:, t], scalar=ss[:, t:t + 1], in1=e.rows[:, 2], op0=ALU.mult, op1=ALU.mult))
                nc.vector.tensor_tensor(h2[:, b], h2[:, b], e.rows[:, 1], ALU.add).then_inc(s_h2, 1)
                dve.wait_ge(s_lg, t + 1)
                step(nc.vector.tensor_reduce(sm[:, b, 0:1], ps[:, 6, 0:NE], AX, ALU.max))
                nc.vector.tensor_scalar(sm[:, b, 1:2], sm[:, b, 0:1], -1.0, None, ALU.mult).then_inc(s_mx, 1)
                dve.wait_ge(s_ex, t + 1)
                step(nc.vector.reciprocal(sm[:, b, 3:4], sm[:, b, 2:3]))
                nc.vector.tensor_scalar(pr[:, b], pr[:, b], sm[:, b, 3:4], None, ALU.mult).then_inc(s_pr, 1)
                dve.wait_ge(s_at, t + 1)
                nc.vector.tensor_copy(e.affT[0:NE, t * P:(t + 1) * P], ps[0:NE, 7, 0:P]).then_inc(s_aff, 1)
    A.give("x1", "w_o", "x_ring", "w_r", "h2", "h2T", "junk", "ss", "r_small", "r_probs", "catA", "catB")


def stage_choose(e):
    nc, A, ps = e.nc, e.arena, e.ps
    val = A.take("val", CAP)
    idx = A.take("idx", CAP)
    idf = A.take("idxf", CAP)
    s_max, s_idx, s_rep, s_f, s_tr, s_own = (e.sem(f"ch_{n}") for n in ("max", "idx", "rep", "f", "tr", "own"))
    idx_u = idx.bitcast(U32)
    with nc.Block() as block:
        @block.vector
        def _(dve):
            a = e.affT[0:NE, :]
            for r in range(CAP // 8):
                s8 = slice(8 * r, 8 * r + 8)
                if r:
                    dve.wait_ge(s_rep, r)
                nc.vector.max(val[0:NE, s8], a).then_inc(s_max, 1)
                dve.wait_ge(s_max, r + 1)
                nc.vector.max_index(idx_u[0:NE, s8], val[0:NE, s8], a).then_inc(s_idx, 1)
                dve.wait_ge(s_idx, r + 1)
                nc.vector.match_replace(a, val[0:NE, s8], a, -1.0).then_inc(s_rep, 1)
            nc.vector.tensor_copy(idf[0:NE, :], idx_u[0:NE, :]).then_inc(s_f, 1)
            dve.wait_ge(s_tr, 1)
            nc.vector.tensor_copy(e.idxT.bitcast(U32), ps[:, 0, 0:NE]).then_inc(s_own, 1)
            nc.vector.tensor_copy(e.gateT, ps[:, 0, NE:2 * NE]).then_inc(s_own, 1)

        @block.tensor
        def _(pe):
            pe.wait_ge(s_f, 1)
            nc.tensor.transpose(ps[:, 0, 0:NE], idf[0:NE, :], e.ident[0:NE, 0:NE])
            nc.tensor.transpose(ps[:, 0, NE:2 * NE], val[0:NE, :], e.ident[0:NE, 0:NE]).then_inc(s_tr, 1)
    A.give("val", "idx", "idxf", "affT")


def stage_experts(e):
    nc, A, ps = e.nc, e.arena, e.ps
    names = ("gate", "up", "down")
    W = {n: A.take("w_" + n, 2, 4, FF) for n in names}
    xe = A.take("xe", 2, D)
    xT = A.take("xT", 2, KD, P)
    sg = A.take("sg", FF)
    hid = A.take("hid", FF)
    hT = A.take("hidT", KD, P)
    y = A.take("y", D)
    gcol = A.take("gcol", 1)
    s_w = {n: [e.sem(f"ex_{n}{i}") for i in range(2)] for n in names}
    s_xe = [e.sw_sem(f"ex_xe{i}") for i in range(2)]
    s_xt, s_xT, s_g, s_u, s_sg, s_hid, s_ht, s_hT, s_d, s_gc, s_y = (
        e.sem(f"ex_{n}") for n in ("xt", "xTin", "gmm", "umm", "sg", "hid", "ht", "hTin", "dmm", "gcol", "y"))
    s_out = e.sw_sem("ex_out")
    done = {"gate": s_g, "up": s_u, "down": s_d}
    src = {n: e.in_["w_" + n][0].rearrange("e (p k) n -> e p k n", k=KD) for n in names}
    with nc.Block() as block:
        @block.sync
        def _(sp):
            def load(n, i, first):
                for half in range(2):
                    if not first:
                        sp.wait_ge(done[n], 2 * i + half - 1)
                    sp.dma_start(W[n][:, half], src[n][bass.ds(i, 1), :, 4 * half:4 * half + 4, :].rearrange("a p k n -> p (a k) n")).then_inc(s_w[n][half], 16)
            for n in names:
                load(n, 0, True)
            load("gate", 1, False)
            load("up", 1, False)
            with sp.Fori(2, NE) as i:
                load("gate", i, False)
                load("down", i - 1, False)
                load("up", i, False)
            load("down", NE - 1, False)

        @block.gpsimd
        def _(pool):
            def gather(i):
                if i >= 2:
                    pool.wait_ge(s_xt, i - 1)
                nc.gpsimd.indirect_dma_start(out=xe[:, i % 2], out_offset=None, in_=e.h_dram,
                                             in_offset=bass.IndirectOffsetOnAxis(ap=e.idxT[:, i:i + 1].bitcast(U32), axis=0)).then_inc(s_xe[i % 2], 16)

            def scatter(i):
                pool.wait_ge(s_y, i + 1)
                nc.gpsimd.indirect_dma_start(out=e.x_dram, out_offset=bass.IndirectOffsetOnAxis(ap=e.idxT[:, i:i + 1].bitcast(U32), axis=0), in_=y,
                                             in_offset=None, compute_op=ALU.add).then_inc(s_out, 16)
                pool.wait_ge(s_out, 16 * (i + 1))
            gather(0)
            gather(1)
            for i in range(NE):
                if 1 <= i < NE - 1:
                    gather(i + 1)
                if i:
                    scatter(i - 1)
            scatter(NE - 1)

        @block.tensor
        def _(pe):
            def half(n, banks, lhs, i, h):
                pe.wait_ge(s_w[n][h], 16 * (i + 1))
                for k in range(4 * h, 4 * h + 4):
                    for j in range(2):
                        ins = nc.tensor.matmul(ps[:, banks + j, :], lhs[:, k], W[n][:, h, k % 4, j * 512:(j + 1) * 512],
                                               start=(k == 0), stop=(k == KD - 1))
                ins.then_inc(done[n], 1)

            def turn(rows, signal):
                for k in range(KD):
                    ins = nc.tensor.transpose(ps[:, 6 + k // 4, (k % 4) * P:(k % 4 + 1) * P], rows.rearrange("p (m k) -> p k m", k=KD)[:, k], e.ident)
                ins.then_inc(signal, 1)

            def down(i, first):
                pe.wait_ge(s_hT, i + 1)
                if not first:
                    pe.wait_ge(s_y, i)
                for h in range(2):
                    half("down", 4, hT, i, h)

            def body(i, b, first, last, second=False, rounds=None):
                x = xT[:, b]
                pe.wait_ge(s_xT, i + 1)
                if not first:
                    pe.wait_ge(s_sg, i)
                half("gate", 0, x, i, 0)
                if not first:
                    pe.wait_ge(s_hid, i)
                    turn(hid, s_ht)
                half("gate", 0, x, i, 1)
                if not first:
                    down(i - 1, second)
                if not last:
                    pe.wait_ge(s_xe[1 - b], 16 * rounds)
                    turn(xe[:, 1 - b], s_xt)
                for h in range(2):
                    half("up", 2, x, i, h)

            pe.wait_ge(s_xe[0], 16)
            turn(xe[:, 0], s_xt)
            body(0, 0, True, False, rounds=1)
            body(1, 1, False, False, second=True, rounds=2)
            with pe.Fori(1, NE // 2 - 1) as j:
                body(2 * j, 0, False, False, rounds=j + 1)
                body(2 * j + 1, 1, False, False, rounds=j + 2)
            body(NE - 2, 0, False, False, rounds=NE // 2)
            body(NE - 1, 1, False, True)
            pe.wait_ge(s_hid, NE)
            turn(hid, s_ht)
            down(NE - 1, False)

        @block.scalar
        def _(act):
            def rows_in(i, b, first):
                act.wait_ge(s_xt, i + 1)
                if not first:
                    act.wait_ge(s_u, 2 * i - 2)
                nc.scalar.activation(xT[:, b], ps[:, 6:8, :].rearrange("p a (b c) -> p (a b) c", c=P), ACT.Copy).then_inc(s_xT, 1)

            def gate(i, first):
                act.wait_ge(s_g, 2 * i + 2)
                if not first:
                    act.wait_ge(s_hid, i)
                nc.scalar.activation(sg, ps[:, 0:2, :].rearrange("p a b -> p (a b)"), ACT.Silu).then_inc(s_sg, 1)
            rows_in(0, 0, True)
            gate(0, True)
            rows_in(1, 1, True)
            gate(1, False)
            with act.Fori(1, NE // 2) as j:
                for b in range(2):
                    rows_in(2 * j + b, b, False)
                    gate(2 * j + b, False)

        @block.vector
        def _(dve):
            def hidden(i, first):
                dve.wait_ge(s_u, 2 * i + 2)
                dve.wait_ge(s_sg, i + 1)
                if not first:
                    dve.wait_ge(s_ht, i)
                nc.vector.tensor_tensor(hid, sg, ps[:, 2:4, :].rearrange("p a b -> p (a b)"), ALU.mult).then_inc(s_hid, 1)

            def output(i, first):
                dve.wait_ge(s_ht, i + 1)
                if not first:
                    dve.wait_ge(s_d, 2 * i)
                nc.vector.tensor_copy(hT, ps[:, 6:8, :].rearrange("p a (b c) -> p (a b) c", c=P)).then_inc(s_hT, 1)
                if not first:
                    dve.wait_ge(s_y, i)
                nc.vector.tensor_copy(gcol, e.gateT[:, bass.ds(i, 1)]).then_inc(s_gc, 1)
                dve.wait_ge(s_gc, i + 1)
                dve.wait_ge(s_d, 2 * i + 2)
                if not first:
                    dve.wait_ge(s_out, 16 * i)
                nc.vector.scalar_tensor_tensor(out=y, in0=ps[:, 4:6, :].rearrange("p a b -> p (a b)"), scalar=gcol, in1=e.rows[:, 3],
                                               op0=ALU.mult, op1=ALU.mult).then_inc(s_y, 1)
            hidden(0, True)
            output(0, True)
            with dve.Fori(1, NE) as i:
                hidden(i, False)
                output(i, False)
    A.give(*("w_" + n for n in names), "xe", "xT", "sg", "hid", "hidT", "y", "gcol", "rows", "idxT", "gateT")


def stage_between(e):
    nc, A, ps = e.nc, e.arena, e.ps
    e.hT2 = A.take("hT2", KD, L)
    e.hT_dram = nc.dram_tensor("hT_scratch", (P, KD * L), F32).ap()
    e.x3_dram = nc.dram_tensor("x3_scratch", (L, D), F32).ap()
    x = A.take("x", TL, D)
    rows = A.take("gains", 2, D)
    junk = A.take("junk", D)
    ss = A.take("ss", 2, TL)
    s_x = [e.sem(f"bt_xin{i}") for i in range(TL)]
    s_in, s_own, s_rt, s_tr, s_ev, s_hst, s_x3 = (e.sem(f"bt_{n}") for n in ("in", "own", "rt", "tr", "ev", "hst", "x3"))
    s_st = [e.sem(f"bt_st{i}") for i in range(TL)]
    s_sq, s_var, s_n = ([e.sem(f"bt_{n}{i}") for i in range(2)] for n in ("sq", "var", "n"))
    with nc.Block() as block:
        @block.sync
        def _(sp):
            sp.dma_start(rows[:, 0], broadcast_rows(e.in_["final_g"])).then_inc(s_in, 16)
            sp.dma_start(rows[:, 1], broadcast_rows(e.in_["norm1_g_2"][0])).then_inc(s_in, 16)
            for t in range(TL):
                sp.dma_start(x[:, t], e.x_dram[t * P:(t + 1) * P, :]).then_inc(s_x[t], 16)
            for t in range(TL):
                sp.wait_ge(s_x3, t + 1)
                sp.dma_start(e.x3_dram[t * P:(t + 1) * P, :], x[:, t]).then_inc(s_st[t], 16)
            sp.wait_ge(s_ev, 2 * TL)
            sp.dma_start(e.hT_dram, e.hT2.rearrange("p a b -> p (a b)")).then_inc(s_hst, 16)
            sp.wait_ge(s_hst, 16)
            for t in range(TL):
                sp.wait_ge(s_st[t], 16)

        @block.scalar
        def _(act):
            n = 0
            for i in range(2):
                for t in range(TL):
                    if i == 0:
                        act.wait_ge(s_x[t], 16)
                    else:
                        act.wait_ge(s_x3, t + 1)
                    if n:
                        act.wait_ge(s_sq[(n - 1) // TL], (n - 1) % TL + 1)
                    nc.scalar.activation(junk, x[:, t], ACT.Square, accum_out=ss[:, i, t:t + 1]).then_inc(s_sq[i], 1)
                    n += 1
                act.wait_ge(s_var[i], 1)
                nc.scalar.activation(ss[:, i], ss[:, i], ACT.Sqrt).then_inc(s_rt, 1)
            for t in range(TL):
                act.wait_ge(s_tr, 2 * t + 2)
                for j in range(2):
                    ins = nc.scalar.activation(e.hT2[:, 4 * j:4 * j + 4, t * P:(t + 1) * P],
                                               ps[:, (2 * t + j) % 8, :].rearrange("p (a b) -> p a b", b=P), ACT.Copy)
                    ins.then_inc(s_ev, 1)

        @block.vector
        def _(dve):
            step = Steps(dve, s_own)
            dve.wait_ge(s_in, 32)
            for i in range(2):
                dve.wait_ge(s_sq[i], TL)
                step(nc.vector.tensor_scalar(ss[:, i], ss[:, i], 1.0 / D, EPS, ALU.mult, ALU.add))
                nc.vector.reciprocal(ss[:, i], ss[:, i]).then_inc(s_var[i], 1)
                dve.wait_ge(s_rt, i + 1)
                for t in range(TL):
                    if i == 1:
                        dve.wait_ge(s_st[t], 16)
                    nc.vector.scalar_tensor_tensor(out=x[:, t], in0=x[:, t], scalar=ss[:, i, t:t + 1], in1=rows[:, i],
                                                   op0=ALU.mult, op1=ALU.mult).then_inc(s_x3 if i == 0 else s_n[1], 1)

        @block.tensor
        def _(pe):
            for t in range(TL):
                pe.wait_ge(s_n[1], t + 1)
                if t >= 4:
                    pe.wait_ge(s_ev, 2 * (t - 3))
                for k in range(KD):
                    ins = nc.tensor.transpose(ps[:, (2 * t + k // 4) % 8, (k % 4) * P:(k % 4 + 1) * P], x[:, t, k * P:(k + 1) * P], e.ident)
                    if k % 4 == 3:
                        ins.then_inc(s_tr, 1)
    A.give("x", "gains", "junk", "ss")


RQ, RK, RV, RQI, RKI, RWI, RN = 0, 512, 576, 640, 896, 960, 964


def stage_project2(e):
    nc, A, ps = e.nc, e.arena, e.ps
    e.U = A.take("U", SG, CH, SP)
    e.r = A.take("r", TL, RN)
    w = A.take("w_ring", 3, KD, 512)
    w_in = e.in_["w_in_2"][0].rearrange("(k p) n -> p k n", p=P)
    chunks = ((0, 512), (512, 512), (1024, RN - 512))
    s_w = [e.sem(f"p2_w{i}") for i in range(3)]
    s_mm, s_ev = e.sem("p2_mm"), e.sem("p2_ev")
    with nc.Block() as block:
        @block.sync
        def _(sp):
            for c, (at, n) in enumerate(chunks):
                sp.dma_start(w[:, c, :, 0:n], w_in[:, :, at:at + n]).then_inc(s_w[c], 16)

        @block.tensor
        def _(pe):
            for i in range(3 * TL):
                c, t = divmod(i, TL)
                n = chunks[c][1]
                if t == 0:
                    pe.wait_ge(s_w[c], 16)
                if i >= 8:
                    pe.wait_ge(s_ev, i - 7)
                for k in range(KD):
                    lhs = e.hT2[:, k, t:L:CH] if c == 0 else e.hT2[:, k, t * P:(t + 1) * P]
                    ins = nc.tensor.matmul(ps[:, i % 8, 0:n], lhs, w[:, c, k, 0:n], start=(k == 0), stop=(k == KD - 1))
                ins.then_inc(s_mm, 1)

        @block.scalar
        def _(act):
            for i in range(3 * TL):
                c, t = divmod(i, TL)
                n = chunks[c][1]
                act.wait_ge(s_mm, i + 1)
                dst = e.U[:, :, t] if c == 0 else e.r[:, t, (c - 1) * 512:(c - 1) * 512 + n]
                src = ps[:, i % 8, 0:n].rearrange("p (g c) -> p g c", c=SP) if c == 0 else ps[:, i % 8, 0:n]
                nc.scalar.activation(dst, src, ACT.Copy).then_inc(s_ev, 1)
    A.give("w_ring", "hT2")


TWO_PI = 2 * np.pi


def stage_ssm_tables(e):
    nc, A, ps = e.nc, e.arena, e.ps
    J = SG // 2
    e.Wr, e.nWi = A.take("Wr", J, (CH + 1), SP), A.take("nWi", J, (CH + 1), SP)
    e.Bc = A.take("Bc", 2, J, SP)
    e.VT = A.take("VT", 2, J, P)
    e.E = A.take("E", 2, J, P)
    e.mag8 = A.take("mag8", J)
    e.uT = A.take("uT", SG, P)
    V = A.take("V", 2 * J, CH, SP)
    q = A.take("q_small", 40, J)
    Bn = A.take("Bn", 2, J, SP)
    Cn = A.take("Cn", 2, 4, P)
    Cc = A.take("Cc", 2, J, SP)
    pw = A.take("powers", 2, J * (CH + 1))
    tmp = A.take("ssm_tmp", J * (CH + 1) * SP)
    tmp2 = A.take("ssm_tmp2", J * (CH + 1) * SP)
    s_in, s_own, s_act, s_tr, s_ct, s_c, s_v, s_u, s_uo, s_vt, s_ang = (e.sem(f"st_{n}") for n in ("in", "own", "act", "tr", "ct", "c", "v", "u", "uo", "vt", "ang"))
    g = lambda n: e.in_[n + "_2"][0]
    (AR, AI, DT, T1, MAG, MAG8, TH, KK, R, SN_, CS, R2, ABR, ABI, DEN, NR, CR, CI, X1, X2, P2R, P2I, P4R, P4I, P8R, P8I, FR, FI, G1, G2) = range(30)
    c_ = lambda i: q[:, i]
    with nc.Block() as block:
        @block.sync
        def _(sp):
            with nc.allow_non_contiguous_dma("small parameters by state"):
                for name, i in (("A_re", AR), ("A_im", AI)):
                    for h in range(2):
                        sp.dma_start(q[64 * h:64 * h + 64, i], g(name).rearrange("(j h) n -> h n j", h=2)[h]).then_inc(s_in, 16)
                for h in range(2):
                    sp.dma_start(q[64 * h:64 * h + 64, DT], g("log_dt").rearrange("(j h) -> h j", h=2)[h].partition_broadcast(64)).then_inc(s_in, 16)
                for name, i in (("B_re", 0), ("B_im", 1)):
                    for h in range(2):
                        sp.dma_start(Bn[64 * h:64 * h + 64, i], g(name).rearrange("(j h) n p -> h n j p", h=2)[h]).then_inc(s_in, 16)
                for name, i in (("C_re", 0), ("C_im", 1)):
                    for h in range(2):
                        sp.dma_start(Cn[:, i, :, 64 * h:64 * h + 64], g(name).rearrange("(a g) p n -> (g p) a n", a=4)).then_inc(s_in, 16)

        @block.tensor
        def _(pe):
            for i in range(8):
                if i >= 2:
                    pe.wait_ge(s_uo, i - 1)
                for k in range(4):
                    gr = 4 * i + k
                    ins = nc.tensor.transpose(ps[:, 4 + i % 2, k * P:(k + 1) * P], e.U[:, gr].rearrange("p a b -> p (a b)"), e.ident)
                ins.then_inc(s_u, 1)
            pe.wait_ge(s_in, 14 * 16)
            for i in range(2):
                for a in range(4):
                    ins = nc.tensor.transpose(ps[:, i, a * P:(a + 1) * P], Cn[:, i, a, :], e.ident)
                ins.then_inc(s_ct, 1)
            pe.wait_ge(s_v, 1)
            for i in range(8):
                if i < 2:
                    pe.wait_ge(s_c, 2)
                else:
                    pe.wait_ge(s_vt, i - 1)
                for k in range(4):
                    ins = nc.tensor.transpose(ps[:, i % 2, k * P:(k + 1) * P], V[:, 4 * i + k].rearrange("p a b -> p (a b)"), e.ident)
                ins.then_inc(s_tr, 1)

        @block.scalar
        def _(act):
            for i in range(8):
                act.wait_ge(s_u, i + 1)
                nc.scalar.activation(e.uT[:, 4 * i:4 * i + 4], ps[:, 4 + i % 2, :].rearrange("p (a b) -> p a b", b=P), ACT.Copy).then_inc(s_uo, 1)
            act.wait_ge(s_ang, 1)
            nc.scalar.activation(q[:, SN_:SN_ + 2], q[:, SN_:SN_ + 2], ACT.Sin).then_inc(s_act, 1)
            for i in range(8):
                act.wait_ge(s_tr, i + 1)
                nc.scalar.activation(e.VT[:, i // 4, 4 * (i % 4):4 * (i % 4) + 4], ps[:, i % 2, :].rearrange("p (a b) -> p a b", b=P), ACT.Copy).then_inc(s_vt, 1)

        @block.vector
        def _(dve):
            step = Steps(dve, s_own)
            TT, TS, STT = nc.vector.tensor_tensor, nc.vector.tensor_scalar, nc.vector.scalar_tensor_tensor

            def cmul(o_r, o_i, a_r, a_i, b_r, b_i, t1, t2):
                step(TT(o_r, a_r, b_r, ALU.mult))
                step(TT(t1, a_i, b_i, ALU.mult))
                step(TT(o_r, o_r, t1, ALU.subtract))
                step(TT(o_i, a_r, b_i, ALU.mult))
                step(TT(t2, a_i, b_r, ALU.mult))
                step(TT(o_i, o_i, t2, ALU.add))

            def exp(out, x):
                n = out.shape[1]
                k, rest, p = (q[:, 30 + 2 * i:30 + 2 * i + n] for i in range(3))
                magic = 12582912.0
                hi = 0.693359375
                lo = float(np.log(2.0) - hi)
                step(TS(rest, x, 88.0, -87.0, ALU.min, ALU.max))
                step(TS(k, rest, float(1 / np.log(2.0)), magic, ALU.mult, ALU.add))
                step(TS(k, k, -magic, None, ALU.add))
                step(STT(out=rest, in0=k, scalar=-hi, in1=rest, op0=ALU.mult, op1=ALU.add))
                step(STT(out=rest, in0=k, scalar=-lo, in1=rest, op0=ALU.mult, op1=ALU.add))
                c = [1.0]
                for i in range(1, 9):
                    c.append(c[-1] / i)
                step(TS(p, rest, c[8], None, ALU.mult))
                for i in range(7, 0, -1):
                    step(STT(out=p, in0=p, scalar=c[i], in1=rest, op0=ALU.add, op1=ALU.mult))
                step(TS(p, p, 1.0, None, ALU.add))
                step(TS(k, k, 127.0, float(2 ** 23), ALU.add, ALU.mult))
                step(nc.vector.tensor_copy(rest.bitcast(I32), k))
                step(TT(out, p, rest, ALU.mult))

            dve.wait_ge(s_in, 14 * 16)
            exp(q[:, DT:DT + 1], q[:, DT:DT + 1])
            step(TT(c_(T1), c_(AR), c_(DT), ALU.mult))
            step(TS(c_(MAG8), c_(T1), 8.0, None, ALU.mult))
            step(nc.vector.tensor_copy(c_(MAG), c_(T1)))
            exp(q[:, MAG:MAG + 2], q[:, MAG:MAG + 2])
            step(nc.vector.tensor_copy(e.mag8, c_(MAG8)))
            step(TT(c_(TH), c_(AI), c_(DT), ALU.mult))
            MAGIC = 12582912.0
            step(TS(c_(KK), c_(TH), 1.0 / TWO_PI, MAGIC, ALU.mult, ALU.add))
            step(TS(c_(KK), c_(KK), -MAGIC, None, ALU.add))
            c1 = 6.28125
            c2 = float(np.float32(round((TWO_PI - c1) * 2 ** 20) / 2 ** 20))
            c3 = TWO_PI - c1 - c2
            step(TS(c_(R), c_(KK), -c1, None, ALU.mult))
            step(TT(c_(R), c_(TH), c_(R), ALU.add))
            step(nc.vector.scalar_tensor_tensor(out=c_(R), in0=c_(KK), scalar=-c2, in1=c_(R), op0=ALU.mult, op1=ALU.add))
            step(nc.vector.scalar_tensor_tensor(out=c_(R), in0=c_(KK), scalar=-c3, in1=c_(R), op0=ALU.mult, op1=ALU.add))
            step(TS(c_(R2), c_(R), np.pi / 2, -TWO_PI, ALU.is_gt, ALU.mult))
            step(TT(c_(R2), c_(R2), c_(R), ALU.add))
            step(TS(c_(R2), c_(R2), np.pi / 2, None, ALU.add))
            step(TS(c_(SN_), c_(R), 3.1415925, -3.1415925, ALU.min, ALU.max))
            TS(c_(CS), c_(R2), 3.1415925, -3.1415925, ALU.min, ALU.max).then_inc(s_ang, 1)
            step(TT(c_(DEN), c_(AR), c_(AR), ALU.mult))
            step(TT(c_(X1), c_(AI), c_(AI), ALU.mult))
            step(TT(c_(DEN), c_(DEN), c_(X1), ALU.add))
            step(nc.vector.reciprocal(c_(DEN), c_(DEN)))
            dve.wait_ge(s_act, 1)
            step(TT(c_(ABR), c_(MAG), c_(CS), ALU.mult))
            step(TT(c_(ABI), c_(MAG), c_(SN_), ALU.mult))
            step(TS(c_(NR), c_(ABR), -1.0, None, ALU.add))
            step(TT(c_(CR), c_(NR), c_(AR), ALU.mult))
            step(TT(c_(X1), c_(ABI), c_(AI), ALU.mult))
            step(TT(c_(CR), c_(CR), c_(X1), ALU.add))
            step(TT(c_(CR), c_(CR), c_(DEN), ALU.mult))
            step(TT(c_(CI), c_(ABI), c_(AR), ALU.mult))
            step(TT(c_(X2), c_(NR), c_(AI), ALU.mult))
            step(TT(c_(CI), c_(CI), c_(X2), ALU.subtract))
            step(TT(c_(CI), c_(CI), c_(DEN), ALU.mult))
            bc = lambda v, *s: v.unsqueeze(2).broadcast_to([P, J, s[0]])
            t3 = lambda v, n: v[:, 0:J * n].rearrange("p (j a) -> p j a", j=J)
            cmul(e.Bc[:, 0], e.Bc[:, 1], Bn[:, 0], Bn[:, 1], bc(c_(CR), SP), bc(c_(CI), SP), t3(tmp, SP), t3(tmp2, SP))
            for i in range(2):
                dve.wait_ge(s_ct, i + 1)
                for h in range(2):
                    src = ps[64 * h:64 * h + 64, i, :].rearrange("p (j h c) -> p j h c", h=2, c=SP)[:, :, h]
                    ins = nc.vector.tensor_copy(Cc[64 * h:64 * h + 64, i], src)
                ins.then_inc(s_c, 1)
            pr, pi = (pw[:, i].rearrange("p (j t) -> p j t", j=J) for i in range(2))
            step(nc.vector.memset(pr[:, :, 0], 1.0))
            step(nc.vector.memset(pi[:, :, 0], 0.0))
            step(nc.vector.tensor_copy(pr[:, :, 1], c_(ABR)))
            step(nc.vector.tensor_copy(pi[:, :, 1], c_(ABI)))
            for m in (1, 2, 4):
                b = [v[:, :, m:m + 1].broadcast_to([P, J, m]) for v in (pr, pi)]
                cmul(pr[:, :, m + 1:2 * m + 1], pi[:, :, m + 1:2 * m + 1], pr[:, :, 1:m + 1], pi[:, :, 1:m + 1], b[0], b[1], t3(tmp, m), t3(tmp2, m))
            T9 = CH + 1
            dve.wait_ge(s_c, 2)
            cb = [Cc[:, i].unsqueeze(2).broadcast_to([P, J, T9, SP]) for i in range(2)]
            pb = [v.unsqueeze(3).broadcast_to([P, J, T9, SP]) for v in (pr, pi)]
            t4 = lambda v, n: v[:, 0:J * n * SP].rearrange("p (j t a) -> p j t a", j=J, t=n)
            cmul(e.Wr, e.nWi, cb[0], cb[1], pb[0], pb[1], t4(tmp, T9), t4(tmp2, T9))
            step(TS(e.nWi, e.nWi, -1.0, None, ALU.mult))
            bb = [e.Bc[:, i].unsqueeze(2).broadcast_to([P, J, CH, SP]) for i in range(2)]
            pb = [v[:, :, CH - 1::-1].unsqueeze(3).broadcast_to([P, J, CH, SP]) for v in (pr, pi)]
            cmul(V[:, 0:J], V[:, J:2 * J], bb[0], bb[1], pb[0], pb[1], t4(tmp, CH), t4(tmp2, CH))
            dve.sem_inc(s_v, 1)
            cmul(c_(P2R), c_(P2I), c_(CS), c_(SN_), c_(CS), c_(SN_), c_(X1), c_(X2))
            cmul(c_(P4R), c_(P4I), c_(P2R), c_(P2I), c_(P2R), c_(P2I), c_(X1), c_(X2))
            cmul(c_(P8R), c_(P8I), c_(P4R), c_(P4I), c_(P4R), c_(P4I), c_(X1), c_(X2))
            step(nc.vector.memset(e.E[:, 0, :, 0:1], 1.0))
            step(nc.vector.memset(e.E[:, 1, :, 0:1], 0.0))
            at = (P8R, P8I)
            m = 1
            while m < NCH:
                b = [c_(v).unsqueeze(2).broadcast_to([P, J, m]) for v in at]
                cmul(e.E[:, 0, :, m:2 * m], e.E[:, 1, :, m:2 * m], e.E[:, 0, :, 0:m], e.E[:, 1, :, 0:m], b[0], b[1], t3(tmp, m), t3(tmp2, m))
                to = (FR, FI) if at != (FR, FI) else (G1, G2)
                cmul(c_(to[0]), c_(to[1]), c_(at[0]), c_(at[1]), c_(at[0]), c_(at[1]), c_(X1), c_(X2))
                at = to
                m *= 2
    A.give("U", "V", "q_small", "Bn", "Cn", "Cc", "powers", "ssm_tmp", "ssm_tmp2")


def stage_ssm(e):
    nc, A, ps = e.nc, e.arena, e.ps
    J = SG // 2
    M = A.take("M", SG, P)
    e.ygT = A.take("ygT", 4, L)
    K = e.ygT.rearrange("p a (g c) -> p (a g) c", c=P)
    Brep = A.take("Brep", 2, 2, CH, SP)
    a8 = A.take("a8", J, P)
    z = A.take("z", 2, J, P)
    Sp = A.take("Sp", 2, J, P + 1)
    t1, t2 = A.take("t1", 512), A.take("t2", 512)
    Y = A.take("Y", CH, 512)
    dd = A.take("d_skip", SG)
    s_in, s_own, s_rep, s_k, s_ke, s_mz, s_sh, s_v, s_vd, s_S, s_y, s_yo, s_tr, s_tro, s_d = (
        e.sem(f"ss_{n}") for n in ("in", "own", "rep", "k", "ke", "mz", "sh", "v", "vd", "S", "y", "yo", "tr", "tro", "d"))
    with nc.Block() as block:
        @block.sync
        def _(sp):
            with nc.allow_non_contiguous_dma("the skip by channel"):
                for t in range(CH):
                    sp.dma_start(dd[SP * t:SP * t + SP, :], e.in_["D_skip_2"][0].rearrange("(g p) -> p g", p=SP)).then_inc(s_in, 16)
            sp.wait_ge(s_ke, SG // 4)
            sp.wait_ge(s_mz, 1)
            for t in range(CH):
                sp.dma_start(M[SP * t:SP * t + SP, :, SP * t:P], K[SP * t:SP * t + SP, :, 0:P - SP * t]).then_inc(s_sh, 16)

        @block.tensor
        def _(pe):
            for g in range(SG):
                j, h = divmod(g, 2)
                b = j // 4
                if h == 0:
                    pe.wait_ge(s_rep, j + 1)
                if g % 8 == 0 and b >= 2:
                    pe.wait_ge(s_ke, 2 * (b - 1))
                o = ps[:, 2 * (b % 2) + h, (j % 4) * P:(j % 4 + 1) * P]
                hh = slice(64 * h, 64 * h + 64)
                nc.tensor.matmul(o, Brep[hh, j % 2, 0].rearrange("p a b -> p (a b)"), e.Wr[hh, j, 0:CH].rearrange("p a b -> p (a b)"), start=True, stop=False)
                ins = nc.tensor.matmul(o, Brep[hh, j % 2, 1].rearrange("p a b -> p (a b)"), e.nWi[hh, j, 0:CH].rearrange("p a b -> p (a b)"), start=False, stop=True)
                ins.then_inc(s_k, 1)
            for b in range(4):
                if b >= 2:
                    pe.wait_ge(s_vd, b - 1)
                for j in range(4 * b, 4 * b + 4):
                    for h in range(2):
                        for c in range(2):
                            ins = nc.tensor.matmul(ps[64 * h:64 * h + 64, 4 + 2 * c + b % 2, (j % 4) * P:(j % 4 + 1) * P],
                                                   e.VT[:, c, j, 64 * h:64 * h + 64], e.uT[:, 2 * j + h], start=True, stop=True)
                ins.then_inc(s_v, 1)
            pe.wait_ge(s_S, 1)
            pe.wait_ge(s_d, 1)
            for g in range(SG):
                j, h = divmod(g, 2)
                b = j // 4
                if g % 8 == 0 and b >= 2:
                    pe.wait_ge(s_yo, 2 * (b - 1))
                o = ps[:, 2 * (b % 2) + h, (j % 4) * P:(j % 4 + 1) * P]
                hh = slice(64 * h, 64 * h + 64)
                nc.tensor.matmul(o, e.uT[:, g], M[:, g], start=True, stop=False)
                nc.tensor.matmul(o, Sp[hh, 0, j, 0:P], e.Wr[hh, j, 1:CH + 1].rearrange("p a b -> p (a b)"), start=False, stop=False)
                ins = nc.tensor.matmul(o, Sp[hh, 1, j, 0:P], e.nWi[hh, j, 1:CH + 1].rearrange("p a b -> p (a b)"), start=False, stop=True)
                ins.then_inc(s_y, 1)
            for s in range(CH):
                pe.wait_ge(s_yo, SG // 4)
                if s >= 2:
                    pe.wait_ge(s_tro, s - 1)
                for k in range(4):
                    ins = nc.tensor.transpose(ps[:, s % 2, k * P:(k + 1) * P], Y[:, s, k * P:(k + 1) * P], e.ident)
                ins.then_inc(s_tr, 1)

        @block.scalar
        def _(act):
            for b in range(4):
                act.wait_ge(s_k, 8 * b + 8)
                for h in range(2):
                    nc.scalar.activation(K.rearrange("p (j h) c -> p h j c", h=2)[:, h, 4 * b:4 * b + 4],
                                         ps[:, 2 * (b % 2) + h, :].rearrange("p (a b) -> p a b", b=P), ACT.Copy).then_inc(s_ke, 1)
            for b in range(4):
                act.wait_ge(s_y, 8 * b + 8)
                for h in range(2):
                    nc.scalar.activation(Y.rearrange("p t (j h c) -> p h j t c", h=2, c=SP)[:, h, 4 * b:4 * b + 4],
                                         ps[:, 2 * (b % 2) + h, :].rearrange("p (g t c) -> p g t c", g=4, t=CH), ACT.Gelu_apprx_tanh).then_inc(s_yo, 1)
            for s in range(CH):
                act.wait_ge(s_tr, s + 1)
                nc.scalar.activation(e.ygT[:, :, s:L:CH], ps[:, s % 2, :].rearrange("p (a b) -> p a b", b=P), ACT.Copy).then_inc(s_tro, 1)

        @block.vector
        def _(dve):
            step = Steps(dve, s_own)
            TT = nc.vector.tensor_tensor
            nc.vector.memset(M, 0.0).then_inc(s_mz, 1)
            for j in range(J):
                if j >= 2:
                    dve.wait_ge(s_k, 2 * (j - 1))
                nc.vector.tensor_copy(Brep[:, j % 2], e.Bc[:, :, j].unsqueeze(2).broadcast_to([P, 2, CH, SP])).then_inc(s_rep, 1)
            step(nc.vector.tensor_copy(a8, e.mag8.unsqueeze(2).broadcast_to([P, J, P])))
            step(nc.vector.memset(a8[:, :, 0:1], 0.0))
            step(nc.vector.memset(Sp[:, :, :, 0:1], 0.0))
            fl = lambda v: v.rearrange("p j c -> p (j c)")
            for b in range(4):
                dve.wait_ge(s_v, b + 1)
                s = slice(4 * b, 4 * b + 4)
                vr, vi = ps[:, 4 + b % 2, :], ps[:, 6 + b % 2, :]
                Er, Ei = fl(e.E[:, 0, s]), fl(e.E[:, 1, s])
                zr, zi = fl(z[:, 0, s]), fl(z[:, 1, s])
                step(TT(t1, vr, Er, ALU.mult))
                step(TT(t2, vi, Ei, ALU.mult))
                step(TT(zr, t1, t2, ALU.add))
                step(TT(t1, vi, Er, ALU.mult))
                step(TT(t2, vr, Ei, ALU.mult))
                TT(zi, t1, t2, ALU.subtract).then_inc(s_vd, 1)
                dve.wait_ge(s_vd, b + 1)
            for c in range(2):
                step(nc.vector.tensor_tensor_scan(fl(z[:, c]), fl(a8), fl(z[:, c]), 0.0, ALU.mult, ALU.add))
            T = a8
            step(TT(T, z[:, 1], e.E[:, 1], ALU.mult))
            step(TT(Sp[:, 0, :, 1:], z[:, 0], e.E[:, 0], ALU.mult))
            step(TT(Sp[:, 0, :, 1:], Sp[:, 0, :, 1:], T, ALU.subtract))
            step(TT(T, z[:, 1], e.E[:, 0], ALU.mult))
            step(TT(Sp[:, 1, :, 1:], z[:, 0], e.E[:, 1], ALU.mult))
            TT(Sp[:, 1, :, 1:], Sp[:, 1, :, 1:], T, ALU.add).then_inc(s_S, 1)
            dve.wait_ge(s_sh, 16 * CH)
            dve.wait_ge(s_in, 16 * CH)
            step(TT(K, e.ident.unsqueeze(1).broadcast_to([P, SG, P]), dd.unsqueeze(2).broadcast_to([P, SG, P]), ALU.mult))
            TT(M, M, K, ALU.add).then_inc(s_d, 1)
    A.give("M", "Brep", "a8", "z", "Sp", "t1", "t2", "Y", "d_skip", "Wr", "nWi", "Bc", "VT", "E", "mag8", "uT")


def stage_glu(e):
    nc, A, ps = e.nc, e.arena, e.ps
    e.yT = A.take("yT", 4, L)
    w = A.take("w_g", 4, 512)
    b = A.take("b_g", 4)
    sg = A.take("sg", 2, 512)
    s_in, s_mm, s_sg, s_y = (e.sem(f"gl_{n}") for n in ("in", "mm", "sg", "y"))
    steps = [(m, n) for m in range(4) for n in range(2)]
    with nc.Block() as block:
        @block.sync
        def _(sp):
            sp.dma_start(w, e.in_["w_glu_2"][0].rearrange("(k p) n -> p k n", p=P)).then_inc(s_in, 16)
            with nc.allow_non_contiguous_dma("a bias by channel"):
                sp.dma_start(b, e.in_["b_glu_2"][0].rearrange("(k p) -> p k", p=P)).then_inc(s_in, 16)

        @block.tensor
        def _(pe):
            pe.wait_ge(s_in, 32)
            for i, (m, n) in enumerate(steps):
                for k in range(4):
                    ins = nc.tensor.matmul(ps[:, i, :], w[:, k, m * P:(m + 1) * P], e.ygT[:, k, n * 512:(n + 1) * 512], start=(k == 0), stop=(k == 3))
                ins.then_inc(s_mm, 1)

        @block.scalar
        def _(act):
            act.wait_ge(s_in, 32)
            for i, (m, n) in enumerate(steps):
                act.wait_ge(s_mm, i + 1)
                if i >= 2:
                    act.wait_ge(s_y, i - 1)
                nc.scalar.activation(sg[:, i % 2], ps[:, i, :], ACT.Sigmoid, bias=b[:, m:m + 1]).then_inc(s_sg, 1)

        @block.vector
        def _(dve):
            for i, (m, n) in enumerate(steps):
                dve.wait_ge(s_sg, i + 1)
                c = slice(n * 512, (n + 1) * 512)
                nc.vector.tensor_tensor(e.yT[:, m, c], e.ygT[:, m, c], sg[:, i % 2], ALU.mult).then_inc(s_y, 1)
    A.give("w_g", "b_g", "sg", "ygT")


def stage_heads(e):
    nc, A, ps = e.nc, e.arena, e.ps
    e.hd = A.take("hd", 8, L)
    G = 15
    gain = A.take("gain", G, HD)
    ss = A.take("ss", TL, G)
    sq = A.take("sq", 2, G * HD)
    dup = A.take("dup", 2, 4, HD)
    s_in, s_sq, s_ss, s_rt, s_own, s_n, s_tr, s_ev = (e.sem(f"hd_{n}") for n in ("in", "sq", "ss", "rt", "own", "n", "tr", "ev"))
    names = [("q_norm_g_2", i) for i in range(8)] + [("k_norm_g_2", 8), ("idx_k_norm_g_2", 14)]
    with nc.Block() as block:
        @block.sync
        def _(sp):
            for name, i in names:
                sp.dma_start(gain[:, i], broadcast_rows(e.in_[name][0])).then_inc(s_in, 16)

        @block.scalar
        def _(act):
            for t in range(TL):
                if t >= 2:
                    act.wait_ge(s_ss, t - 1)
                nc.scalar.activation(sq[:, t % 2], e.r[:, t, 0:G * HD], ACT.Square).then_inc(s_sq, 1)
            act.wait_ge(s_own, 2)
            nc.scalar.activation(ss, ss, ACT.Sqrt).then_inc(s_rt, 1)
            for t in range(TL):
                for j in range(2):
                    act.wait_ge(s_tr, 2 * t + j + 1)
                    nc.scalar.activation(e.hd[:, 4 * j:4 * j + 4, t * P:(t + 1) * P], ps[:, (2 * t + j) % 8, :].rearrange("p (a b) -> p a b", b=P), ACT.Copy).then_inc(s_ev, 1)

        @block.vector
        def _(dve):
            step = Steps(dve, s_own)
            step(nc.vector.memset(gain[:, 9:14], 1.0))
            for t in range(TL):
                dve.wait_ge(s_sq, t + 1)
                nc.vector.tensor_reduce(ss[:, t], sq[:, t % 2].rearrange("p (g c) -> p g c", c=HD), AX, ALU.add).then_inc(s_ss, 1)
            dve.wait_ge(s_ss, TL)
            step(nc.vector.tensor_scalar(ss, ss, 1.0 / HD, EPS, ALU.mult, ALU.add))
            dve.wait_ge(s_rt, 1)
            step(nc.vector.reciprocal(ss, ss))
            step(nc.vector.memset(ss[:, :, 9:14], 1.0))
            dve.wait_ge(s_in, 16 * len(names))
            for t in range(TL):
                v = e.r[:, t, 0:G * HD].rearrange("p (g c) -> p g c", c=HD)
                step(nc.vector.tensor_tensor(v, v, ss[:, t].unsqueeze(2).broadcast_to([P, G, HD]), ALU.mult))
                step(nc.vector.tensor_tensor(v, v, gain, ALU.mult))
                if t >= 2:
                    dve.wait_ge(s_tr, 2 * (t - 1))
                step(nc.vector.tensor_copy(dup[:, t % 2, 0:2], v[:, 8:9].broadcast_to([P, 2, HD])))
                nc.vector.tensor_copy(dup[:, t % 2, 2:4], v[:, 14:15].broadcast_to([P, 2, HD])).then_inc(s_n, 1)

        @block.tensor
        def _(pe):
            for t in range(TL):
                pe.wait_ge(s_n, t + 1)
                if t >= 4:
                    pe.wait_ge(s_ev, 2 * (t - 3))
                blocks = [e.r[:, t, RQ + i * P:RQ + (i + 1) * P] for i in range(4)] + [e.r[:, t, RQI + i * P:RQI + (i + 1) * P] for i in range(2)]
                blocks += [dup[:, t % 2, 2 * i:2 * i + 2].rearrange("p a b -> p (a b)") for i in range(2)]
                for i, b in enumerate(blocks):
                    ins = nc.tensor.transpose(ps[:, (2 * t + i // 4) % 8, (i % 4) * P:(i % 4 + 1) * P], b, e.ident)
                    if i % 4 == 3:
                        ins.then_inc(s_tr, 1)
    A.give("gain", "ss", "sq", "dup")


def stage_sparse(e):
    nc, A, ps = e.nc, e.arena, e.ps
    e.yaT = A.take("yaT", 4, L)
    bias = A.take("bias", sum(range(1, TL + 1)) * P)
    rel = A.take("rel", 2, 512)
    m8 = A.take("m8", 8)
    pr = A.take("pr", 2, L)
    pT = A.take("pT", 2, TL, P)
    sm = A.take("sm", 2, 3, HEADS)
    on = A.take("on", 2, HEADS * HD)
    at = [sum(range(1, i + 1)) * P for i in range(TL)]
    B = lambda i: bias[:, at[i]:at[i] + (i + 1) * P]
    QI, KB, KI = 4, 6, 7
    REPL = -3e38
    rounds = TOPK // 8
    chosen = [i for i in range(TL) if (i + 1) * P > TOPK]
    idx_tasks = [(i, c, h) for i in chosen for c in range(0, (i + 1) * P, 512) for h in range(IH)]
    s_mm, s_rel, s_acc, s_own, s_m8, s_mr, s_bias = (e.sem(f"sp_{n}") for n in ("mm", "rel", "acc", "own", "m8", "mr", "bias"))
    s_lg, s_pm, s_ex, s_tr, s_pT, s_pv, s_on, s_ot, s_o = (e.sem(f"sp_{n}") for n in ("lg", "pm", "ex", "tr", "pT", "pv", "on", "ot", "o"))
    heads = [(i, h) for i in range(TL) for h in range(HEADS)]
    with nc.Block() as block:
        @block.tensor
        def _(pe):
            for n, (i, c, h) in enumerate(idx_tasks):
                w = min(512, (i + 1) * P - c)
                hh = slice(64 * (h % 2), 64 * (h % 2) + 64)
                if n >= 4:
                    pe.wait_ge(s_rel, n - 3)
                nc.tensor.matmul(ps[:, n % 4, 0:w], e.hd[hh, QI + h // 2, i * P:(i + 1) * P], e.hd[hh, KI, c:c + w], start=True, stop=True).then_inc(s_mm, 1)

            def logits(n):
                i, h = heads[n]
                hh = slice(64 * (h % 2), 64 * (h % 2) + 64)
                if n >= 2:
                    pe.wait_ge(s_pm, n - 1)
                for c in range(0, (i + 1) * P, 512):
                    w = min(512, (i + 1) * P - c)
                    ins = nc.tensor.matmul(ps[:, 2 * (n % 2) + c // 512, 0:w], e.hd[hh, h // 2, i * P:(i + 1) * P], e.hd[hh, KB, c:c + w], start=True, stop=True)
                ins.then_inc(s_lg, 1)

            def values(n):
                i, h = heads[n]
                pe.wait_ge(s_ex, n + 1)
                if n >= 1:
                    pe.wait_ge(s_pT, n)
                for b in range(i + 1):
                    ins = nc.tensor.transpose(ps[:, 4 + b // 4, (b % 4) * P:(b % 4 + 1) * P], pr[:, n % 2, b * P:(b + 1) * P], e.ident)
                ins.then_inc(s_tr, 1)
                pe.wait_ge(s_pT, n + 1)
                if h == 0 and i >= 1:
                    pe.wait_ge(s_on, i)
                for b in range(i + 1):
                    ins = nc.tensor.matmul(ps[:, 6, h * HD:(h + 1) * HD], pT[:, n % 2, b], e.r[:, b, RV:RV + HD], start=(b == 0), stop=(b == i))
                ins.then_inc(s_pv, 1)
                if h == HEADS - 1:
                    pe.wait_ge(s_on, i + 1)
                    if i >= 1:
                        pe.wait_ge(s_o, i)
                    for k in range(4):
                        ins = nc.tensor.transpose(ps[:, 7, k * P:(k + 1) * P], on[:, i % 2, k * P:(k + 1) * P], e.ident)
                    ins.then_inc(s_ot, 1)

            pe.wait_ge(s_rel, len(idx_tasks))
            for n in range(len(heads) + 1):
                if n < len(heads):
                    logits(n)
                if n >= 1:
                    values(n - 1)

        @block.scalar
        def _(act):
            for n, (i, c, h) in enumerate(idx_tasks):
                w = min(512, (i + 1) * P - c)
                act.wait_ge(s_mm, n + 1)
                if n >= 2:
                    act.wait_ge(s_acc, n - 1)
                nc.scalar.activation(rel[:, n % 2, 0:w], ps[:, n % 4, 0:w], ACT.Relu, scale=IH ** -0.5 * HD ** -0.5).then_inc(s_rel, 1)

            def softmax(n):
                i, h = heads[n]
                act.wait_ge(s_pm, n + 1)
                nc.scalar.activation(pr[:, n % 2, 0:(i + 1) * P], pr[:, n % 2, 0:(i + 1) * P], ACT.Exp, bias=sm[:, i % 2, 1, h:h + 1],
                                     scale=HD ** -0.5, accum_out=sm[:, i % 2, 2, h:h + 1]).then_inc(s_ex, 1)

            def turned(n):
                i, h = heads[n]
                act.wait_ge(s_tr, n + 1)
                if n >= 2:
                    act.wait_ge(s_pv, n - 1)
                nc.scalar.activation(pT[:, n % 2, 0:i + 1], ps[:, 4:6, :].rearrange("p a (b c) -> p (a b) c", c=P)[:, 0:i + 1], ACT.Copy).then_inc(s_pT, 1)
                if h == HEADS - 1:
                    act.wait_ge(s_ot, i + 1)
                    nc.scalar.activation(e.yaT[:, :, i * P:(i + 1) * P], ps[:, 7, :].rearrange("p (a b) -> p a b", b=P), ACT.Copy).then_inc(s_o, 1)

            for n in range(len(heads) + 1):
                border = n % HEADS == 0
                if n >= 1 and border:
                    turned(n - 1)
                if n < len(heads):
                    softmax(n)
                if n >= 1 and not border:
                    turned(n - 1)

        @block.vector
        def _(dve):
            step = Steps(dve, s_own)
            for i in range(TL):
                if i not in chosen:
                    if i:
                        nc.vector.memset(B(i)[:, 0:i * P], 0.0)
                    nc.vector.tensor_copy(B(i)[:, i * P:], e.const("causal")).then_inc(s_bias, 1)
            for n, (i, c, h) in enumerate(idx_tasks):
                w = min(512, (i + 1) * P - c)
                dst = B(i)[:, c:c + w]
                wi = e.r[:, i, RWI + h:RWI + h + 1]
                dve.wait_ge(s_rel, n + 1)
                if h == 0:
                    nc.vector.tensor_scalar(dst, rel[:, n % 2, 0:w], wi, None, ALU.mult).then_inc(s_acc, 1)
                else:
                    dve.wait_ge(s_acc, n)
                    nc.vector.scalar_tensor_tensor(out=dst, in0=rel[:, n % 2, 0:w], scalar=wi, in1=dst, op0=ALU.mult, op1=ALU.add).then_inc(s_acc, 1)
            dve.wait_ge(s_acc, len(idx_tasks))
            for i in chosen:
                step(nc.vector.tensor_tensor(B(i)[:, i * P:], B(i)[:, i * P:], e.const("causal"), ALU.add))

            def choose(t):
                b = B(chosen[t])
                for r in range(t * rounds, (t + 1) * rounds):
                    nc.vector.max(m8, b).then_inc(s_m8, 1)
                    dve.wait_ge(s_m8, r + 1)
                    nc.vector.match_replace(b, m8, b, REPL).then_inc(s_mr, 1)
                    dve.wait_ge(s_mr, r + 1)
                nc.vector.tensor_scalar(b, b, 0.5 * REPL, -BIG, ALU.is_gt, ALU.mult).then_inc(s_bias, 1)

            def attend(i):
                dve.wait_ge(s_bias, i + 1)
                for h in range(HEADS):
                    n = i * HEADS + h
                    w = (i + 1) * P
                    dve.wait_ge(s_lg, n + 1)
                    if n >= 2:
                        dve.wait_ge(s_tr, n - 1)
                    step(nc.vector.tensor_tensor_reduce(out=pr[:, n % 2, 0:w], in0=ps[:, 2 * (n % 2):2 * (n % 2) + 2, :].rearrange("p a b -> p (a b)")[:, 0:w],
                                                        in1=B(i), scale=1.0, scalar=REPL, op0=ALU.add, op1=ALU.max, accum_out=sm[:, i % 2, 0, h:h + 1]))
                    nc.vector.tensor_scalar(sm[:, i % 2, 1, h:h + 1], sm[:, i % 2, 0, h:h + 1], -HD ** -0.5, None, ALU.mult).then_inc(s_pm, 1)
                dve.wait_ge(s_ex, 8 * i + 8)
                step(nc.vector.reciprocal(sm[:, i % 2, 0], sm[:, i % 2, 2]))
                dve.wait_ge(s_pv, 8 * i + 8)
                nc.vector.tensor_tensor(on[:, i % 2].rearrange("p (h c) -> p h c", h=HEADS), ps[:, 6, :].rearrange("p (h c) -> p h c", h=HEADS),
                                        sm[:, i % 2, 0].unsqueeze(2).broadcast_to([P, HEADS, HD]), ALU.mult).then_inc(s_on, 1)

            for i in range(TL):
                if i < len(chosen):
                    choose(i)
                attend(i)
    A.give("bias", "rel", "m8", "pr", "pT", "sm", "on", "hd", "r")


def stage_merge(e):
    nc, A, ps = e.nc, e.arena, e.ps
    e.merged = A.take("merged", KD, L)
    hT = A.take("hT2", KD, L)
    wp = A.take("w_proj", 2, 4, D)
    wg = A.take("w_gates", 2, 2, KD, 256)
    sg = A.take("sig", 2, 2, 512)
    w_in = e.in_["w_in_2"][0].rearrange("(k p) n -> p k n", p=P)
    at = 512 + RN
    s_h, s_p, s_mm, s_sg, s_m1, s_m2, s_out = (e.sem(f"mg_{n}") for n in ("h", "p", "mm", "sg", "m1", "m2", "out"))
    s_w = [e.sem(f"mg_w{i}") for i in range(2)]
    steps = [(m, n) for m in range(KD) for n in range(2)]
    with nc.Block() as block:
        @block.sync
        def _(sp):
            sp.dma_start(hT.rearrange("p a b -> p (a b)"), e.hT_dram).then_inc(s_h, 16)
            for c in range(4):
                if c >= 2:
                    sp.wait_ge(s_mm, 4 * (c - 1))
                for g in range(2):
                    a = at + g * D + c * 256
                    sp.dma_start(wg[:, c % 2, g], w_in[:, :, a:a + 256]).then_inc(s_w[c % 2], 16)
                if c == 0:
                    for i, name in enumerate(("w_proj_ssm_2", "w_proj_attn_2")):
                        sp.dma_start(wp[:, i], e.in_[name][0].rearrange("(k p) n -> p k n", p=P)).then_inc(s_p, 16)

        @block.tensor
        def _(pe):
            pe.wait_ge(s_h, 16)
            for i, (m, n) in enumerate(steps):
                c = m // 2
                if i % 4 == 0:
                    pe.wait_ge(s_w[c % 2], 32 * (c // 2 + 1))
                if i >= 2:
                    pe.wait_ge(s_out, i - 1)
                B = 4 * (i % 2)
                tok = slice(n * 512, (n + 1) * 512)
                for g in range(2):
                    for k in range(KD):
                        nc.tensor.matmul(ps[:, B + g, :], wg[:, c % 2, g, k, (m % 2) * P:(m % 2 + 1) * P], hT[:, k, tok], start=(k == 0), stop=(k == KD - 1))
                if i == 0:
                    pe.wait_ge(s_p, 32)
                for g, y in enumerate((e.yT, e.yaT)):
                    for k in range(4):
                        ins = nc.tensor.matmul(ps[:, B + 2 + g, :], wp[:, g, k, m * P:(m + 1) * P], y[:, k, tok], start=(k == 0), stop=(k == 3))
                ins.then_inc(s_mm, 1)

        @block.scalar
        def _(act):
            for i in range(len(steps)):
                act.wait_ge(s_mm, i + 1)
                if i >= 2:
                    act.wait_ge(s_out, i - 1)
                nc.scalar.activation(sg[:, i % 2], ps[:, 4 * (i % 2):4 * (i % 2) + 2, :], ACT.Sigmoid).then_inc(s_sg, 1)

        @block.vector
        def _(dve):
            for i, (m, n) in enumerate(steps):
                dve.wait_ge(s_sg, i + 1)
                nc.vector.tensor_tensor(sg[:, i % 2], sg[:, i % 2], ps[:, 4 * (i % 2) + 2:4 * (i % 2) + 4, :], ALU.mult).then_inc(s_m1, 1)
                dve.wait_ge(s_m1, i + 1)
                nc.vector.tensor_tensor(e.merged[:, m, n * 512:(n + 1) * 512], sg[:, i % 2, 0], sg[:, i % 2, 1], ALU.add).then_inc(s_out, 1)
    A.give("hT2", "w_proj", "w_gates", "sig", "yT", "yaT")


def stage_out2(e):
    nc, A, ps = e.nc, e.arena, e.ps
    e.x4 = A.take("x4", TL, D, high=True)
    e.hT3 = A.take("hT3", KD, L, high=True)
    w = A.take("w_o", KD, D)
    xr = A.take("x_ring", 2, D)
    g = A.take("gain", D)
    h = A.take("h", 2, D)
    junk = A.take("junk", D)
    ss = A.take("ss", TL)
    s_x = [e.sem(f"o2_xin{i}") for i in range(2)]
    s_w, s_g, s_mm, s_x4, s_sq, s_var, s_rt, s_own, s_h, s_tr, s_ev = (e.sem(f"o2_{n}") for n in ("w", "g", "mm", "x4", "sq", "var", "rt", "own", "h", "tr", "ev"))
    two = lambda v: v.rearrange("p (a n) -> p a n", a=2)
    with nc.Block() as block:
        @block.sync
        def _(sp):
            sp.dma_start(w, e.in_["w_out_2"][0].rearrange("(k p) n -> p k n", p=P)).then_inc(s_w, 16)
            sp.dma_start(g, broadcast_rows(e.in_["norm2_g_2"][0])).then_inc(s_g, 16)
            for t in range(TL):
                if t >= 2:
                    sp.wait_ge(s_x4, t - 1)
                sp.dma_start(xr[:, t % 2], e.x3_dram[t * P:(t + 1) * P, :]).then_inc(s_x[t % 2], 16)

        @block.tensor
        def _(pe):
            pe.wait_ge(s_w, 16)
            for t in range(TL):
                if t >= 4:
                    pe.wait_ge(s_x4, t - 3)
                for j in range(2):
                    for k in range(KD):
                        ins = nc.tensor.matmul(ps[:, 2 * (t % 4) + j, :], e.merged[:, k, t * P:(t + 1) * P], w[:, k, j * 512:(j + 1) * 512], start=(k == 0), stop=(k == KD - 1))
                ins.then_inc(s_mm, 1)
            pe.wait_ge(s_x4, TL)
            for t in range(TL):
                pe.wait_ge(s_h, t + 1)
                if t >= 4:
                    pe.wait_ge(s_ev, 2 * (t - 3))
                for k in range(KD):
                    ins = nc.tensor.transpose(ps[:, (2 * t + k // 4) % 8, (k % 4) * P:(k % 4 + 1) * P], h[:, t % 2, k * P:(k + 1) * P], e.ident)
                    if k % 4 == 3:
                        ins.then_inc(s_tr, 1)

        @block.scalar
        def _(act):
            for t in range(TL):
                act.wait_ge(s_x4, t + 1)
                if t:
                    act.wait_ge(s_sq, t)
                nc.scalar.activation(junk, e.x4[:, t], ACT.Square, accum_out=ss[:, t:t + 1]).then_inc(s_sq, 1)
            act.wait_ge(s_var, 1)
            nc.scalar.activation(ss, ss, ACT.Sqrt).then_inc(s_rt, 1)
            for t in range(TL):
                for j in range(2):
                    act.wait_ge(s_tr, 2 * t + j + 1)
                    nc.scalar.activation(e.hT3[:, 4 * j:4 * j + 4, t * P:(t + 1) * P], ps[:, (2 * t + j) % 8, :].rearrange("p (a b) -> p a b", b=P), ACT.Copy).then_inc(s_ev, 1)

        @block.vector
        def _(dve):
            step = Steps(dve, s_own)
            for t in range(TL):
                dve.wait_ge(s_mm, t + 1)
                dve.wait_ge(s_x[t % 2], 16 * (t // 2 + 1))
                nc.vector.tensor_tensor(two(e.x4[:, t]), two(xr[:, t % 2]), ps[:, 2 * (t % 4):2 * (t % 4) + 2, :], ALU.add).then_inc(s_x4, 1)
            dve.wait_ge(s_sq, TL)
            step(nc.vector.tensor_scalar(ss, ss, 1.0 / D, EPS, ALU.mult, ALU.add))
            nc.vector.reciprocal(ss, ss).then_inc(s_var, 1)
            dve.wait_ge(s_rt, 1)
            dve.wait_ge(s_g, 16)
            for t in range(TL):
                if t >= 2:
                    dve.wait_ge(s_tr, 2 * (t - 1))
                nc.vector.scalar_tensor_tensor(out=h[:, t % 2], in0=e.x4[:, t], scalar=ss[:, t:t + 1], in1=g, op0=ALU.mult, op1=ALU.mult).then_inc(s_h, 1)
    A.give("merged", "w_o", "x_ring", "gain", "h", "junk", "ss")


def stage_ffn_up(e):
    nc, A, ps = e.nc, e.arena, e.ps
    MB = DFF // P
    e.hid = A.take("hid", MB, L)
    w = A.take("w_ring", 2, 2, KD, 256)
    sg = A.take("sg", 2, 512)
    s_w = [e.sem(f"fu_w{i}") for i in range(2)]
    s_mm, s_sg, s_h = e.sem("fu_mm"), e.sem("fu_sg"), e.sem("fu_h")
    steps = [(m, n) for m in range(MB) for n in range(2)]
    src = [e.in_[n][0].rearrange("(k p) n -> p k n", p=P) for n in ("w_ffn_gate_2", "w_ffn_up_2")]
    with nc.Block() as block:
        @block.sync
        def _(sp):
            for c in range(MB // 2):
                if c >= 2:
                    sp.wait_ge(s_mm, 4 * (c - 1))
                for g in range(2):
                    sp.dma_start(w[:, c % 2, g], src[g][:, :, c * 256:(c + 1) * 256]).then_inc(s_w[c % 2], 16)

        @block.tensor
        def _(pe):
            for i, (m, n) in enumerate(steps):
                c = m // 2
                if i % 4 == 0:
                    pe.wait_ge(s_w[c % 2], 32 * (c // 2 + 1))
                if i >= 4:
                    pe.wait_ge(s_h, i - 3)
                for g in range(2):
                    for k in range(KD):
                        ins = nc.tensor.matmul(ps[:, 2 * (i % 4) + g, :], w[:, c % 2, g, k, (m % 2) * P:(m % 2 + 1) * P], e.hT3[:, k, n * 512:(n + 1) * 512],
                                               start=(k == 0), stop=(k == KD - 1))
                ins.then_inc(s_mm, 1)

        @block.scalar
        def _(act):
            for i in range(len(steps)):
                act.wait_ge(s_mm, i + 1)
                if i >= 2:
                    act.wait_ge(s_h, i - 1)
                nc.scalar.activation(sg[:, i % 2], ps[:, 2 * (i % 4), :], ACT.Silu).then_inc(s_sg, 1)

        @block.vector
        def _(dve):
            for i, (m, n) in enumerate(steps):
                dve.wait_ge(s_sg, i + 1)
                nc.vector.tensor_tensor(e.hid[:, m, n * 512:(n + 1) * 512], sg[:, i % 2], ps[:, 2 * (i % 4) + 1, :], ALU.mult).then_inc(s_h, 1)
    A.give("w_ring", "sg", "hT3")


def stage_ffn_down(e):
    nc, A, ps = e.nc, e.arena, e.ps
    MB = DFF // P
    NW = 3
    w = A.take("w_ring", NW, 2, 512)
    o = A.take("o_ring", 4, 512)
    s_w = [e.sem(f"fd_w{i}") for i in range(NW)]
    s_o = [e.sw_sem(f"fd_o{i}") for i in range(4)]
    s_mm, s_acc, s_out = e.sem("fd_mm"), e.sem("fd_acc"), e.sem("fd_out")
    chunks = [(j, c) for j in range(2) for c in range(MB // 2)]
    src = e.in_["w_ffn_down_2"][0].rearrange("(k p) n -> p k n", p=P)
    with nc.Block() as block:
        @block.sync
        def _(sp):
            for i, (j, c) in enumerate(chunks):
                if i >= NW:
                    sp.wait_ge(s_mm, i - NW + 1)
                sp.dma_start(w[:, i % NW], src[:, 2 * c:2 * c + 2, j * 512:(j + 1) * 512]).then_inc(s_w[i % NW], 16)

        @block.gpsimd
        def _(pool):
            for i in range(2 * TL):
                j, t = divmod(i, TL)
                pool.wait_ge(s_out, i + 1)
                pool.dma_start(e.out[0, t * P:(t + 1) * P, j * 512:(j + 1) * 512], o[:, i % 4]).then_inc(s_o[i % 4], 16)
            for i in range(4):
                pool.wait_ge(s_o[i], 16 * 4)

        @block.tensor
        def _(pe):
            for i, (j, c) in enumerate(chunks):
                pe.wait_ge(s_w[i % NW], 16 * (i // NW + 1))
                for k in range(2):
                    for t in range(TL):
                        if j == 1 and c == 0 and k == 0:
                            pe.wait_ge(s_out, t + 1)
                        ins = nc.tensor.matmul(ps[:, t, :], e.hid[:, 2 * c + k, t * P:(t + 1) * P], w[:, i % NW, k], start=(c == 0 and k == 0), stop=(c == MB // 2 - 1 and k == 1))
                        if c == MB // 2 - 1 and k == 1:
                            ins.then_inc(s_acc, 1)
                        elif k == 1 and t == TL - 1:
                            ins.then_inc(s_mm, 1)
                if c == MB // 2 - 1 and j == 0:
                    pe.wait_ge(s_acc, TL)
                    pe.sem_inc(s_mm, 1)

        @block.vector
        def _(dve):
            for i in range(2 * TL):
                j, t = divmod(i, TL)
                dve.wait_ge(s_acc, i + 1)
                if i >= 4:
                    dve.wait_ge(s_o[i % 4], 16 * (i // 4))
                nc.vector.tensor_tensor(o[:, i % 4], e.x4[:, t, j * 512:(j + 1) * 512], ps[:, t, :], ALU.add).then_inc(s_out, 1)
    A.give("w_ring", "o_ring", "hid", "x4")


STAGES = [stage_modulation, stage_norm1, stage_da_project, stage_da, stage_gdn_project, stage_gdn, stage_gdn_out, stage_rows,
          stage_out_router, stage_choose, stage_experts, stage_between, stage_project2,
          stage_ssm_tables, stage_ssm, stage_glu, stage_heads, stage_sparse,
          stage_merge, stage_out2, stage_ffn_up, stage_ffn_down]


def build(nc, in_, out):
    e = Env()
    e.nc, e.in_, e.out = nc, in_, out
    with ExitStack() as ctx:
        words = 53000
        tensor = ctx.enter_context(nc.sbuf_tensor("arena", [P, words], F32))
        e.ps = ctx.enter_context(nc.psum_tensor("psum", [P, 8, 512], F32))
        e.arena = Arena(tensor, words)
        _, names, _ = constant_tables()
        width = sum(n for _, n in names.values())
        e.consts = e.arena.take("consts", width)
        e.const = lambda name: e.consts[:, names[name][0]:names[name][0] + names[name][1]]
        e.ident = e.const("ident")
        e.shift1 = e.arena.take("shift1", KD, 2)
        e.scale1 = e.arena.take("scale1", KD, 2)
        e.eps = e.const("eps")
        e.catA = e.arena.take("catA", 4, L)
        e.hT = e.arena.take("hT", KD, LA)
        e.sw_sem = nc.alloc_semaphore
        e.sw_sem = nc.alloc_semaphore
        for stage in STAGES:
            own = []
            e.sem = lambda name: own.append(nc.alloc_semaphore(name)) or own[-1]
            stage(e)
            for sem in own:
                nc.gpsimd.sem_clear(sem)
                nc.release_semaphore(sem)


def make_inputs(nc, inputs):
    tables, _, rope = constant_tables()
    arrays, aps = {}, {}
    for name, a in list(inputs.items()) + [("tables", tables), ("rope", rope)]:
        a = np.ascontiguousarray(a)
        arrays[f"in_{name}_dram"] = a
        aps[name] = nc.dram_tensor(f"in_{name}_dram", a.shape, mybir.dt.from_np(a.dtype), kind="ExternalInput").ap()
    return arrays, aps


def kernel(**inputs):
    import concourse.bacc as bacc
    from concourse.bass_utils import run_bass_kernel_spmd

    nc = bacc.Bacc("TRN2", target_bir_lowering=False, num_devices=1)
    arrays, aps = make_inputs(nc, inputs)
    out = nc.dram_tensor("out_0_dram", (1, L, D), F32, kind="ExternalOutput").ap()
    build(nc, aps, out)
    result = run_bass_kernel_spmd(nc, [arrays], core_ids=[0])
    return result.results[0]["out_0_dram"]
```

```python
from contextlib import ExitStack

import numpy as np

import concourse.bass as bass
from concourse import mybir

F32 = mybir.dt.float32
U32 = mybir.dt.uint32
I32 = mybir.dt.int32
ALU = mybir.AluOpType
ACT = mybir.ActivationFunctionType
AX = mybir.AxisListType.X

P = 128
D = 1024
KD = D // P
L = 1024
LC = 256
LA = LC + L
TC, TL, TA = LC // P, L // P, LA // P
EPS = 1e-6
BIG = 1e30
DAH, DAD, DAV = 4, 64, 128
GH, GD = 4, 128
NE, CAP, FF = 16, 128, 1024
SG, SP, SN = 32, 16, 64
CH = 8
NCH = L // CH
HEADS, HD = 8, 64
IH = 4
TOPK = 256
DFF = 2816
TOKEN_RANGES = ((0, 256), (256, 512), (768, 512))


def constant_tables():
    i = np.arange(P)
    col, row = i[None, :], i[:, None]
    parts = {"ident": (row == col).astype(np.float32), "ones": np.ones((P, P), np.float32)}
    parts["cum0"] = (row <= col).astype(np.float32)
    parts["cum1"] = (row >= col).astype(np.float32)
    big = np.float32(-BIG)
    parts["strict0"] = np.where(col < row, 0, big)
    parts["strict1"] = np.where(col > row, 0, big)
    parts["incl0"] = np.where(row <= col, 0, big)
    parts["incl1"] = np.where(row >= col, 0, big)
    for lv in range(7):
        s = 1 << lv
        same = (row // (2 * s)) == (col // (2 * s))
        low = same & ((row // s) % 2 == 1) & ((col // s) % 2 == 0)
        parts[f"level0_{lv}"] = low.astype(np.float32)
        parts[f"level1_{lv}"] = low.T.astype(np.float32)
    d = i % 64
    axis, within = d // 32, d % 32
    inv = 10000.0 ** (-(2.0 * (within % 16)) / 32.0)
    t = np.arange(L)
    pos = np.where(axis[:, None] == 0, t[None, :] // 64, t[None, :] % 64)
    ang = pos.astype(np.float32) * inv.astype(np.float32)[:, None]
    swap = np.zeros((P, P), np.float32)
    for m in range(P):
        first = (m % 32) < 16
        swap[m + 16 if first else m - 16, m] = -1.0 if first else 1.0
    parts["swap"] = swap
    parts["eps"] = np.full((P, 1), EPS, np.float32)
    parts["causal"] = np.where(col <= row, 0, big)
    rope = {"cos": np.cos(ang), "sin": np.sin(ang)}
    names, at, arrays = {}, 0, []
    for name, a in parts.items():
        names[name] = (at, a.shape[1])
        at += a.shape[1]
        arrays.append(a.astype(np.float32))
    return (np.concatenate(arrays, 1), names,
            np.concatenate([rope["cos"], rope["sin"]], 1).astype(np.float32))


class Arena:

    def __init__(self, tensor, words):
        self.tensor, self.words, self.used = tensor, words, {}

    def take(self, name, *shape, high=False):
        n = int(np.prod(shape))
        if high:
            at = self.words - n
            for a, b in sorted(self.used.values(), reverse=True):
                if b <= at:
                    break
                at = min(at, a - n)
        else:
            at = 0
            for a, b in sorted(self.used.values()):
                if at + n <= a:
                    break
                at = max(at, b)
        assert at >= 0 and at + n <= self.words, f"{name}: {at + n} of {self.words} words"
        assert name not in self.used, name
        self.used[name] = (at, at + n)
        v = self.tensor[:, at:at + n]
        if len(shape) > 1:
            axes = [f"a{i}" for i in range(len(shape))]
            v = v.rearrange(f"p ({' '.join(axes)}) -> p {' '.join(axes)}", **dict(zip(axes[:-1], shape)))
        return v

    def give(self, *names):
        for name in names:
            del self.used[name]


class Steps:

    def __init__(self, eng, sem, base=0):
        self.eng, self.sem, self.n = eng, sem, base

    def __call__(self, ins):
        self.n += 1
        ins.then_inc(self.sem, 1)
        self.eng.wait_ge(self.sem, self.n)


class Env:
    pass


def broadcast_rows(ap, n=P):
    return ap.partition_broadcast(n)


def row_of(vec):
    return vec.rearrange("(a n) -> a n", a=1)


def stage_modulation(e):
    nc, A = e.nc, e.arena
    cc = A.take("cc", 2, KD)
    e.silu_c = A.take("silu_c", KD, 2)
    w = A.take("w_ring", 3, KD, 512)
    bm = A.take("b_mod1", 2 * KD)
    g1 = A.take("norm1", KD)
    e.xa, e.s_xa = A.take("xa", TA, D), [e.keep_sem(f"n1_x{i}") for i in range(TA)]
    w_mod = e.in_["w_mod"][0].rearrange("(k p) n -> p k n", p=P)
    s_in, s_w = e.sem("mod_in"), [e.sem(f"mod_w{i}") for i in range(3)]
    s_silu, s_mm, s_own = e.sem("mod_silu"), e.sem("mod_mm"), e.sem("mod_own")
    with nc.Block() as block:
        @block.sync
        def _(sp):
            sp.dma_start(e.consts, e.in_["tables"]).then_inc(s_in, 16)
            with nc.allow_non_contiguous_dma("vectors by channel"):
                sp.dma_start(cc[:, 0, :], e.in_["c"].rearrange("a (k p) -> p (a k)", p=P)).then_inc(s_in, 16)
                sp.dma_start(cc[:, 1, :], e.in_["c_ctx"].rearrange("(k p) -> p k", p=P)).then_inc(s_in, 16)
                sp.dma_start(bm, e.in_["b_mod"][0, 0:2 * D].rearrange("(k p) -> p k", p=P)).then_inc(s_in, 16)
                sp.dma_start(g1, e.in_["norm1_g"][0].rearrange("(k p) -> p k", p=P)).then_inc(s_in, 16)
            for c in range(4):
                if c >= 3:
                    sp.wait_ge(s_mm, c - 2)
                sp.dma_start(w[:, c % 3], w_mod[:, :, c * 512:(c + 1) * 512]).then_inc(s_w[c % 3], 16)
            for t in range(TA):
                src = e.in_["ctx"][0, t * P:(t + 1) * P, :] if t < TC else e.in_["x"][0, (t - TC) * P:(t - TC + 1) * P, :]
                sp.dma_start(e.xa[:, t], src).then_inc(e.s_xa[t], 16)

        @block.scalar
        def _(act):
            act.wait_ge(s_in, 80)
            nc.scalar.activation(e.silu_c.rearrange("p k v -> p v k"), cc, ACT.Silu).then_inc(s_silu, 1)

        @block.tensor
        def _(pe):
            pe.wait_ge(s_silu, 1)
            for c in range(4):
                pe.wait_ge(s_w[c % 3], 16 * (c // 3 + 1))
                for j in range(4):
                    for k in range(KD):
                        last = nc.tensor.matmul(e.ps[:, 0, 2 * (4 * c + j):2 * (4 * c + j) + 2],
                                                w[:, c % 3, k, j * P:(j + 1) * P], e.silu_c[:, k, :],
                                                start=(k == 0), stop=(k == KD - 1))
                last.then_inc(s_mm, 1)

        @block.vector
        def _(dve):
            step = Steps(dve, s_own)
            dve.wait_ge(s_in, 80)
            dve.wait_ge(s_mm, 4)
            out = e.ps[:, 0, 0:4 * KD].rearrange("p (m v) -> p m v", v=2)
            step(nc.vector.tensor_tensor(e.shift1, out[:, 0:KD], bm[:, 0:KD].unsqueeze(2).broadcast_to([P, KD, 2]), ALU.add))
            step(nc.vector.tensor_tensor(e.scale1, out[:, KD:], bm[:, KD:].unsqueeze(2).broadcast_to([P, KD, 2]), ALU.add))
            step(nc.vector.tensor_scalar(e.scale1, e.scale1, 1.0, None, ALU.add))
            step(nc.vector.tensor_tensor(e.scale1, e.scale1, g1.unsqueeze(2).broadcast_to([P, KD, 2]), ALU.mult))
    A.give("cc", "w_ring", "b_mod1", "norm1")


def stage_norm1(e):
    nc, A = e.nc, e.arena
    xa, s_x = e.xa, e.s_xa
    e.w_da, e.s_wda = A.take("w_da", 2, KD, 512, high=True), [e.keep_sem(f"da_w{i}") for i in range(2)]
    junk = A.take("junk", D)
    ss = A.take("ss", TA)
    s_sq, s_rs, s_rt, s_xn, s_tr, s_ev, s_own = (e.sem(f"n1_{n}") for n in ("sq", "rs", "rt", "xn", "tr", "ev", "own"))
    s_ev2 = e.sem("n1_ev2")
    with nc.Block() as block:
        @block.sync
        def _(sp):
            w_in = e.in_["w_in"][0].rearrange("(k p) n -> p k n", p=P)
            for c in range(2):
                sp.dma_start(e.w_da[:, c], w_in[:, :, c * 512:(c + 1) * 512]).then_inc(e.s_wda[c], 16)

        @block.scalar
        def _(act):
            for t in range(TA):
                act.wait_ge(s_x[t], 16)
                if t:
                    act.wait_ge(s_sq, t)
                nc.scalar.activation(junk, xa[:, t], ACT.Square, accum_out=ss[:, t:t + 1]).then_inc(s_sq, 1)
            act.wait_ge(s_rs, 1)
            nc.scalar.activation(ss, ss, ACT.Sqrt).then_inc(s_rt, 1)
            for t in range(TA):
                v = 1 if t < TC else 0
                act.wait_ge(s_tr, 2 * t + 1)
                for k in range(4):
                    ins = nc.scalar.activation(e.hT[:, k, t * P:(t + 1) * P], e.ps[:, (2 * t) % 8, k * P:(k + 1) * P],
                                               ACT.Identity, bias=e.shift1[:, k, v:v + 1], scale=e.scale1[:, k, v:v + 1])
                ins.then_inc(s_ev, 1)

        @block.vector
        def _(dve):
            step = Steps(dve, s_own)
            dve.wait_ge(s_sq, TA)
            step(nc.vector.tensor_scalar(ss, ss, 1.0 / D, EPS, ALU.mult, ALU.add))
            nc.vector.reciprocal(ss, ss).then_inc(s_rs, 1)
            dve.wait_ge(s_rt, 1)
            for t in range(TA):
                nc.vector.tensor_scalar(xa[:, t], xa[:, t], ss[:, t:t + 1], None, ALU.mult).then_inc(s_xn, 1)
            for t in range(TA):
                v = 1 if t < TC else 0
                dve.wait_ge(s_tr, 2 * t + 2)
                for k in range(4, 8):
                    ins = nc.vector.tensor_scalar(e.hT[:, k, t * P:(t + 1) * P], e.ps[:, (2 * t + 1) % 8, (k - 4) * P:(k - 3) * P],
                                                  e.scale1[:, k, v:v + 1], e.shift1[:, k, v:v + 1], ALU.mult, ALU.add)
                ins.then_inc(s_ev2, 1)

        @block.tensor
        def _(pe):
            for t in range(TA):
                pe.wait_ge(s_xn, t + 1)
                for half, s in ((0, s_ev), (1, s_ev2)):
                    if t >= 4:
                        pe.wait_ge(s, t - 3)
                    for k in range(4):
                        last = nc.tensor.transpose(e.ps[:, (2 * t + half) % 8, k * P:(k + 1) * P],
                                                   xa[:, t, (4 * half + k) * P:(4 * half + k + 1) * P], e.ident)
                    last.then_inc(s_tr, 1)
    A.give("xa", "junk", "ss")


def stage_da_project(e):
    nc, A = e.nc, e.arena
    e.qT = A.take("qT", DAH, L)
    e.kT = A.take("kT", DAH, LA)
    e.v = A.take("v", TA, DAH * DAV)
    w, s_w = e.w_da, e.s_wda
    rope = A.take("rope", 2, L)
    raw = A.take("raw", 3, 512)
    tmp = A.take("rope_tmp", 2, 512)
    w_in = e.in_["w_in"][0].rearrange("(k p) n -> p k n", p=P)
    tasks = []
    for m in range(DAH):
        tasks += [("q", 0, m, s, n) for s, n in TOKEN_RANGES[1:]]
    for m in range(DAH):
        tasks += [("k", 1, m, s, n) for s, n in TOKEN_RANGES]
    tasks += [("v", 2, t, t * P, P) for t in range(TA)]
    first = {c: min(i for i, t in enumerate(tasks) if t[1] == c) for c in range(3)}
    last_of = {c: max(i for i, t in enumerate(tasks) if t[1] == c) for c in range(3)}
    roped = [i for i, t in enumerate(tasks) if t[0] in "qk" and t[3] >= LC]
    s_rope, s_mm, s_raw, s_swap, s_done, s_own = (e.sem(f"dap_{n}") for n in ("rope", "mm", "raw", "swap", "done", "own"))
    with nc.Block() as block:
        @block.sync
        def _(sp):
            sp.dma_start(rope, e.in_["rope"].rearrange("p (a n) -> p a n", a=2)).then_inc(s_rope, 16)
            sp.wait_ge(s_mm, last_of[0] + 1)
            sp.dma_start(w[:, 0], w_in[:, :, 1024:1536]).then_inc(s_w[0], 16)

        @block.tensor
        def _(pe):
            def swap(r):
                pe.wait_ge(s_raw, roped[r] + 1)
                if r >= 2:
                    pe.wait_ge(s_done, r - 1)
                nc.tensor.matmul(e.ps[:, 4 + r % 2, :], e.const("swap"), raw[:, r % 3], start=True, stop=True).then_inc(s_swap, 1)

            done = 0
            for i, (kind, c, m, s, n) in enumerate(tasks):
                if i == first[c]:
                    pe.wait_ge(s_w[c % 2], 16 * (c // 2 + 1))
                if i >= 4:
                    pe.wait_ge(s_raw, i - 3)
                for k in range(KD):
                    if kind == "v":
                        ins = nc.tensor.matmul(e.ps[:, i % 4, :], e.hT[:, k, s:s + n], w[:, c % 2, k, :],
                                               start=(k == 0), stop=(k == KD - 1))
                    else:
                        ins = nc.tensor.matmul(e.ps[:, i % 4, 0:n], w[:, c % 2, k, m * P:(m + 1) * P], e.hT[:, k, s:s + n],
                                               start=(k == 0), stop=(k == KD - 1))
                ins.then_inc(s_mm, 1)
                while done < len(roped) and roped[done] < i:
                    swap(done)
                    done += 1
            while done < len(roped):
                swap(done)
                done += 1

        @block.scalar
        def _(act):
            for i, (kind, c, m, s, n) in enumerate(tasks):
                act.wait_ge(s_mm, i + 1)
                if i in roped:
                    r = roped.index(i)
                    if r >= 3:
                        act.wait_ge(s_done, r - 2)
                    dst = raw[:, r % 3]
                elif kind == "k":
                    dst = e.kT[:, m, s:s + n]
                else:
                    dst = e.v[:, m, :]
                nc.scalar.activation(dst, e.ps[:, i % 4, 0:n if kind != "v" else 512], ACT.Copy).then_inc(s_raw, 1)

        @block.vector
        def _(dve):
            step = Steps(dve, s_own)
            dve.wait_ge(s_rope, 16)
            for r, i in enumerate(roped):
                kind, c, m, s, n = tasks[i]
                o = s - LC
                dst = e.qT[:, m, o:o + n] if kind == "q" else e.kT[:, m, s:s + n]
                dve.wait_ge(s_raw, i + 1)
                nc.vector.tensor_tensor(tmp[:, 0], raw[:, r % 3], rope[:, 0, o:o + n], ALU.mult).then_inc(s_own, 1)
                dve.wait_ge(s_swap, r + 1)
                nc.vector.tensor_tensor(tmp[:, 1], e.ps[:, 4 + r % 2, :], rope[:, 1, o:o + n], ALU.mult).then_inc(s_own, 1)
                dve.wait_ge(s_own, 2 * r + 2)
                nc.vector.tensor_tensor(dst, tmp[:, 0], tmp[:, 1], ALU.add).then_inc(s_done, 1)
                dve.wait_ge(s_done, r + 1)
    A.give("w_da", "rope", "raw", "rope_tmp")


def stage_da(e):
    nc, A, ps = e.nc, e.arena, e.ps
    SLOTS = 3
    e.w_gdn, e.s_wgdn = A.take("w_gdn", 2, KD, 256, high=True), [e.keep_sem(f"gp_w{i}") for i in range(2)]
    pr = A.take("probs", SLOTS, 2, LA)
    aT = A.take("aT", 2, TA, P)
    o = A.take("o", TL, DAH * DAV)
    mx = A.take("mx", SLOTS, 2, 2)
    sm = A.take("sm", SLOTS + 1, 4)
    lamv = A.take("lamv", 4, DAD)
    lam = A.take("lam", 8)
    sub = A.take("subln", 1)
    sq = A.take("sq", 2, DAH * DAV)
    ss = A.take("ss", TL, DAH)
    steps = [(t, h) for t in range(TL) for h in range(DAH)]
    N = len(steps)
    COLS = ((0, 512), (512, 512), (1024, 256))
    GROUPS = [range(g, min(g + 4, TA)) for g in range(0, TA, 4)]
    s_in, s_own, s_lam, s_lam2, s_comb, s_tr, s_aT, s_pv, s_o = (
        e.sem(f"da_{n}") for n in ("in", "own", "lam", "lam2", "comb", "tr", "aT", "pv", "o"))
    s_qk, s_mx, s_exp = ([e.sem(f"da_{n}{m}") for m in range(2)] for n in ("qk", "mx", "exp"))
    s_sq, s_ss, s_rt, s_on, s_oT, s_cat = (e.sem(f"da_{n}") for n in ("sq", "ss", "rt", "on", "oT", "cat"))
    SC = DAD ** -0.5
    h4 = lambda v: v.rearrange("p (h n) -> p h n", h=DAH)
    scores = lambda m: ps[:, 3 * m:3 * m + 3, :].rearrange("p a b -> p (a b)")[:, 0:LA]
    with nc.Block() as block:
        @block.sync
        def _(sp):
            for j, name in enumerate(("lam_q1", "lam_k1", "lam_q2", "lam_k2")):
                sp.dma_start(lamv[:, j], broadcast_rows(e.in_[name][0])).then_inc(s_in, 16)
            with nc.allow_non_contiguous_dma("a vector by channel"):
                sp.dma_start(sub, e.in_["da_subln_g"][0].rearrange("(p a) -> p a", a=1)).then_inc(s_in, 16)
            w_in = e.in_["w_in"][0].rearrange("(k p) n -> p k n", p=P)
            for c in range(2):
                at = 3 * DAH * DAV + 256 * c
                sp.dma_start(e.w_gdn[:, c], w_in[:, :, at:at + 256]).then_inc(e.s_wgdn[c], 16)

        @block.tensor
        def _(pe):
            def qk(i, m):
                if i >= N:
                    return
                t, h = steps[i]
                if i:
                    pe.wait_ge(s_exp[m], i)
                for j, (c, n) in enumerate(COLS):
                    ins = nc.tensor.matmul(ps[:, 3 * m + j, 0:n], e.qT[64 * m:64 * m + 64, h, t * P:(t + 1) * P],
                                           e.kT[64 * m:64 * m + 64, h, c:c + n], start=True, stop=True)
                ins.then_inc(s_qk[m], 1)

            def turn(i, g):
                if 3 * i + g:
                    pe.wait_ge(s_aT, 3 * i + g)
                for j in GROUPS[g]:
                    ins = nc.tensor.transpose(ps[:, 6, (j % 4) * P:(j % 4 + 1) * P], pr[:, i % SLOTS, 0, j * P:(j + 1) * P], e.ident)
                ins.then_inc(s_tr, 1)

            def weigh(i, g):
                t, h = steps[i]
                pe.wait_ge(s_aT, 3 * i + g + 1)
                if g == 0 and i:
                    pe.wait_ge(s_o, i)
                for j in GROUPS[g]:
                    ins = nc.tensor.matmul(ps[:, 7, 0:P], aT[:, i % 2, j, :], e.v[:, j, h * P:(h + 1) * P],
                                           start=(j == 0), stop=(j == TA - 1))
                if g == 2:
                    ins.then_inc(s_pv, 1)

            for i in range(2):
                for m in range(2):
                    qk(i, m)
            for i in range(N):
                pe.wait_ge(s_comb, i + 1)
                turn(i, 0)
                qk(i + 2, 0)
                turn(i, 1)
                weigh(i, 0)
                qk(i + 2, 1)
                turn(i, 2)
                weigh(i, 1)
                weigh(i, 2)
            for t in range(TL):
                pe.wait_ge(s_on, t + 1)
                if t >= 4:
                    pe.wait_ge(s_cat, t - 3)
                for h in range(DAH):
                    ins = nc.tensor.transpose(ps[:, t % 4, h * P:(h + 1) * P], o[:, t, h * P:(h + 1) * P], e.ident)
                ins.then_inc(s_oT, 1)

        @block.scalar
        def _(act):
            act.wait_ge(s_lam, 2)
            nc.scalar.activation(lam[:, 2:4], lam[:, 0:2], ACT.Exp).then_inc(s_lam2, 1)

            def exp(i, m):
                if i >= N:
                    return
                act.wait_ge(s_mx[m], i + 1)
                if i >= SLOTS and m == 0:
                    act.wait_ge(s_tr, 3 * (i - SLOTS) + 3)
                nc.scalar.activation(pr[:, i % SLOTS, m], scores(m), ACT.Exp, bias=mx[:, i % SLOTS, m, 1:2], scale=SC,
                                     accum_out=sm[:, i % (SLOTS + 1), m:m + 1]).then_inc(s_exp[m], 1)

            def copy(i, g):
                act.wait_ge(s_tr, 3 * i + g + 1)
                if g == 0 and i >= 2:
                    act.wait_ge(s_pv, i - 1)
                n = len(GROUPS[g])
                nc.scalar.activation(aT[:, i % 2, 4 * g:4 * g + n, :], ps[:, 6, 0:n * P].rearrange("p (a b) -> p a b", b=P), ACT.Copy).then_inc(s_aT, 1)

            exp(0, 0)
            exp(0, 1)
            exp(1, 0)
            for i in range(N):
                copy(i, 0)
                exp(i + 1, 1)
                copy(i, 1)
                exp(i + 2, 0)
                copy(i, 2)
            for t in range(TL):
                act.wait_ge(s_o, DAH * (t + 1))
                if t >= 2:
                    act.wait_ge(s_ss, t - 1)
                nc.scalar.activation(sq[:, t % 2], o[:, t], ACT.Square).then_inc(s_sq, 1)
            act.wait_ge(s_ss, TL + 1)
            nc.scalar.activation(ss, ss, ACT.Sqrt).then_inc(s_rt, 1)

        @block.vector
        def _(dve):
            step = Steps(dve, s_own)
            dve.wait_ge(s_in, 80)
            for j in range(2):
                step(nc.vector.tensor_tensor(lamv[:, 2 * j], lamv[:, 2 * j], lamv[:, 2 * j + 1], ALU.mult))
                nc.vector.tensor_reduce(lam[:, j:j + 1], lamv[:, 2 * j], AX, ALU.add).then_inc(s_lam, 1)
            dve.wait_ge(s_lam2, 1)
            step(nc.vector.tensor_tensor(lam[:, 4:5], lam[:, 3:4], lam[:, 2:3], ALU.subtract))
            step(nc.vector.tensor_scalar(lam[:, 4:5], lam[:, 4:5], -0.2, None, ALU.add))
            step(nc.vector.tensor_scalar(sub, sub, 0.8, None, ALU.mult))

            def maximum(i, m):
                if i >= N:
                    return
                v = mx[:, i % SLOTS, m]
                dve.wait_ge(s_qk[m], i + 1)
                step(nc.vector.tensor_reduce(v[:, 0:1], scores(m), AX, ALU.max))
                nc.vector.tensor_scalar(v[:, 1:2], v[:, 0:1], -SC, None, ALU.mult).then_inc(s_mx[m], 1)

            def combine(i):
                if i >= N:
                    return
                v = sm[:, i % (SLOTS + 1)]
                dve.wait_ge(s_exp[0], i + 1)
                dve.wait_ge(s_exp[1], i + 1)
                step(nc.vector.reciprocal(v[:, 2:4], v[:, 0:2]))
                step(nc.vector.tensor_scalar(v[:, 3:4], v[:, 3:4], lam[:, 4:5], v[:, 0:1], ALU.mult, ALU.mult))
                nc.vector.scalar_tensor_tensor(out=pr[:, i % SLOTS, 0], in0=pr[:, i % SLOTS, 1], scalar=v[:, 3:4],
                                               in1=pr[:, i % SLOTS, 0], op0=ALU.mult, op1=ALU.add).then_inc(s_comb, 1)

            def output(i):
                t, h = steps[i]
                dve.wait_ge(s_pv, i + 1)
                nc.vector.tensor_scalar(o[:, t, h * P:(h + 1) * P], ps[:, 7, 0:P], sm[:, i % (SLOTS + 1), 2:3], None, ALU.mult).then_inc(s_o, 1)

            for i in range(2):
                for m in range(2):
                    maximum(i, m)
                    if i == 0 and m == 1:
                        combine(0)
            for i in range(N):
                if i:
                    output(i - 1)
                combine(i + 1)
                maximum(i + 2, 0)
                maximum(i + 2, 1)
            output(N - 1)
            for t in range(TL):
                dve.wait_ge(s_sq, t + 1)
                nc.vector.tensor_reduce(ss[:, t], h4(sq[:, t % 2]), AX, ALU.add).then_inc(s_ss, 1)
            dve.wait_ge(s_ss, TL)
            step(nc.vector.tensor_scalar(ss, ss, 1.0 / DAV, EPS, ALU.mult, ALU.add))
            nc.vector.reciprocal(ss, ss).then_inc(s_ss, 1)
            dve.wait_ge(s_rt, 1)
            for t in range(TL):
                nc.vector.tensor_tensor(h4(o[:, t]), h4(o[:, t]), ss[:, t].unsqueeze(2).broadcast_to([P, DAH, DAV]), ALU.mult).then_inc(s_on, 1)
            for t in range(TL):
                dve.wait_ge(s_oT, t + 1)
                nc.vector.tensor_scalar(e.catA[:, :, t * P:(t + 1) * P], h4(ps[:, t % 4, :]), sub[:, 0:1], None, ALU.mult).then_inc(s_cat, 1)
    A.give("probs", "aT", "o", "mx", "sm", "lamv", "lam", "subln", "sq", "ss", "qT", "kT", "v")


def stage_gdn_project(e):
    nc, A = e.nc, e.arena
    NB = 3 * GH
    e.gqT = A.take("gqT", GH, LA)
    e.gkT = A.take("gkT", GH, LA)
    e.gvt = A.take("gvt", TA, GH * GD)
    e.gkt = A.take("gkt", TA, GH * GD)
    e.g = A.take("g", TA, 8)
    e.beta = A.take("beta", TA, 8)
    e.gate_dram = nc.dram_tensor("gate_scratch", (L, GH * GD), F32).ap()
    vT = A.take("vT", 2, LA)
    w, s_w = e.w_gdn, e.s_wgdn
    xc = A.take("conv_in", 2, LA + 4)
    cw = A.take("conv_w", 3, NB)
    rw = A.take("ab_rows", 2, 8)
    abt = A.take("ab", TA, 16)
    gs = A.take("gate_out", 2, 256)
    sq = A.take("sq", 2, 512)
    NI = 4
    inv = A.take("inv", NI, 512)
    w_in = e.in_["w_in"][0].rearrange("(k p) n -> p k n", p=P)
    V = lambda b, sh: (xc[:, b, sh:sh + LC], xc[:, b, LC + 2 + sh:LC + 2 + sh + L])
    names = ("in", "taps", "mm", "raw", "conv", "silu", "own", "sq", "ss", "ln", "inv", "nrm", "tr", "tok",
             "ab", "gate", "store", "actown", "pad")
    s_in, s_taps, s_mm, s_raw, s_conv, s_silu, s_own, s_sq, s_ss, s_ln, s_inv, s_nrm, s_tr, s_tok, s_ab, s_gate, s_store, s_ao, s_pad = (
        e.sem(f"gp_{n}") for n in names)
    s_st = [e.keep_sem(f"gp_st{i}") for i in range(2)]
    chunks = [(1536 + 256 * c, 256) for c in range(8)] + [(3584, 16)]
    ranges = TOKEN_RANGES
    qkv = [(m, r) for m in range(NB) for r in range(3)]
    NQ = len(qkv)
    gate = [(c, t) for c in range(2) for t in range(TL)]
    NG = len(gate)
    norms = [(m, r) for m in range(2 * GH) for r in range(3)]
    dst_of = lambda m: (e.gqT, e.gkT)[m // GH][:, m % GH] if m < 2 * GH else vT[:, m % 2]
    with nc.Block() as block:
        @block.sync
        def _(sp):
            def small():
                with nc.allow_non_contiguous_dma("vectors by channel"):
                    for i in range(3):
                        sp.dma_start(cw[:, i], e.in_["conv_w"][0, i].rearrange("(m p) -> p m", p=P)).then_inc(s_in, 16)
                sp.dma_start(rw[:, 0], broadcast_rows(e.in_["a_log"][0].rearrange("a b -> (a b)"))).then_inc(s_in, 16)
                sp.dma_start(rw[:, 1], broadcast_rows(e.in_["dt_bias"][0].rearrange("a b -> (a b)"))).then_inc(s_in, 16)

            for c, (at, n) in enumerate(chunks):
                if c >= 2:
                    d = c - 2
                    sp.wait_ge(s_mm, 6 * (d + 1) if d < 6 else NQ + TL * (d - 5))
                if c == 0:
                    small()
                if c >= 2:
                    sp.dma_start(w[:, c % 2, :, 0:n], w_in[:, :, at:at + n]).then_inc(s_w[c % 2], 16)

        @block.gpsimd
        def _(pool):
            for i, (c, t) in enumerate(gate):
                pool.wait_ge(s_raw, NQ + i + 1)
                pool.dma_start(e.gate_dram[t * P:(t + 1) * P, c * 256:(c + 1) * 256], gs[:, i % 2, 0:256]).then_inc(s_st[i % 2], 16)
            for i in range(2):
                pool.wait_ge(s_st[i], 16 * NG // 2)

        @block.tensor
        def _(pe):
            def loaded(c):
                pe.wait_ge(s_w[c % 2], 16 * (c // 2 + 1))

            def v_tokens(m):
                pe.wait_ge(s_silu, m + 1)
                h = m - 2 * GH
                for g in range(3):
                    u = 3 * h + g
                    if u >= 2:
                        pe.wait_ge(s_tok, u - 1)
                    for j in range(4 * g, min(4 * g + 4, TA)):
                        ins = nc.tensor.transpose(e.ps[:, 4 + u % 2, (j % 4) * P:(j % 4 + 1) * P], vT[:, m % 2, j * P:(j + 1) * P], e.ident)
                    ins.then_inc(s_tr, 1)

            def squares_sum(i):
                s, n = ranges[norms[i][1]]
                pe.wait_ge(s_sq, i + 1)
                if i >= 2:
                    pe.wait_ge(s_ln, i - 1)
                nc.tensor.matmul(e.ps[:, 6 + i % 2, 0:n], e.const("ones"), sq[:, i % 2, 0:n], start=True, stop=True).then_inc(s_ss, 1)

            for i, (m, r) in enumerate(qkv):
                if m % 2 == 0 and r == 0:
                    loaded(m // 2)
                if i >= 4:
                    pe.wait_ge(s_raw, i - 3)
                s, n = ranges[r]
                for k in range(KD):
                    ins = nc.tensor.matmul(e.ps[:, i % 4, 0:n], w[:, (m // 2) % 2, k, (m % 2) * P:(m % 2 + 1) * P],
                                           e.hT[:, k, s:s + n], start=(k == 0), stop=(k == KD - 1))
                ins.then_inc(s_mm, 1)
                if 0 <= i - 10 < len(norms):
                    squares_sum(i - 10)
                if r == 0 and m - 2 >= 2 * GH:
                    v_tokens(m - 2)
            for i, (c, t) in enumerate(gate):
                if t == 0:
                    loaded(6 + c)
                n = NQ + i
                pe.wait_ge(s_raw, n - 3)
                for k in range(KD):
                    ins = nc.tensor.matmul(e.ps[:, n % 4, 0:256], e.hT[:, k, LC + t * P:LC + (t + 1) * P], w[:, (6 + c) % 2, k, :],
                                           start=(k == 0), stop=(k == KD - 1))
                ins.then_inc(s_mm, 1)
                if i in (0, 2):
                    v_tokens(NB - 2 + i // 2)
            loaded(8)
            pe.wait_ge(s_ln, len(norms))
            for t in range(TA):
                for k in range(KD):
                    ins = nc.tensor.matmul(e.ps[:, 6, 16 * t:16 * t + 16], e.hT[:, k, t * P:(t + 1) * P], w[:, 0, k, 0:16],
                                           start=(k == 0), stop=(k == KD - 1))
            ins.then_inc(s_ab, 1)
            for t in range(TA):
                pe.wait_ge(s_nrm, len(norms))
                if t >= 2:
                    pe.wait_ge(s_tok, 3 * GH + t - 1)
                else:
                    pe.wait_ge(s_tok, 3 * GH)
                for h in range(GH):
                    ins = nc.tensor.transpose(e.ps[:, 4 + t % 2, h * P:(h + 1) * P], e.gkT[:, h, t * P:(t + 1) * P], e.ident)
                ins.then_inc(s_tr, 1)

        @block.scalar
        def _(act):
            def silu(m):
                act.wait_ge(s_conv, m + 1)
                if m >= 2 * GH + 2:
                    act.wait_ge(s_tr, 3 * (m - 2 * GH - 1))
                d = dst_of(m)
                nc.scalar.activation(d, d, ACT.Silu).then_inc(s_silu, 1)

            def square(i):
                m, r = norms[i]
                s, n = ranges[r]
                act.wait_ge(s_silu, m + 1)
                if i >= 2:
                    act.wait_ge(s_ss, i - 1)
                nc.scalar.activation(sq[:, i % 2, 0:n], dst_of(m)[:, s:s + n], ACT.Square).then_inc(s_sq, 1)

            def root(i):
                n = ranges[norms[i][1]][1]
                act.wait_ge(s_ss, i + 1)
                if i >= NI:
                    act.wait_ge(s_nrm, i - NI + 1)
                nc.scalar.activation(inv[:, i % NI, 0:n], e.ps[:, 6 + i % 2, 0:n], ACT.Sqrt, bias=e.eps[:, 0:1]).then_inc(s_ln, 1)

            act.wait_ge(s_pad, 1)
            for i, (m, r) in enumerate(qkv):
                s, n = ranges[r]
                act.wait_ge(s_mm, i + 1)
                if m >= 2 and r == 0:
                    act.wait_ge(s_conv, m - 1)
                at = 1 + s if r == 0 else 3 + s
                nc.scalar.activation(xc[:, m % 2, at:at + n], e.ps[:, i % 4, 0:n], ACT.Copy).then_inc(s_raw, 1)
                if 0 <= i - 9 < len(norms):
                    square(i - 9)
                if 0 <= i - 11 < len(norms):
                    root(i - 11)
                if r == 2 and m >= 1:
                    silu(m - 1)
            silu(NB - 1)
            for i, (c, t) in enumerate(gate):
                act.wait_ge(s_mm, NQ + i + 1)
                if i >= 2:
                    act.wait_ge(s_st[i % 2], 16 * (i // 2))
                nc.scalar.activation(gs[:, i % 2, 0:256], e.ps[:, (NQ + i) % 4, 0:256], ACT.Silu).then_inc(s_raw, 1)
            act.wait_ge(s_own, len(norms) + 1)
            nc.scalar.activation(e.beta, abt[:, :, 8:16], ACT.Sigmoid).then_inc(s_ao, 1)
            nc.scalar.activation(rw[:, 0], rw[:, 0], ACT.Exp).then_inc(s_ao, 1)
            act.wait_ge(s_own, len(norms) + 4)
            nc.scalar.activation(abt[:, :, 8:16], abt[:, :, 8:16], ACT.Exp).then_inc(s_ao, 1)
            act.wait_ge(s_ao, 3)
            nc.scalar.activation(abt[:, :, 8:16], abt[:, :, 8:16], ACT.Ln, bias=e.const("ones")[:, 0:1]).then_inc(s_ao, 1)

        @block.vector
        def _(dve):
            step = Steps(dve, s_own)
            nc.vector.memset(xc, 0.0).then_inc(s_pad, 1)
            dve.wait_ge(s_in, 80)

            def v_out(m):
                h = m - 2 * GH
                for g in range(3):
                    n = min(4, TA - 4 * g)
                    dve.wait_ge(s_tr, 3 * h + g + 1)
                    nc.vector.tensor_copy(e.gvt[:, 4 * g:4 * g + n, h * GD:(h + 1) * GD],
                                          e.ps[:, 4 + (3 * h + g) % 2, 0:n * P].rearrange("p (a b) -> p a b", b=P)).then_inc(s_tok, 1)

            def normalise(i):
                m, r = norms[i]
                s, n = ranges[r]
                dve.wait_ge(s_ln, i + 1)
                v = inv[:, i % NI, 0:n]
                step(nc.vector.reciprocal(v, v))
                d = dst_of(m)[:, s:s + n]
                nc.vector.scalar_tensor_tensor(out=d, in0=d, scalar=GD ** -0.5 if m < GH else 1.0, in1=v,
                                               op0=ALU.mult, op1=ALU.mult).then_inc(s_nrm, 1)

            for m in range(NB):
                if m - 2 >= 2 * GH:
                    v_out(m - 2)
                dve.wait_ge(s_raw, 3 * m + 3)
                d = dst_of(m)
                if m >= 2 * GH + 2:
                    dve.wait_ge(s_tr, 3 * (m - 2 * GH - 1))
                D2 = (d[:, 0:LC], d[:, LC:LA])
                for a in range(2):
                    nc.vector.tensor_scalar(D2[a], V(m % 2, 0)[a], cw[:, 0, m:m + 1], None, ALU.mult).then_inc(s_taps, 1)
                dve.wait_ge(s_taps, 2 * (2 * m + 1))
                for a in range(2):
                    nc.vector.scalar_tensor_tensor(out=D2[a], in0=V(m % 2, 1)[a], scalar=cw[:, 1, m:m + 1], in1=D2[a],
                                                   op0=ALU.mult, op1=ALU.add).then_inc(s_taps, 1)
                dve.wait_ge(s_taps, 2 * (2 * m + 2))
                for a in range(2):
                    ins = nc.vector.scalar_tensor_tensor(out=D2[a], in0=V(m % 2, 2)[a], scalar=cw[:, 2, m:m + 1], in1=D2[a],
                                                         op0=ALU.mult, op1=ALU.add)
                ins.then_inc(s_conv, 1)
                if m >= 4:
                    for i in range(3 * (m - 4), 3 * (m - 3)):
                        normalise(i)
            v_out(NB - 2)
            v_out(NB - 1)
            dve.wait_ge(s_ab, 1)
            step(nc.vector.tensor_copy(abt, e.ps[:, 6, 0:16 * TA].rearrange("p (t c) -> p t c", c=16)))
            z = abt[:, :, 0:8]
            dve.wait_ge(s_ao, 2)
            step(nc.vector.tensor_tensor(z, z, rw[:, 1].unsqueeze(1).broadcast_to([P, TA, 8]), ALU.add))
            step(nc.vector.tensor_scalar(abt[:, :, 8:16], z, -1.0, None, ALU.mult))
            step(nc.vector.tensor_tensor(abt[:, :, 8:16], abt[:, :, 8:16], z, ALU.min))
            dve.wait_ge(s_ao, 4)
            step(nc.vector.tensor_scalar(z, z, 0.0, None, ALU.max))
            step(nc.vector.tensor_tensor(z, z, abt[:, :, 8:16], ALU.add))
            step(nc.vector.tensor_scalar(rw[:, 0], rw[:, 0], -1.0, None, ALU.mult))
            step(nc.vector.tensor_tensor(e.g, z, rw[:, 0].unsqueeze(1).broadcast_to([P, TA, 8]), ALU.mult))
            for t in range(TA):
                dve.wait_ge(s_tr, 3 * GH + t + 1)
                nc.vector.tensor_copy(e.gkt[:, t], e.ps[:, 4 + t % 2, :]).then_inc(s_tok, 1)
    A.give("vT", "w_gdn", "conv_in", "conv_w", "ab_rows", "ab", "gate_out", "sq", "inv", "hT")


def stage_gdn(e):
    nc, A, ps = e.nc, e.arena, e.ps
    H4 = GH * P
    e.og = A.take("og", TL, H4)
    F = {n: A.take("f_" + n, 2, H4) for n in ("D", "Dt", "eG", "N", "X", "Y", "T1", "C", "aqk", "kb", "vb", "kd", "qd", "wT", "u")}
    S = A.take("state", 2, H4)
    small = A.take("g_small", 2, 7, GH)
    b4 = lambda m: m.unsqueeze(1).broadcast_to([P, GH, P])
    h4 = lambda v: v.rearrange("p (h n) -> p h n", h=GH)
    col = lambda v: v.unsqueeze(2).broadcast_to([P, GH, P])
    hs = [slice(h * P, (h + 1) * P) for h in range(GH)]
    chunk = [[s for s in range(TA)], [TC - 1 - s if s < TC else TA - 1 - (s - TC) for s in range(TA)]]
    both = lambda name: [e.sem(f"gd_{name}{d}") for d in range(2)]
    LV = 6
    cum_mm, kk_mm, kq_mm, c0t_mm, t1_mm, y_mm, x_mm, w_mm, u_mm, o_mm, ku_mm = (
        both(n) for n in ("cum", "kk", "kq", "c0t", "t1m", "ym", "xm", "wm", "um", "om", "kum"))
    d_exp, dt_exp, sm_exp, eg_exp, t1_in, w_in_, u_in = (both(n) for n in ("dexp", "dtexp", "smexp", "egexp", "t1", "w", "u"))
    sm_in, d_arg, dt_arg, c_in, xy_in, prods, state, o_read, own = (
        both(n) for n in ("sm", "darg", "dtarg", "c", "xy", "prod", "state", "oread", "own"))
    with nc.Block() as block:
        @block.tensor
        def _(pe):
            for s in range(TA):
                lat = s >= TC
                for d in range(2):
                    c, B, g0 = chunk[d][s], 4 * d, 4 * d
                    tok = slice(c * P, (c + 1) * P)
                    cum = e.const(f"cum{d}")
                    pe.wait_ge(state[d], s + 1)
                    if s > TC:
                        pe.wait_ge(o_read[d], s - TC)
                    for h in range(GH):
                        nc.tensor.matmul(ps[:, B, hs[h]], e.g[:, c, g0 + h:g0 + h + 1].broadcast_to([P, P]), cum, start=True, stop=True)
                    nc.tensor.matmul(ps[:, B + 1, 0:GH], cum, e.g[:, c, g0:g0 + 4], start=True, stop=True)
                    nc.tensor.matmul(ps[:, B + 1, GH:2 * GH], e.const("ones"), e.g[:, c, g0:g0 + 4], start=True, stop=True).then_inc(cum_mm[d], 1)
                    for h in range(GH):
                        ins = nc.tensor.matmul(ps[:, B + 2, hs[h]], e.gkT[:, h, tok], e.gkT[:, h, tok], start=True, stop=True)
                    ins.then_inc(kk_mm[d], 1)
                    if lat:
                        for h in range(GH):
                            ins = nc.tensor.matmul(ps[:, B + 3, hs[h]], e.gkT[:, h, tok], e.gqT[:, h, tok], start=True, stop=True)
                        ins.then_inc(kq_mm[d], 1)
                for d in range(2):
                    B, C = 4 * d, F["C"][:, d]
                    pe.wait_ge(c_in[d], 7 * s + 1)
                    for h in range(GH):
                        ins = nc.tensor.matmul(ps[:, B + 1, hs[h]], C[:, hs[h]], e.ident, start=True, stop=True)
                    ins.then_inc(c0t_mm[d], 1)
                for lv in range(1, LV + 1):
                    for d in range(2):
                        B, C, Y = 4 * d, F["C"][:, d], F["Y"][:, d]
                        pe.wait_ge(c_in[d], 7 * s + lv + 1)
                        pe.wait_ge(xy_in[d], 7 * s + lv)
                        if lv == 1:
                            pe.wait_ge(eg_exp[d], s + 1)
                        for h in range(GH):
                            ins = nc.tensor.matmul(ps[:, B, hs[h]], C[:, hs[h]], Y[:, hs[h]], start=True, stop=True)
                        ins.then_inc(t1_mm[d], 1)
                    for d in range(2):
                        B, X, T1 = 4 * d, F["X"][:, d], F["T1"][:, d]
                        pe.wait_ge(t1_in[d], LV * s + lv)
                        for h in range(GH):
                            ins = nc.tensor.matmul(ps[:, B + 1, hs[h]], X[:, hs[h]], T1[:, hs[h]], start=True, stop=True)
                        ins.then_inc(y_mm[d], 1)
                        if lv < LV:
                            for h in range(GH):
                                ins = nc.tensor.matmul(ps[:, B + 2, hs[h]], T1[:, hs[h]], X[:, hs[h]], start=True, stop=True)
                            ins.then_inc(x_mm[d], 1)
                for d in range(2):
                    B, Y = 4 * d, F["Y"][:, d]
                    pe.wait_ge(prods[d], s + 1)
                    pe.wait_ge(xy_in[d], 7 * s + 7)
                    for h in range(GH):
                        ins = nc.tensor.matmul(ps[:, B + 2, hs[h]], F["kb"][:, d, hs[h]], Y[:, hs[h]], start=True, stop=True)
                    ins.then_inc(w_mm[d], 1)
                for d in range(2):
                    B, Y = 4 * d, F["Y"][:, d]
                    pe.wait_ge(w_in_[d], s + 1)
                    for h in range(GH):
                        nc.tensor.matmul(ps[:, B, hs[h]], Y[:, hs[h]], F["vb"][:, d, hs[h]], start=True, stop=False)
                        ins = nc.tensor.matmul(ps[:, B, hs[h]], F["wT"][:, d, hs[h]], S[:, d, hs[h]], start=False, stop=True)
                    ins.then_inc(u_mm[d], 1)
                for d in range(2):
                    B = 4 * d
                    pe.wait_ge(u_in[d], s + 1)
                    if lat:
                        for h in range(GH):
                            nc.tensor.matmul(ps[:, B + 3, hs[h]], F["qd"][:, d, hs[h]], S[:, d, hs[h]], start=True, stop=False)
                            ins = nc.tensor.matmul(ps[:, B + 3, hs[h]], F["aqk"][:, d, hs[h]], F["u"][:, d, hs[h]], start=False, stop=True)
                        ins.then_inc(o_mm[d], 1)
                    for h in range(GH):
                        ins = nc.tensor.matmul(ps[:, B + 1, hs[h]], F["kd"][:, d, hs[h]], F["u"][:, d, hs[h]], start=True, stop=True)
                    ins.then_inc(ku_mm[d], 1)

        @block.scalar
        def _(act):
            for s in range(TA):
                lat = s >= TC
                for d in range(2):
                    B = 4 * d
                    act.wait_ge(sm_in[d], s + 1)
                    nc.scalar.activation(small[:, d, 3:6], small[:, d, 0:3], ACT.Exp).then_inc(sm_exp[d], 1)
                    act.wait_ge(d_arg[d], s + 1)
                    nc.scalar.activation(F["D"][:, d], F["D"][:, d], ACT.Exp).then_inc(d_exp[d], 1)
                    act.wait_ge(dt_arg[d], s + 1)
                    if lat:
                        nc.scalar.activation(F["Dt"][:, d], F["Dt"][:, d], ACT.Exp).then_inc(dt_exp[d], 1)
                    nc.scalar.activation(F["eG"][:, d], ps[:, B, :], ACT.Exp).then_inc(eg_exp[d], 1)
                for lv in range(1, LV + 1):
                    for d in range(2):
                        act.wait_ge(t1_mm[d], LV * s + lv)
                        nc.scalar.activation(F["T1"][:, d], ps[:, 4 * d, :], ACT.Copy).then_inc(t1_in[d], 1)
                for d in range(2):
                    act.wait_ge(w_mm[d], s + 1)
                    nc.scalar.activation(F["wT"][:, d], ps[:, 4 * d + 2, :], ACT.Copy, scale=-1.0).then_inc(w_in_[d], 1)
                for d in range(2):
                    act.wait_ge(u_mm[d], s + 1)
                    nc.scalar.activation(F["u"][:, d], ps[:, 4 * d, :], ACT.Copy).then_inc(u_in[d], 1)

        @block.vector
        def _(dve):
            seen = [False] * TL
            step = [Steps(dve, own[d]) for d in range(2)]
            for d in range(2):
                nc.vector.memset(S[:, d], 0.0).then_inc(state[d], 1)
            TT = nc.vector.tensor_tensor
            for s in range(TA):
                lat = s >= TC
                for d in range(2):
                    B, sm, st = 4 * d, small[:, d], step[d]
                    D, Dt = F["D"][:, d], F["Dt"][:, d]
                    dve.wait_ge(cum_mm[d], s + 1)
                    st(nc.vector.tensor_copy(sm[:, 0:3:2], ps[:, B + 1, 0:2 * GH].rearrange("p (a h) -> p a h", a=2)))
                    TT(sm[:, 1], sm[:, 2], sm[:, 0], ALU.subtract).then_inc(sm_in[d], 1)
                    st(TT(h4(D), b4(e.const(f"strict{d}")), col(sm[:, 0]), ALU.add))
                    TT(D, D, ps[:, B, :], ALU.subtract).then_inc(d_arg[d], 1)
                    if lat:
                        st(TT(h4(Dt), b4(e.const(f"incl{d}")), col(sm[:, 0]), ALU.subtract))
                        TT(Dt, Dt, ps[:, B, :], ALU.add).then_inc(dt_arg[d], 1)
                    else:
                        dve.wait_ge(d_arg[d], s + 1)
                        dve.sem_inc(dt_arg[d], 1)
                for d in range(2):
                    B, sm, st, c = 4 * d, small[:, d], step[d], chunk[d][s]
                    bt = e.beta[:, c, 4 * d:4 * d + 4]
                    N, C, X, Y = (F[n][:, d] for n in ("N", "C", "X", "Y"))
                    dve.wait_ge(d_exp[d], s + 1)
                    dve.wait_ge(kk_mm[d], s + 1)
                    st(TT(N, F["D"][:, d], ps[:, B + 2, :], ALU.mult))
                    st(TT(h4(N), h4(N), col(bt), ALU.mult))
                    TT(h4(C), h4(N), b4(e.const(f"level{d}_0")), ALU.mult).then_inc(c_in[d], 1)
                    dve.wait_ge(c_in[d], 7 * s + 1)
                    st(TT(h4(X), b4(e.ident), h4(C), ALU.subtract))
                for d in range(2):
                    B, st = 4 * d, step[d]
                    N, C, X, Y = (F[n][:, d] for n in ("N", "C", "X", "Y"))
                    dve.wait_ge(c0t_mm[d], s + 1)
                    TT(h4(C), h4(N), b4(e.const(f"level{d}_1")), ALU.mult).then_inc(c_in[d], 1)
                    TT(h4(Y), b4(e.ident), ps[:, B + 1, :].rearrange("p (h n) -> p h n", h=GH), ALU.subtract).then_inc(xy_in[d], 1)
                for d in range(2):
                    B, sm, st, c = 4 * d, small[:, d], step[d], chunk[d][s]
                    bt = e.beta[:, c, 4 * d:4 * d + 4]
                    dve.wait_ge(sm_exp[d], s + 1)
                    st(TT(sm[:, 6], sm[:, 3], bt, ALU.mult))
                    TT(h4(F["kb"][:, d]), h4(e.gkt[:, c]), col(sm[:, 6]), ALU.mult)
                    TT(h4(F["vb"][:, d]), h4(e.gvt[:, c]), col(bt), ALU.mult)
                    if lat:
                        dve.wait_ge(dt_exp[d], s - TC + 1)
                        dve.wait_ge(kq_mm[d], s - TC + 1)
                        TT(F["aqk"][:, d], F["Dt"][:, d], ps[:, B + 3, :], ALU.mult)
                        dve.wait_ge(eg_exp[d], s + 1)
                        TT(h4(F["qd"][:, d]), e.gqT[:, :, c * P:(c + 1) * P], h4(F["eG"][:, d]), ALU.mult)
                    TT(h4(F["kd"][:, d]), h4(e.gkt[:, c]), col(sm[:, 4]), ALU.mult).then_inc(prods[d], 1)
                for lv in range(1, LV + 1):
                    if lv < LV:
                        for d in range(2):
                            dve.wait_ge(t1_mm[d], LV * s + lv)
                            TT(h4(F["C"][:, d]), h4(F["N"][:, d]), b4(e.const(f"level{d}_{lv + 1}")), ALU.mult).then_inc(c_in[d], 1)
                    for d in range(2):
                        B, X, Y = 4 * d, F["X"][:, d], F["Y"][:, d]
                        dve.wait_ge(y_mm[d], LV * s + lv)
                        if lv < LV:
                            TT(Y, Y, ps[:, B + 1, :], ALU.subtract).then_inc(own[d], 1)
                            step[d].n += 1
                            dve.wait_ge(x_mm[d], (LV - 1) * s + lv)
                            TT(X, X, ps[:, B + 2, :], ALU.subtract).then_inc(xy_in[d], 1)
                        else:
                            TT(Y, Y, ps[:, B + 1, :], ALU.subtract).then_inc(xy_in[d], 1)
                for d in range(2):
                    B, sm, st, c = 4 * d, small[:, d], step[d], chunk[d][s]
                    if lat:
                        j = c - TC
                        dve.wait_ge(o_mm[d], s - TC + 1)
                        if seen[j]:
                            TT(e.og[:, j], e.og[:, j], ps[:, B + 3, :], ALU.add).then_inc(o_read[d], 1)
                        else:
                            nc.vector.tensor_copy(e.og[:, j], ps[:, B + 3, :]).then_inc(o_read[d], 1)
                        seen[j] = True
                    dve.wait_ge(ku_mm[d], s + 1)
                    st(TT(h4(S[:, d]), h4(S[:, d]), col(sm[:, 5]), ALU.mult))
                    TT(S[:, d], S[:, d], ps[:, B + 1, :], ALU.add).then_inc(state[d], 1)
    A.give(*("f_" + n for n in F), "state", "g_small", "gqT", "gkT", "gvt", "gkt", "g", "beta")


def stage_gdn_out(e):
    nc, A = e.nc, e.arena
    e.catB = A.take("catB", GH, L)
    gate = A.take("gate", TL, GH * GD)
    gn = A.take("gdn_norm", GD)
    e.w_rows, e.s_wrows = A.take("w_rows", 3, KD, 512, high=True), [e.keep_sem(f"mr_w{i}") for i in range(3)]
    sq = A.take("gsq", 2, GH * GD)
    ss = A.take("gss", TL, GH)
    s_in, s_sq, s_ss, s_rt, s_own, s_y, s_tr, s_ev = (e.sem(f"go_{n}") for n in ("in", "sq", "ss", "rt", "own", "y", "tr", "ev"))
    h4 = lambda v: v.rearrange("p (h n) -> p h n", h=GH)
    with nc.Block() as block:
        @block.sync
        def _(sp):
            sp.dma_start(gate, e.gate_dram.rearrange("(t p) n -> p t n", p=P)).then_inc(s_in, 16)
            sp.dma_start(gn, broadcast_rows(e.in_["gdn_norm_g"][0])).then_inc(s_in, 16)
            w_mod = e.in_["w_mod"][0].rearrange("(k p) n -> p k n", p=P)
            for c in range(3):
                at = 2 * D + c * 512
                sp.dma_start(e.w_rows[:, c], w_mod[:, :, at:at + 512]).then_inc(e.s_wrows[c], 16)

        @block.scalar
        def _(act):
            for t in range(TL):
                if t >= 2:
                    act.wait_ge(s_ss, t - 1)
                nc.scalar.activation(sq[:, t % 2], e.og[:, t], ACT.Square).then_inc(s_sq, 1)
            act.wait_ge(s_own, 1)
            nc.scalar.activation(ss, ss, ACT.Sqrt).then_inc(s_rt, 1)
            for t in range(TL):
                act.wait_ge(s_tr, t + 1)
                nc.scalar.activation(e.catB[:, :, t * P:(t + 1) * P], h4(e.ps[:, t % 4, :]), ACT.Copy).then_inc(s_ev, 1)

        @block.vector
        def _(dve):
            step = Steps(dve, s_own)
            for t in range(TL):
                dve.wait_ge(s_sq, t + 1)
                nc.vector.tensor_reduce(ss[:, t], h4(sq[:, t % 2]), AX, ALU.add).then_inc(s_ss, 1)
            dve.wait_ge(s_ss, TL)
            step(nc.vector.tensor_scalar(ss, ss, 1.0 / GD, EPS, ALU.mult, ALU.add))
            dve.wait_ge(s_rt, 1)
            step(nc.vector.reciprocal(ss, ss))
            dve.wait_ge(s_in, 32)
            for t in range(TL):
                step(nc.vector.tensor_tensor(h4(gate[:, t]), h4(gate[:, t]), ss[:, t].unsqueeze(2).broadcast_to([P, GH, GD]), ALU.mult))
                step(nc.vector.tensor_tensor(h4(gate[:, t]), h4(gate[:, t]), gn.unsqueeze(1).broadcast_to([P, GH, GD]), ALU.mult))
                nc.vector.tensor_tensor(e.og[:, t], e.og[:, t], gate[:, t], ALU.mult).then_inc(s_y, 1)

        @block.tensor
        def _(pe):
            for t in range(TL):
                pe.wait_ge(s_y, t + 1)
                if t >= 4:
                    pe.wait_ge(s_ev, t - 3)
                for h in range(GH):
                    ins = nc.tensor.transpose(e.ps[:, t % 4, h * P:(h + 1) * P], e.og[:, t, h * P:(h + 1) * P], e.ident)
                ins.then_inc(s_tr, 1)
    A.give("gate", "gdn_norm", "gsq", "gss", "og")


def stage_rows(e):
    nc, A = e.nc, e.arena
    e.rows = A.take("rows", 4, D)
    w, s_w = e.w_rows, e.s_wrows
    bm = A.take("b_row", 2, 512)
    g2 = A.take("norm2", D)
    e.w_o, e.s_wo = A.take("w_o", KD, D), e.keep_sem("or_wo")
    w_mod = e.in_["w_mod"][0].rearrange("(k p) n -> p k n", p=P)
    s_b = [e.sem(f"mr_b{i}") for i in range(2)]
    s_in, s_mm, s_row, s_own = (e.sem(f"mr_{n}") for n in ("in", "mm", "row", "own"))
    NC = 8
    with nc.Block() as block:
        @block.sync
        def _(sp):
            for c in range(NC):
                if c >= 3:
                    sp.wait_ge(s_mm, c - 2)
                at = 2 * D + c * 512
                if c >= 3:
                    sp.dma_start(w[:, c % 3], w_mod[:, :, at:at + 512]).then_inc(s_w[c % 3], 16)
                if c >= 2:
                    sp.wait_ge(s_row, c - 1)
                sp.dma_start(bm[:, c % 2], broadcast_rows(e.in_["b_mod"][0, at:at + 512])).then_inc(s_b[c % 2], 16)
            sp.dma_start(g2, broadcast_rows(e.in_["norm2_g"][0])).then_inc(s_in, 16)
            sp.dma_start(e.w_o, e.in_["w_out"][0].rearrange("(k p) n -> p k n", p=P)).then_inc(e.s_wo, 16)

        @block.tensor
        def _(pe):
            for c in range(NC):
                pe.wait_ge(s_w[c % 3], 16 * (c // 3 + 1))
                if c >= 4:
                    pe.wait_ge(s_row, c - 3)
                for k in range(KD):
                    ins = nc.tensor.matmul(e.ps[:, c % 4, :], e.silu_c[:, k, 0:1].broadcast_to([P, P]), w[:, c % 3, k, :],
                                           start=(k == 0), stop=(k == KD - 1))
                ins.then_inc(s_mm, 1)

        @block.vector
        def _(dve):
            step = Steps(dve, s_own)
            for c in range(NC):
                dve.wait_ge(s_b[c % 2], 16 * (c // 2 + 1))
                dve.wait_ge(s_mm, c + 1)
                nc.vector.tensor_tensor(e.rows[:, c // 2, (c % 2) * 512:(c % 2 + 1) * 512], e.ps[:, c % 4, :], bm[:, c % 2], ALU.add).then_inc(s_row, 1)
            dve.wait_ge(s_row, NC)
            dve.wait_ge(s_in, 16)
            step(nc.vector.scalar_tensor_tensor(out=e.rows[:, 2], in0=e.rows[:, 2], scalar=1.0, in1=g2, op0=ALU.add, op1=ALU.mult))
    A.give("w_rows", "b_row", "norm2", "silu_c")


def stage_out_router(e):
    nc, A, ps = e.nc, e.arena, e.ps
    e.affT = A.take("affT", L)
    e.gateT = A.take("gateT", NE)
    e.idxT = A.take("idxT", NE)
    x1 = A.take("x1", TL, D)
    w = e.w_o
    xr = A.take("x_ring", 2, D)
    wr = A.take("w_r", KD, NE)
    h2 = A.take("h2", 2, D)
    h2T = A.take("h2T", 2, KD, P)
    junk = A.take("junk", D)
    ss = A.take("ss", TL)
    sm = A.take("r_small", 3, TL)
    pr = A.take("r_probs", TL, NE)
    e.x_dram = nc.dram_tensor("x_scratch", (L, D), F32).ap()
    e.h_dram = nc.dram_tensor("h_scratch", (L, D), F32).ap()
    s_x, s_hst = [e.sem(f"or_xin{i}") for i in range(2)], [e.keep_sem(f"or_hst{i}") for i in range(2)]
    s_w, s_mm, s_x1, s_x1a, s_sq, s_var, s_rt, s_own, s_h2, s_tr, s_hT, s_lg, s_mx, s_ex, s_pr, s_at = (
        e.sem(f"or_{n}") for n in ("w", "mm", "x1", "x1a", "sq", "var", "rt", "own", "h2", "tr", "hT", "lg", "mx", "ex", "pr", "at"))
    s_xst = e.keep_sem("or_xst")
    cat = lambda k: e.catA[:, k] if k < 4 else e.catB[:, k - 4]
    with nc.Block() as block:
        @block.sync
        def _(sp):
            sp.dma_start(wr, e.in_["w_router"][0].rearrange("(k p) n -> p k n", p=P)).then_inc(s_w, 16)
            for t in range(TL):
                if t >= 2:
                    sp.wait_ge(s_x1, t - 1)
                sp.dma_start(xr[:, t % 2], e.in_["x"][0, t * P:(t + 1) * P, :]).then_inc(s_x[t % 2], 16)

        @block.gpsimd
        def _(pool):
            for t in range(TL):
                pool.wait_ge(s_x1, t + 1)
                pool.dma_start(e.x_dram[t * P:(t + 1) * P, :], x1[:, t]).then_inc(s_xst, 16)
            for t in range(TL):
                pool.wait_ge(s_h2, t + 1)
                pool.dma_start(e.h_dram[t * P:(t + 1) * P, :], h2[:, t % 2]).then_inc(s_hst[t % 2], 16)
            pool.wait_ge(s_xst, 16 * TL)
            for i in range(2):
                pool.wait_ge(s_hst[i], 16 * TL // 2)

        @block.tensor
        def _(pe):
            pe.wait_ge(e.s_wo, 16)
            pe.wait_ge(s_w, 16)
            for t in range(TL):
                if t >= 2:
                    pe.wait_ge(s_x1a, t - 1)
                for j in range(2):
                    for k in range(KD):
                        ins = nc.tensor.matmul(ps[:, 2 * (t % 2) + j, :], cat(k)[:, t * P:(t + 1) * P], w[:, k, j * 512:(j + 1) * 512],
                                               start=(k == 0), stop=(k == KD - 1))
                ins.then_inc(s_mm, 1)
            def logits(t):
                pe.wait_ge(s_hT, t + 1)
                for k in range(KD):
                    ins = nc.tensor.matmul(ps[:, 0, t * NE:(t + 1) * NE], h2T[:, t % 2, k], wr[:, k], start=(k == 0), stop=(k == KD - 1))
                ins.then_inc(s_lg, 1)

            for t in range(TL):
                pe.wait_ge(s_h2, t + 1)
                if t >= 2:
                    pe.wait_ge(s_hT, t - 1)
                for k in range(KD):
                    ins = nc.tensor.transpose(ps[:, 4 + 2 * (t % 2) + k // 4, (k % 4) * P:(k % 4 + 1) * P], h2[:, t % 2, k * P:(k + 1) * P], e.ident)
                ins.then_inc(s_tr, 1)
                if t:
                    logits(t - 1)
            logits(TL - 1)
            pe.wait_ge(s_pr, 1)
            for t in range(TL):
                ins = nc.tensor.transpose(ps[0:NE, 2 + t // 4, (t % 4) * P:(t % 4 + 1) * P], pr[:, t], e.ident)
            ins.then_inc(s_at, 1)

        @block.scalar
        def _(act):
            for t in range(TL):
                act.wait_ge(s_x1, t + 1)
                if t:
                    act.wait_ge(s_sq, t)
                nc.scalar.activation(junk, x1[:, t], ACT.Square, accum_out=ss[:, t:t + 1]).then_inc(s_sq, 1)
            act.wait_ge(s_var, 1)
            nc.scalar.activation(ss, ss, ACT.Sqrt).then_inc(s_rt, 1)
            for t in range(TL):
                act.wait_ge(s_tr, t + 1)
                if t >= 2:
                    act.wait_ge(s_lg, t - 1)
                B = 4 + 2 * (t % 2)
                nc.scalar.activation(h2T[:, t % 2], ps[:, B:B + 2, :].rearrange("p a (b c) -> p (a b) c", c=P), ACT.Copy).then_inc(s_hT, 1)
            act.wait_ge(s_mx, 1)
            nc.scalar.activation(pr, pr, ACT.Exp).then_inc(s_ex, 1)

        @block.vector
        def _(dve):
            step = Steps(dve, s_own)
            for t in range(TL):
                dve.wait_ge(s_mm, t + 1)
                v = x1[:, t].rearrange("p (a n) -> p a n", a=2)
                nc.vector.tensor_tensor(v, ps[:, 2 * (t % 2):2 * (t % 2) + 2, :], e.rows[:, 0].rearrange("p (a n) -> p a n", a=2), ALU.mult).then_inc(s_x1a, 1)
                dve.wait_ge(s_x1a, t + 1)
                dve.wait_ge(s_x[t % 2], 16 * (t // 2 + 1))
                nc.vector.tensor_tensor(x1[:, t], x1[:, t], xr[:, t % 2], ALU.add).then_inc(s_x1, 1)
            dve.wait_ge(s_sq, TL)
            step(nc.vector.tensor_scalar(ss, ss, 1.0 / D, EPS, ALU.mult, ALU.add))
            nc.vector.reciprocal(ss, ss).then_inc(s_var, 1)
            dve.wait_ge(s_rt, 1)
            for t in range(TL):
                b = t % 2
                if t >= 2:
                    dve.wait_ge(s_hst[b], 16 * (t // 2))
                    dve.wait_ge(s_tr, t - 1)
                step(nc.vector.scalar_tensor_tensor(out=h2[:, b], in0=x1[:, t], scalar=ss[:, t:t + 1], in1=e.rows[:, 2], op0=ALU.mult, op1=ALU.mult))
                nc.vector.tensor_tensor(h2[:, b], h2[:, b], e.rows[:, 1], ALU.add).then_inc(s_h2, 1)
            all_ = lambda v: v.unsqueeze(2).broadcast_to([P, TL, NE])
            lg = ps[:, 0, 0:TL * NE].rearrange("p (t n) -> p t n", n=NE)
            dve.wait_ge(s_lg, TL)
            step(nc.vector.tensor_reduce(sm[:, 0], lg, AX, ALU.max))
            nc.vector.tensor_tensor(pr, lg, all_(sm[:, 0]), ALU.subtract).then_inc(s_mx, 1)
            dve.wait_ge(s_ex, 1)
            step(nc.vector.tensor_reduce(sm[:, 1], pr, AX, ALU.add))
            step(nc.vector.reciprocal(sm[:, 2], sm[:, 1]))
            nc.vector.tensor_tensor(pr, pr, all_(sm[:, 2]), ALU.mult).then_inc(s_pr, 1)
            dve.wait_ge(s_at, 1)
            nc.vector.tensor_copy(e.affT[0:NE, :], ps[0:NE, 2:4, :].rearrange("p a b -> p (a b)")).then_inc(s_own, 1)
    A.give("x1", "w_o", "x_ring", "w_r", "h2", "h2T", "junk", "ss", "r_small", "r_probs", "catA", "catB")


def stage_choose(e):
    nc, A, ps = e.nc, e.arena, e.ps
    val = A.take("val", CAP)
    idx = A.take("idx", CAP)
    idf = A.take("idxf", CAP)
    s_max, s_idx, s_rep, s_f, s_tr, s_own = (e.sem(f"ch_{n}") for n in ("max", "idx", "rep", "f", "tr", "own"))
    idx_u = idx.bitcast(U32)
    names = ("gate", "up", "down")
    e.W = {n: A.take("w_" + n, 2, 4, FF) for n in names}
    e.s_we = {n: [e.keep_sem(f"ex_{n}{i}") for i in range(2)] for n in names}
    with nc.Block() as block:
        @block.sync
        def _(sp):
            for n in names:
                for h in range(2):
                    src = e.in_["w_" + n][0, 0].rearrange("(p k) n -> p k n", k=KD)
                    sp.dma_start(e.W[n][:, h], src[:, 4 * h:4 * h + 4, :]).then_inc(e.s_we[n][h], 16)

        @block.vector
        def _(dve):
            a = e.affT[0:NE, :]
            for r in range(CAP // 8):
                s8 = slice(8 * r, 8 * r + 8)
                if r:
                    dve.wait_ge(s_rep, r)
                nc.vector.max(val[0:NE, s8], a).then_inc(s_max, 1)
                dve.wait_ge(s_max, r + 1)
                nc.vector.max_index(idx_u[0:NE, s8], val[0:NE, s8], a).then_inc(s_idx, 1)
                dve.wait_ge(s_idx, r + 1)
                nc.vector.match_replace(a, val[0:NE, s8], a, -1.0).then_inc(s_rep, 1)
            nc.vector.tensor_copy(idf[0:NE, :], idx_u[0:NE, :]).then_inc(s_f, 1)
            dve.wait_ge(s_tr, 1)
            nc.vector.tensor_copy(e.idxT.bitcast(U32), ps[:, 0, 0:NE]).then_inc(s_own, 1)
            nc.vector.tensor_copy(e.gateT, ps[:, 0, NE:2 * NE]).then_inc(s_own, 1)

        @block.tensor
        def _(pe):
            pe.wait_ge(s_f, 1)
            nc.tensor.transpose(ps[:, 0, 0:NE], idf[0:NE, :], e.ident[0:NE, 0:NE])
            nc.tensor.transpose(ps[:, 0, NE:2 * NE], val[0:NE, :], e.ident[0:NE, 0:NE]).then_inc(s_tr, 1)
    A.give("val", "idx", "idxf", "affT")


def stage_experts(e):
    nc, A, ps = e.nc, e.arena, e.ps
    names = ("gate", "up", "down")
    W, s_w = e.W, e.s_we
    xe = A.take("xe", 2, D)
    xT = A.take("xT", 2, KD, P)
    sg = A.take("sg", FF)
    hid = A.take("hid", FF)
    hT = A.take("hidT", KD, P)
    y = A.take("y", D)
    gcol = A.take("gcol", 1)
    s_xe = [e.keep_sem(f"ex_xe{i}") for i in range(2)]
    s_xt, s_xT, s_g, s_u, s_sg, s_hid, s_ht, s_hT, s_d, s_gc, s_y = (
        e.sem(f"ex_{n}") for n in ("xt", "xTin", "gmm", "umm", "sg", "hid", "ht", "hTin", "dmm", "gcol", "y"))
    s_out = e.keep_sem("ex_out")
    done = {"gate": s_g, "up": s_u, "down": s_d}
    src = {n: e.in_["w_" + n][0].rearrange("e (p k) n -> e p k n", k=KD) for n in names}
    with nc.Block() as block:
        @block.sync
        def _(sp):
            def load(n, i):
                for half in range(2):
                    sp.wait_ge(done[n], 2 * i + half - 1)
                    sp.dma_start(W[n][:, half], src[n][bass.ds(i, 1), :, 4 * half:4 * half + 4, :].rearrange("a p k n -> p (a k) n")).then_inc(s_w[n][half], 16)
            load("gate", 1)
            load("up", 1)
            with sp.Fori(2, NE) as i:
                load("gate", i)
                load("down", i - 1)
                load("up", i)
            load("down", NE - 1)

        @block.gpsimd
        def _(pool):
            def gather(i):
                if i >= 2:
                    pool.wait_ge(s_xt, i - 1)
                nc.gpsimd.indirect_dma_start(out=xe[:, i % 2], out_offset=None, in_=e.h_dram,
                                             in_offset=bass.IndirectOffsetOnAxis(ap=e.idxT[:, i:i + 1].bitcast(U32), axis=0)).then_inc(s_xe[i % 2], 16)

            def scatter(i):
                pool.wait_ge(s_y, i + 1)
                nc.gpsimd.indirect_dma_start(out=e.x_dram, out_offset=bass.IndirectOffsetOnAxis(ap=e.idxT[:, i:i + 1].bitcast(U32), axis=0), in_=y,
                                             in_offset=None, compute_op=ALU.add).then_inc(s_out, 16)
                pool.wait_ge(s_out, 16 * (i + 1))
            gather(0)
            gather(1)
            for i in range(NE):
                if 1 <= i < NE - 1:
                    gather(i + 1)
                if i:
                    scatter(i - 1)
            scatter(NE - 1)

        @block.tensor
        def _(pe):
            def half(n, banks, lhs, i, h):
                pe.wait_ge(s_w[n][h], 16 * (i + 1))
                for k in range(4 * h, 4 * h + 4):
                    for j in range(2):
                        ins = nc.tensor.matmul(ps[:, banks + j, :], lhs[:, k], W[n][:, h, k % 4, j * 512:(j + 1) * 512],
                                               start=(k == 0), stop=(k == KD - 1))
                ins.then_inc(done[n], 1)

            def turn(rows, signal):
                for k in range(KD):
                    ins = nc.tensor.transpose(ps[:, 6 + k // 4, (k % 4) * P:(k % 4 + 1) * P], rows.rearrange("p (m k) -> p k m", k=KD)[:, k], e.ident)
                ins.then_inc(signal, 1)

            def down(i, first):
                pe.wait_ge(s_hT, i + 1)
                if not first:
                    pe.wait_ge(s_y, i)
                for h in range(2):
                    half("down", 4, hT, i, h)

            def body(i, b, first, last, second=False, rounds=None):
                x = xT[:, b]
                pe.wait_ge(s_xT, i + 1)
                if not first:
                    pe.wait_ge(s_sg, i)
                half("gate", 0, x, i, 0)
                if not first:
                    pe.wait_ge(s_hid, i)
                    turn(hid, s_ht)
                half("gate", 0, x, i, 1)
                if not first:
                    down(i - 1, second)
                if not last:
                    pe.wait_ge(s_xe[1 - b], 16 * rounds)
                    turn(xe[:, 1 - b], s_xt)
                for h in range(2):
                    half("up", 2, x, i, h)

            pe.wait_ge(s_xe[0], 16)
            turn(xe[:, 0], s_xt)
            body(0, 0, True, False, rounds=1)
            body(1, 1, False, False, second=True, rounds=2)
            with pe.Fori(1, NE // 2 - 1) as j:
                body(2 * j, 0, False, False, rounds=j + 1)
                body(2 * j + 1, 1, False, False, rounds=j + 2)
            body(NE - 2, 0, False, False, rounds=NE // 2)
            body(NE - 1, 1, False, True)
            pe.wait_ge(s_hid, NE)
            turn(hid, s_ht)
            down(NE - 1, False)

        @block.scalar
        def _(act):
            def rows_in(i, b, first):
                act.wait_ge(s_xt, i + 1)
                if not first:
                    act.wait_ge(s_u, 2 * i - 2)
                nc.scalar.activation(xT[:, b], ps[:, 6:8, :].rearrange("p a (b c) -> p (a b) c", c=P), ACT.Copy).then_inc(s_xT, 1)

            def gate(i, first):
                act.wait_ge(s_g, 2 * i + 2)
                if not first:
                    act.wait_ge(s_hid, i)
                nc.scalar.activation(sg, ps[:, 0:2, :].rearrange("p a b -> p (a b)"), ACT.Silu).then_inc(s_sg, 1)
            rows_in(0, 0, True)
            gate(0, True)
            rows_in(1, 1, True)
            gate(1, False)
            with act.Fori(1, NE // 2) as j:
                for b in range(2):
                    rows_in(2 * j + b, b, False)
                    gate(2 * j + b, False)

        @block.vector
        def _(dve):
            def hidden(i, first):
                dve.wait_ge(s_u, 2 * i + 2)
                dve.wait_ge(s_sg, i + 1)
                if not first:
                    dve.wait_ge(s_ht, i)
                nc.vector.tensor_tensor(hid, sg, ps[:, 2:4, :].rearrange("p a b -> p (a b)"), ALU.mult).then_inc(s_hid, 1)

            def output(i, first):
                dve.wait_ge(s_ht, i + 1)
                if not first:
                    dve.wait_ge(s_d, 2 * i)
                nc.vector.tensor_copy(hT, ps[:, 6:8, :].rearrange("p a (b c) -> p (a b) c", c=P)).then_inc(s_hT, 1)
                if not first:
                    dve.wait_ge(s_y, i)
                nc.vector.tensor_copy(gcol, e.gateT[:, bass.ds(i, 1)]).then_inc(s_gc, 1)
                dve.wait_ge(s_gc, i + 1)
                dve.wait_ge(s_d, 2 * i + 2)
                if not first:
                    dve.wait_ge(s_out, 16 * i)
                nc.vector.scalar_tensor_tensor(out=y, in0=ps[:, 4:6, :].rearrange("p a b -> p (a b)"), scalar=gcol, in1=e.rows[:, 3],
                                               op0=ALU.mult, op1=ALU.mult).then_inc(s_y, 1)
            hidden(0, True)
            output(0, True)
            with dve.Fori(1, NE) as i:
                hidden(i, False)
                output(i, False)
    A.give(*("w_" + n for n in names), "xe", "xT", "sg", "hid", "hidT", "y", "gcol", "rows", "idxT", "gateT")


def stage_between(e):
    nc, A, ps = e.nc, e.arena, e.ps
    e.hT2 = A.take("hT2", KD, L)
    e.hT_dram = nc.dram_tensor("hT_scratch", (P, KD * L), F32).ap()
    e.x3_dram = nc.dram_tensor("x3_scratch", (L, D), F32).ap()
    x = A.take("x", TL, D)
    rows = A.take("gains", 2, D)
    xn = A.take("xn", 2, D)
    junk = A.take("junk", D)
    ss = A.take("ss", 2, TL)
    s_x = [e.sem(f"bt_xin{i}") for i in range(TL)]
    e.w_p2, e.s_wp2 = A.take("w_p2", 3, KD, 512, high=True), [e.keep_sem(f"p2_w{i}") for i in range(3)]
    s_in, s_own, s_rt, s_tr, s_ev, s_hst, s_x3 = (e.sem(f"bt_{n}") for n in ("in", "own", "rt", "tr", "ev", "hst", "x3"))
    s_st = [e.sem(f"bt_st{i}") for i in range(TL)]
    s_sq, s_var, s_n = ([e.sem(f"bt_{n}{i}") for i in range(2)] for n in ("sq", "var", "n"))
    with nc.Block() as block:
        @block.sync
        def _(sp):
            sp.dma_start(rows[:, 0], broadcast_rows(e.in_["final_g"])).then_inc(s_in, 16)
            sp.dma_start(rows[:, 1], broadcast_rows(e.in_["norm1_g_2"][0])).then_inc(s_in, 16)
            for t in range(TL):
                sp.dma_start(x[:, t], e.x_dram[t * P:(t + 1) * P, :]).then_inc(s_x[t], 16)
            w_in = e.in_["w_in_2"][0].rearrange("(k p) n -> p k n", p=P)
            for c, (at, n) in enumerate(CHUNKS2):
                sp.dma_start(e.w_p2[:, c, :, 0:n], w_in[:, :, at:at + n]).then_inc(e.s_wp2[c], 16)
            for t in range(TL):
                sp.wait_ge(s_x3, t + 1)
                sp.dma_start(e.x3_dram[t * P:(t + 1) * P, :], x[:, t]).then_inc(s_st[t], 16)
            sp.wait_ge(s_ev, 2 * TL)
            sp.dma_start(e.hT_dram, e.hT2.rearrange("p a b -> p (a b)")).then_inc(s_hst, 16)
            sp.wait_ge(s_hst, 16)
            for t in range(TL):
                sp.wait_ge(s_st[t], 16)

        @block.scalar
        def _(act):
            n = 0
            for i in range(2):
                for t in range(TL):
                    if i == 0:
                        act.wait_ge(s_x[t], 16)
                    else:
                        act.wait_ge(s_x3, t + 1)
                    if n:
                        act.wait_ge(s_sq[(n - 1) // TL], (n - 1) % TL + 1)
                    nc.scalar.activation(junk, x[:, t], ACT.Square, accum_out=ss[:, i, t:t + 1]).then_inc(s_sq[i], 1)
                    n += 1
                act.wait_ge(s_var[i], 1)
                nc.scalar.activation(ss[:, i], ss[:, i], ACT.Sqrt).then_inc(s_rt, 1)
            for t in range(TL):
                act.wait_ge(s_tr, 2 * t + 2)
                for j in range(2):
                    ins = nc.scalar.activation(e.hT2[:, 4 * j:4 * j + 4, t * P:(t + 1) * P],
                                               ps[:, (2 * t + j) % 8, :].rearrange("p (a b) -> p a b", b=P), ACT.Copy)
                    ins.then_inc(s_ev, 1)

        @block.vector
        def _(dve):
            step = Steps(dve, s_own)
            dve.wait_ge(s_in, 32)
            for i in range(2):
                dve.wait_ge(s_sq[i], TL)
                step(nc.vector.tensor_scalar(ss[:, i], ss[:, i], 1.0 / D, EPS, ALU.mult, ALU.add))
                nc.vector.reciprocal(ss[:, i], ss[:, i]).then_inc(s_var[i], 1)
                dve.wait_ge(s_rt, i + 1)
                for t in range(TL):
                    if i == 1 and t >= 2:
                        dve.wait_ge(s_tr, 2 * (t - 1))
                    out = x[:, t] if i == 0 else xn[:, t % 2]
                    nc.vector.scalar_tensor_tensor(out=out, in0=x[:, t], scalar=ss[:, i, t:t + 1], in1=rows[:, i],
                                                   op0=ALU.mult, op1=ALU.mult).then_inc(s_x3 if i == 0 else s_n[1], 1)

        @block.tensor
        def _(pe):
            for t in range(TL):
                pe.wait_ge(s_n[1], t + 1)
                if t >= 4:
                    pe.wait_ge(s_ev, 2 * (t - 3))
                for k in range(KD):
                    ins = nc.tensor.transpose(ps[:, (2 * t + k // 4) % 8, (k % 4) * P:(k % 4 + 1) * P], xn[:, t % 2, k * P:(k + 1) * P], e.ident)
                    if k % 4 == 3:
                        ins.then_inc(s_tr, 1)
    A.give("x", "xn", "gains", "junk", "ss")


TWO_PI = 2 * np.pi
RQ, RK, RV, RQI, RKI, RWI, RN = 0, 512, 576, 640, 896, 960, 964
CHUNKS2 = ((0, 512), (512, 512), (1024, RN - 512))


def stage_project2(e):
    nc, A, ps = e.nc, e.arena, e.ps
    e.U = A.take("U", SG, CH, SP)
    e.r = A.take("r", TL, RN)
    w, s_w, chunks = e.w_p2, e.s_wp2, CHUNKS2
    s_mm, s_ev = e.sem("p2_mm"), e.sem("p2_ev")
    NP = len(chunks) * TL
    BANK = lambda i: 2 + i % 6
    J = SG // 2
    e.Wr, e.nWi = A.take("Wr", J, (CH + 1), SP), A.take("nWi", J, (CH + 1), SP)
    e.Bc = A.take("Bc", 2, J, SP)
    room = w.rearrange("p a b c -> p (a b c)")
    e.VT, e.E = (room[:, i * 2 * J * P:(i + 1) * 2 * J * P].rearrange("p (a b c) -> p a b c", a=2, b=J) for i in range(2))
    e.uT = room[:, 4 * J * P:6 * J * P].rearrange("p (a b) -> p a b", a=SG)
    e.mag8 = A.take("mag8", J)
    V = A.take("V", 2 * J, CH, SP)
    q = A.take("q_small", 40, J)
    Bn = A.take("Bn", 2, J, SP)
    Cn = A.take("Cn", 2, 4, P)
    Cc = A.take("Cc", 2, J, SP)
    pw = A.take("powers", 2, J * (CH + 1))
    tmp = A.take("ssm_tmp", J * (CH + 1) * SP)
    tmp2 = A.take("ssm_tmp2", J * (CH + 1) * SP)
    s_in, s_own, s_act, s_tr, s_ct, s_c, s_v, s_u, s_uo, s_vt, s_ang = (e.sem(f"st_{n}") for n in ("in", "own", "act", "tr", "ct", "c", "v", "u", "uo", "vt", "ang"))
    g = lambda n: e.in_[n + "_2"][0]
    (AR, AI, DT, T1, MAG, MAG8, TH, KK, R, SN_, CS, R2, ABR, ABI, DEN, NR, CR, CI, X1, X2, P2R, P2I, P4R, P4I, P8R, P8I, FR, FI, G1, G2) = range(30)
    c_ = lambda i: q[:, i]
    with nc.Block() as block:
        @block.sync
        def _(sp):
            with nc.allow_non_contiguous_dma("small parameters by state"):
                for name, i in (("A_re", AR), ("A_im", AI)):
                    for h in range(2):
                        sp.dma_start(q[64 * h:64 * h + 64, i], g(name).rearrange("(j h) n -> h n j", h=2)[h]).then_inc(s_in, 16)
                for h in range(2):
                    sp.dma_start(q[64 * h:64 * h + 64, DT], g("log_dt").rearrange("(j h) -> h j", h=2)[h].partition_broadcast(64)).then_inc(s_in, 16)
                for name, i in (("B_re", 0), ("B_im", 1)):
                    for h in range(2):
                        sp.dma_start(Bn[64 * h:64 * h + 64, i], g(name).rearrange("(j h) n p -> h n j p", h=2)[h]).then_inc(s_in, 16)
                for name, i in (("C_re", 0), ("C_im", 1)):
                    for h in range(2):
                        sp.dma_start(Cn[:, i, :, 64 * h:64 * h + 64], g(name).rearrange("(a g) p n -> (g p) a n", a=4)).then_inc(s_in, 16)

        @block.tensor
        def _(pe):
            pe.wait_ge(s_in, 14 * 16)
            for i in range(2):
                for a in range(4):
                    ins = nc.tensor.transpose(ps[:, i, a * P:(a + 1) * P], Cn[:, i, a, :], e.ident)
                ins.then_inc(s_ct, 1)
            for i in range(NP):
                c, t = divmod(i, TL)
                n = chunks[c][1]
                if t == 0:
                    pe.wait_ge(s_w[c], 16)
                if i >= 6:
                    pe.wait_ge(s_ev, i - 5)
                for k in range(KD):
                    lhs = e.hT2[:, k, t:L:CH] if c == 0 else e.hT2[:, k, t * P:(t + 1) * P]
                    ins = nc.tensor.matmul(ps[:, BANK(i), 0:n], lhs, w[:, c, k, 0:n], start=(k == 0), stop=(k == KD - 1))
                ins.then_inc(s_mm, 1)
            pe.wait_ge(s_ev, NP)
            for i in range(8):
                if i >= 2:
                    pe.wait_ge(s_uo, i - 1)
                for k in range(4):
                    gr = 4 * i + k
                    ins = nc.tensor.transpose(ps[:, 4 + i % 2, k * P:(k + 1) * P], e.U[:, gr].rearrange("p a b -> p (a b)"), e.ident)
                ins.then_inc(s_u, 1)
            pe.wait_ge(s_v, 1)
            for i in range(8):
                if i < 2:
                    pe.wait_ge(s_c, 2)
                else:
                    pe.wait_ge(s_vt, i - 1)
                for k in range(4):
                    ins = nc.tensor.transpose(ps[:, i % 2, k * P:(k + 1) * P], V[:, 4 * i + k].rearrange("p a b -> p (a b)"), e.ident)
                ins.then_inc(s_tr, 1)

        @block.scalar
        def _(act):
            act.wait_ge(s_ang, 1)
            nc.scalar.activation(q[:, SN_:SN_ + 2], q[:, SN_:SN_ + 2], ACT.Sin).then_inc(s_act, 1)
            for i in range(NP):
                c, t = divmod(i, TL)
                n = chunks[c][1]
                act.wait_ge(s_mm, i + 1)
                dst = e.U[:, :, t] if c == 0 else e.r[:, t, (c - 1) * 512:(c - 1) * 512 + n]
                src = ps[:, BANK(i), 0:n].rearrange("p (g c) -> p g c", c=SP) if c == 0 else ps[:, BANK(i), 0:n]
                nc.scalar.activation(dst, src, ACT.Copy).then_inc(s_ev, 1)
            for i in range(8):
                act.wait_ge(s_u, i + 1)
                nc.scalar.activation(e.uT[:, 4 * i:4 * i + 4], ps[:, 4 + i % 2, :].rearrange("p (a b) -> p a b", b=P), ACT.Copy).then_inc(s_uo, 1)
            for i in range(8):
                act.wait_ge(s_tr, i + 1)
                nc.scalar.activation(e.VT[:, i // 4, 4 * (i % 4):4 * (i % 4) + 4], ps[:, i % 2, :].rearrange("p (a b) -> p a b", b=P), ACT.Copy).then_inc(s_vt, 1)

        @block.vector
        def _(dve):
            step = Steps(dve, s_own)
            TT, TS, STT = nc.vector.tensor_tensor, nc.vector.tensor_scalar, nc.vector.scalar_tensor_tensor

            def cmul(o_r, o_i, a_r, a_i, b_r, b_i, t1, t2):
                step(TT(o_r, a_r, b_r, ALU.mult))
                step(TT(t1, a_i, b_i, ALU.mult))
                step(TT(o_r, o_r, t1, ALU.subtract))
                step(TT(o_i, a_r, b_i, ALU.mult))
                step(TT(t2, a_i, b_r, ALU.mult))
                step(TT(o_i, o_i, t2, ALU.add))

            def exp(out, x):
                n = out.shape[1]
                k, rest, p = (q[:, 30 + 2 * i:30 + 2 * i + n] for i in range(3))
                magic = 12582912.0
                hi = 0.693359375
                lo = float(np.log(2.0) - hi)
                step(TS(rest, x, 88.0, -87.0, ALU.min, ALU.max))
                step(TS(k, rest, float(1 / np.log(2.0)), magic, ALU.mult, ALU.add))
                step(TS(k, k, -magic, None, ALU.add))
                step(STT(out=rest, in0=k, scalar=-hi, in1=rest, op0=ALU.mult, op1=ALU.add))
                step(STT(out=rest, in0=k, scalar=-lo, in1=rest, op0=ALU.mult, op1=ALU.add))
                c = [1.0]
                for i in range(1, 9):
                    c.append(c[-1] / i)
                step(TS(p, rest, c[8], None, ALU.mult))
                for i in range(7, 0, -1):
                    step(STT(out=p, in0=p, scalar=c[i], in1=rest, op0=ALU.add, op1=ALU.mult))
                step(TS(p, p, 1.0, None, ALU.add))
                step(TS(k, k, 127.0, float(2 ** 23), ALU.add, ALU.mult))
                step(nc.vector.tensor_copy(rest.bitcast(I32), k))
                step(TT(out, p, rest, ALU.mult))

            dve.wait_ge(s_in, 14 * 16)
            exp(q[:, DT:DT + 1], q[:, DT:DT + 1])
            step(TT(c_(T1), c_(AR), c_(DT), ALU.mult))
            step(TS(c_(MAG8), c_(T1), 8.0, None, ALU.mult))
            step(nc.vector.tensor_copy(c_(MAG), c_(T1)))
            exp(q[:, MAG:MAG + 2], q[:, MAG:MAG + 2])
            step(nc.vector.tensor_copy(e.mag8, c_(MAG8)))
            step(TT(c_(TH), c_(AI), c_(DT), ALU.mult))
            MAGIC = 12582912.0
            step(TS(c_(KK), c_(TH), 1.0 / TWO_PI, MAGIC, ALU.mult, ALU.add))
            step(TS(c_(KK), c_(KK), -MAGIC, None, ALU.add))
            c1 = 6.28125
            c2 = float(np.float32(round((TWO_PI - c1) * 2 ** 20) / 2 ** 20))
            c3 = TWO_PI - c1 - c2
            step(TS(c_(R), c_(KK), -c1, None, ALU.mult))
            step(TT(c_(R), c_(TH), c_(R), ALU.add))
            step(nc.vector.scalar_tensor_tensor(out=c_(R), in0=c_(KK), scalar=-c2, in1=c_(R), op0=ALU.mult, op1=ALU.add))
            step(nc.vector.scalar_tensor_tensor(out=c_(R), in0=c_(KK), scalar=-c3, in1=c_(R), op0=ALU.mult, op1=ALU.add))
            step(TS(c_(R2), c_(R), np.pi / 2, -TWO_PI, ALU.is_gt, ALU.mult))
            step(TT(c_(R2), c_(R2), c_(R), ALU.add))
            step(TS(c_(R2), c_(R2), np.pi / 2, None, ALU.add))
            step(TS(c_(SN_), c_(R), 3.1415925, -3.1415925, ALU.min, ALU.max))
            TS(c_(CS), c_(R2), 3.1415925, -3.1415925, ALU.min, ALU.max).then_inc(s_ang, 1)
            step(TT(c_(DEN), c_(AR), c_(AR), ALU.mult))
            step(TT(c_(X1), c_(AI), c_(AI), ALU.mult))
            step(TT(c_(DEN), c_(DEN), c_(X1), ALU.add))
            step(nc.vector.reciprocal(c_(DEN), c_(DEN)))
            dve.wait_ge(s_act, 1)
            step(TT(c_(ABR), c_(MAG), c_(CS), ALU.mult))
            step(TT(c_(ABI), c_(MAG), c_(SN_), ALU.mult))
            step(TS(c_(NR), c_(ABR), -1.0, None, ALU.add))
            step(TT(c_(CR), c_(NR), c_(AR), ALU.mult))
            step(TT(c_(X1), c_(ABI), c_(AI), ALU.mult))
            step(TT(c_(CR), c_(CR), c_(X1), ALU.add))
            step(TT(c_(CR), c_(CR), c_(DEN), ALU.mult))
            step(TT(c_(CI), c_(ABI), c_(AR), ALU.mult))
            step(TT(c_(X2), c_(NR), c_(AI), ALU.mult))
            step(TT(c_(CI), c_(CI), c_(X2), ALU.subtract))
            step(TT(c_(CI), c_(CI), c_(DEN), ALU.mult))
            bc = lambda v, *s: v.unsqueeze(2).broadcast_to([P, J, s[0]])
            t3 = lambda v, n: v[:, 0:J * n].rearrange("p (j a) -> p j a", j=J)
            cmul(e.Bc[:, 0], e.Bc[:, 1], Bn[:, 0], Bn[:, 1], bc(c_(CR), SP), bc(c_(CI), SP), t3(tmp, SP), t3(tmp2, SP))
            for i in range(2):
                dve.wait_ge(s_ct, i + 1)
                for h in range(2):
                    src = ps[64 * h:64 * h + 64, i, :].rearrange("p (j h c) -> p j h c", h=2, c=SP)[:, :, h]
                    ins = nc.vector.tensor_copy(Cc[64 * h:64 * h + 64, i], src)
                ins.then_inc(s_c, 1)
            pr, pi = (pw[:, i].rearrange("p (j t) -> p j t", j=J) for i in range(2))
            step(nc.vector.memset(pr[:, :, 0], 1.0))
            step(nc.vector.memset(pi[:, :, 0], 0.0))
            step(nc.vector.tensor_copy(pr[:, :, 1], c_(ABR)))
            step(nc.vector.tensor_copy(pi[:, :, 1], c_(ABI)))
            for m in (1, 2, 4):
                b = [v[:, :, m:m + 1].broadcast_to([P, J, m]) for v in (pr, pi)]
                cmul(pr[:, :, m + 1:2 * m + 1], pi[:, :, m + 1:2 * m + 1], pr[:, :, 1:m + 1], pi[:, :, 1:m + 1], b[0], b[1], t3(tmp, m), t3(tmp2, m))
            T9 = CH + 1
            dve.wait_ge(s_c, 2)
            cb = [Cc[:, i].unsqueeze(2).broadcast_to([P, J, T9, SP]) for i in range(2)]
            pb = [v.unsqueeze(3).broadcast_to([P, J, T9, SP]) for v in (pr, pi)]
            t4 = lambda v, n: v[:, 0:J * n * SP].rearrange("p (j t a) -> p j t a", j=J, t=n)
            cmul(e.Wr, e.nWi, cb[0], cb[1], pb[0], pb[1], t4(tmp, T9), t4(tmp2, T9))
            step(TS(e.nWi, e.nWi, -1.0, None, ALU.mult))
            bb = [e.Bc[:, i].unsqueeze(2).broadcast_to([P, J, CH, SP]) for i in range(2)]
            pb = [v[:, :, CH - 1::-1].unsqueeze(3).broadcast_to([P, J, CH, SP]) for v in (pr, pi)]
            cmul(V[:, 0:J], V[:, J:2 * J], bb[0], bb[1], pb[0], pb[1], t4(tmp, CH), t4(tmp2, CH))
            dve.sem_inc(s_v, 1)
            cmul(c_(P2R), c_(P2I), c_(CS), c_(SN_), c_(CS), c_(SN_), c_(X1), c_(X2))
            cmul(c_(P4R), c_(P4I), c_(P2R), c_(P2I), c_(P2R), c_(P2I), c_(X1), c_(X2))
            cmul(c_(P8R), c_(P8I), c_(P4R), c_(P4I), c_(P4R), c_(P4I), c_(X1), c_(X2))
            dve.wait_ge(s_mm, NP)
            step(nc.vector.memset(e.E[:, 0, :, 0:1], 1.0))
            step(nc.vector.memset(e.E[:, 1, :, 0:1], 0.0))
            at = (P8R, P8I)
            m = 1
            while m < NCH:
                b = [c_(v).unsqueeze(2).broadcast_to([P, J, m]) for v in at]
                cmul(e.E[:, 0, :, m:2 * m], e.E[:, 1, :, m:2 * m], e.E[:, 0, :, 0:m], e.E[:, 1, :, 0:m], b[0], b[1], t3(tmp, m), t3(tmp2, m))
                to = (FR, FI) if at != (FR, FI) else (G1, G2)
                cmul(c_(to[0]), c_(to[1]), c_(at[0]), c_(at[1]), c_(at[0]), c_(at[1]), c_(X1), c_(X2))
                at = to
                m *= 2
    A.give("hT2", "U", "V", "q_small", "Bn", "Cn", "Cc", "powers", "ssm_tmp", "ssm_tmp2")


def stage_ssm(e):
    nc, A, ps = e.nc, e.arena, e.ps
    J = SG // 2
    M = A.take("M", SG, P)
    e.ygT = A.take("ygT", 4, L)
    K = e.ygT.rearrange("p a (g c) -> p (a g) c", c=P)
    Brep = A.take("Brep", 2, 2, CH, SP)
    a8 = A.take("a8", J, P)
    z = A.take("z", 2, J, P)
    Sp = A.take("Sp", 2, J, P + 1)
    t1, t2 = A.take("t1", 512), A.take("t2", 512)
    Y = A.take("Y", CH, 512)
    dd = A.take("d_skip", SG)
    s_in, s_own, s_rep, s_k, s_ke, s_mz, s_sh, s_v, s_vd, s_S, s_y, s_yo, s_tr, s_tro, s_d = (
        e.sem(f"ss_{n}") for n in ("in", "own", "rep", "k", "ke", "mz", "sh", "v", "vd", "S", "y", "yo", "tr", "tro", "d"))
    with nc.Block() as block:
        @block.sync
        def _(sp):
            with nc.allow_non_contiguous_dma("the skip by channel"):
                for t in range(CH):
                    sp.dma_start(dd[SP * t:SP * t + SP, :], e.in_["D_skip_2"][0].rearrange("(g p) -> p g", p=SP)).then_inc(s_in, 16)
            sp.wait_ge(s_ke, SG // 4)
            sp.wait_ge(s_mz, 1)
            for t in range(CH):
                sp.dma_start(M[SP * t:SP * t + SP, :, SP * t:P], K[SP * t:SP * t + SP, :, 0:P - SP * t]).then_inc(s_sh, 16)

        @block.tensor
        def _(pe):
            for g in range(SG):
                j, h = divmod(g, 2)
                b = j // 4
                if h == 0:
                    pe.wait_ge(s_rep, j + 1)
                if g % 8 == 0 and b >= 2:
                    pe.wait_ge(s_ke, 2 * (b - 1))
                o = ps[:, 2 * (b % 2) + h, (j % 4) * P:(j % 4 + 1) * P]
                hh = slice(64 * h, 64 * h + 64)
                nc.tensor.matmul(o, Brep[hh, j % 2, 0].rearrange("p a b -> p (a b)"), e.Wr[hh, j, 0:CH].rearrange("p a b -> p (a b)"), start=True, stop=False)
                ins = nc.tensor.matmul(o, Brep[hh, j % 2, 1].rearrange("p a b -> p (a b)"), e.nWi[hh, j, 0:CH].rearrange("p a b -> p (a b)"), start=False, stop=True)
                ins.then_inc(s_k, 1)
            for b in range(4):
                if b >= 2:
                    pe.wait_ge(s_vd, b - 1)
                for j in range(4 * b, 4 * b + 4):
                    for h in range(2):
                        for c in range(2):
                            ins = nc.tensor.matmul(ps[64 * h:64 * h + 64, 4 + 2 * c + b % 2, (j % 4) * P:(j % 4 + 1) * P],
                                                   e.VT[:, c, j, 64 * h:64 * h + 64], e.uT[:, 2 * j + h], start=True, stop=True)
                ins.then_inc(s_v, 1)
            pe.wait_ge(s_S, 1)
            pe.wait_ge(s_d, 1)
            for g in range(SG):
                j, h = divmod(g, 2)
                b = j // 4
                if g % 8 == 0 and b >= 2:
                    pe.wait_ge(s_yo, 2 * (b - 1))
                o = ps[:, 2 * (b % 2) + h, (j % 4) * P:(j % 4 + 1) * P]
                hh = slice(64 * h, 64 * h + 64)
                nc.tensor.matmul(o, e.uT[:, g], M[:, g], start=True, stop=False)
                nc.tensor.matmul(o, Sp[hh, 0, j, 0:P], e.Wr[hh, j, 1:CH + 1].rearrange("p a b -> p (a b)"), start=False, stop=False)
                ins = nc.tensor.matmul(o, Sp[hh, 1, j, 0:P], e.nWi[hh, j, 1:CH + 1].rearrange("p a b -> p (a b)"), start=False, stop=True)
                ins.then_inc(s_y, 1)
            for s in range(CH):
                pe.wait_ge(s_yo, SG // 4)
                if s >= 2:
                    pe.wait_ge(s_tro, s - 1)
                for k in range(4):
                    ins = nc.tensor.transpose(ps[:, s % 2, k * P:(k + 1) * P], Y[:, s, k * P:(k + 1) * P], e.ident)
                ins.then_inc(s_tr, 1)

        @block.scalar
        def _(act):
            for b in range(4):
                act.wait_ge(s_k, 8 * b + 8)
                for h in range(2):
                    nc.scalar.activation(K.rearrange("p (j h) c -> p h j c", h=2)[:, h, 4 * b:4 * b + 4],
                                         ps[:, 2 * (b % 2) + h, :].rearrange("p (a b) -> p a b", b=P), ACT.Copy).then_inc(s_ke, 1)
            for b in range(4):
                act.wait_ge(s_y, 8 * b + 8)
                for h in range(2):
                    nc.scalar.activation(Y.rearrange("p t (j h c) -> p h j t c", h=2, c=SP)[:, h, 4 * b:4 * b + 4],
                                         ps[:, 2 * (b % 2) + h, :].rearrange("p (g t c) -> p g t c", g=4, t=CH), ACT.Gelu_apprx_tanh).then_inc(s_yo, 1)
            for s in range(CH):
                act.wait_ge(s_tr, s + 1)
                nc.scalar.activation(e.ygT[:, :, s:L:CH], ps[:, s % 2, :].rearrange("p (a b) -> p a b", b=P), ACT.Copy).then_inc(s_tro, 1)

        @block.vector
        def _(dve):
            step = Steps(dve, s_own)
            TT = nc.vector.tensor_tensor
            nc.vector.memset(M, 0.0).then_inc(s_mz, 1)
            for j in range(J):
                if j >= 2:
                    dve.wait_ge(s_k, 2 * (j - 1))
                nc.vector.tensor_copy(Brep[:, j % 2], e.Bc[:, :, j].unsqueeze(2).broadcast_to([P, 2, CH, SP])).then_inc(s_rep, 1)
            step(nc.vector.tensor_copy(a8, e.mag8.unsqueeze(2).broadcast_to([P, J, P])))
            step(nc.vector.memset(a8[:, :, 0:1], 0.0))
            step(nc.vector.memset(Sp[:, :, :, 0:1], 0.0))
            fl = lambda v: v.rearrange("p j c -> p (j c)")
            for b in range(4):
                dve.wait_ge(s_v, b + 1)
                s = slice(4 * b, 4 * b + 4)
                vr, vi = ps[:, 4 + b % 2, :], ps[:, 6 + b % 2, :]
                Er, Ei = fl(e.E[:, 0, s]), fl(e.E[:, 1, s])
                zr, zi = fl(z[:, 0, s]), fl(z[:, 1, s])
                step(TT(t1, vr, Er, ALU.mult))
                step(TT(t2, vi, Ei, ALU.mult))
                step(TT(zr, t1, t2, ALU.add))
                step(TT(t1, vi, Er, ALU.mult))
                step(TT(t2, vr, Ei, ALU.mult))
                TT(zi, t1, t2, ALU.subtract).then_inc(s_vd, 1)
                dve.wait_ge(s_vd, b + 1)
            for c in range(2):
                step(nc.vector.tensor_tensor_scan(fl(z[:, c]), fl(a8), fl(z[:, c]), 0.0, ALU.mult, ALU.add))
            T = a8
            step(TT(T, z[:, 1], e.E[:, 1], ALU.mult))
            step(TT(Sp[:, 0, :, 1:], z[:, 0], e.E[:, 0], ALU.mult))
            step(TT(Sp[:, 0, :, 1:], Sp[:, 0, :, 1:], T, ALU.subtract))
            step(TT(T, z[:, 1], e.E[:, 0], ALU.mult))
            step(TT(Sp[:, 1, :, 1:], z[:, 0], e.E[:, 1], ALU.mult))
            TT(Sp[:, 1, :, 1:], Sp[:, 1, :, 1:], T, ALU.add).then_inc(s_S, 1)
            dve.wait_ge(s_sh, 16 * CH)
            dve.wait_ge(s_in, 16 * CH)
            step(TT(K, e.ident.unsqueeze(1).broadcast_to([P, SG, P]), dd.unsqueeze(2).broadcast_to([P, SG, P]), ALU.mult))
            TT(M, M, K, ALU.add).then_inc(s_d, 1)
    A.give("M", "Brep", "a8", "z", "Sp", "t1", "t2", "Y", "d_skip", "Wr", "nWi", "Bc", "w_p2", "mag8")


def stage_glu(e):
    nc, A, ps = e.nc, e.arena, e.ps
    e.yT = A.take("yT", 4, L)
    w = A.take("w_g", 4, 512)
    b = A.take("b_g", 4)
    sg = A.take("sg", 2, 512)
    s_in, s_mm, s_sg, s_y = (e.sem(f"gl_{n}") for n in ("in", "mm", "sg", "y"))
    steps = [(m, n) for m in range(4) for n in range(2)]
    with nc.Block() as block:
        @block.sync
        def _(sp):
            sp.dma_start(w, e.in_["w_glu_2"][0].rearrange("(k p) n -> p k n", p=P)).then_inc(s_in, 16)
            with nc.allow_non_contiguous_dma("a bias by channel"):
                sp.dma_start(b, e.in_["b_glu_2"][0].rearrange("(k p) -> p k", p=P)).then_inc(s_in, 16)

        @block.tensor
        def _(pe):
            pe.wait_ge(s_in, 32)
            for i, (m, n) in enumerate(steps):
                for k in range(4):
                    ins = nc.tensor.matmul(ps[:, i, :], w[:, k, m * P:(m + 1) * P], e.ygT[:, k, n * 512:(n + 1) * 512], start=(k == 0), stop=(k == 3))
                ins.then_inc(s_mm, 1)

        @block.scalar
        def _(act):
            act.wait_ge(s_in, 32)
            for i, (m, n) in enumerate(steps):
                act.wait_ge(s_mm, i + 1)
                if i >= 2:
                    act.wait_ge(s_y, i - 1)
                nc.scalar.activation(sg[:, i % 2], ps[:, i, :], ACT.Sigmoid, bias=b[:, m:m + 1]).then_inc(s_sg, 1)

        @block.vector
        def _(dve):
            for i, (m, n) in enumerate(steps):
                dve.wait_ge(s_sg, i + 1)
                c = slice(n * 512, (n + 1) * 512)
                nc.vector.tensor_tensor(e.yT[:, m, c], e.ygT[:, m, c], sg[:, i % 2], ALU.mult).then_inc(s_y, 1)
    A.give("w_g", "b_g", "sg", "ygT")


def stage_heads(e):
    nc, A, ps = e.nc, e.arena, e.ps
    e.hd = A.take("hd", 8, L)
    G = 15
    gain = A.take("gain", G, HD)
    ss = A.take("ss", TL, G)
    sq = A.take("sq", 2, G * HD)
    dup = A.take("dup", 2, 4, HD)
    s_in, s_sq, s_ss, s_rt, s_own, s_n, s_tr, s_ev = (e.sem(f"hd_{n}") for n in ("in", "sq", "ss", "rt", "own", "n", "tr", "ev"))
    names = [("q_norm_g_2", i) for i in range(8)] + [("k_norm_g_2", 8), ("idx_k_norm_g_2", 14)]
    with nc.Block() as block:
        @block.sync
        def _(sp):
            for name, i in names:
                sp.dma_start(gain[:, i], broadcast_rows(e.in_[name][0])).then_inc(s_in, 16)

        @block.scalar
        def _(act):
            for t in range(TL):
                if t >= 2:
                    act.wait_ge(s_ss, t - 1)
                nc.scalar.activation(sq[:, t % 2], e.r[:, t, 0:G * HD], ACT.Square).then_inc(s_sq, 1)
            act.wait_ge(s_own, 2)
            nc.scalar.activation(ss, ss, ACT.Sqrt).then_inc(s_rt, 1)
            for t in range(TL):
                for j in range(2):
                    act.wait_ge(s_tr, 2 * t + j + 1)
                    nc.scalar.activation(e.hd[:, 4 * j:4 * j + 4, t * P:(t + 1) * P], ps[:, (2 * t + j) % 8, :].rearrange("p (a b) -> p a b", b=P), ACT.Copy).then_inc(s_ev, 1)

        @block.vector
        def _(dve):
            step = Steps(dve, s_own)
            step(nc.vector.memset(gain[:, 9:14], 1.0))
            for t in range(TL):
                dve.wait_ge(s_sq, t + 1)
                nc.vector.tensor_reduce(ss[:, t], sq[:, t % 2].rearrange("p (g c) -> p g c", c=HD), AX, ALU.add).then_inc(s_ss, 1)
            dve.wait_ge(s_ss, TL)
            step(nc.vector.tensor_scalar(ss, ss, 1.0 / HD, EPS, ALU.mult, ALU.add))
            dve.wait_ge(s_rt, 1)
            step(nc.vector.reciprocal(ss, ss))
            step(nc.vector.memset(ss[:, :, 9:14], 1.0))
            dve.wait_ge(s_in, 16 * len(names))
            for t in range(TL):
                v = e.r[:, t, 0:G * HD].rearrange("p (g c) -> p g c", c=HD)
                step(nc.vector.tensor_tensor(v, v, ss[:, t].unsqueeze(2).broadcast_to([P, G, HD]), ALU.mult))
                step(nc.vector.tensor_tensor(v, v, gain, ALU.mult))
                if t >= 2:
                    dve.wait_ge(s_tr, 2 * (t - 1))
                step(nc.vector.tensor_copy(dup[:, t % 2, 0:2], v[:, 8:9].broadcast_to([P, 2, HD])))
                nc.vector.tensor_copy(dup[:, t % 2, 2:4], v[:, 14:15].broadcast_to([P, 2, HD])).then_inc(s_n, 1)

        @block.tensor
        def _(pe):
            for t in range(TL):
                pe.wait_ge(s_n, t + 1)
                if t >= 4:
                    pe.wait_ge(s_ev, 2 * (t - 3))
                blocks = [e.r[:, t, RQ + i * P:RQ + (i + 1) * P] for i in range(4)] + [e.r[:, t, RQI + i * P:RQI + (i + 1) * P] for i in range(2)]
                blocks += [dup[:, t % 2, 2 * i:2 * i + 2].rearrange("p a b -> p (a b)") for i in range(2)]
                for i, b in enumerate(blocks):
                    ins = nc.tensor.transpose(ps[:, (2 * t + i // 4) % 8, (i % 4) * P:(i % 4 + 1) * P], b, e.ident)
                    if i % 4 == 3:
                        ins.then_inc(s_tr, 1)
    A.give("gain", "ss", "sq", "dup")


def stage_sparse(e):
    nc, A, ps = e.nc, e.arena, e.ps
    e.yaT = A.take("yaT", 4, L)
    bias = A.take("bias", sum(range(1, TL + 1)) * P)
    rel = A.take("rel", 2, 512)
    m8 = A.take("m8", 8)
    pr = A.take("pr", 2, L)
    pT = A.take("pT", 2, TL, P)
    sm = A.take("sm", 2, 3, HEADS)
    on = A.take("on", 2, HEADS * HD)
    hT = A.take("hT2", KD, L)
    wg = A.take("w_gates", 2, KD, P)
    go = A.take("gate_out", 2, 512)
    e.gates_dram = nc.dram_tensor("gates_scratch", (2 * KD, P, L), F32).ap()
    w_in = e.in_["w_in_2"][0].rearrange("(k p) n -> p k n", p=P)
    at = [sum(range(1, i + 1)) * P for i in range(TL)]
    B = lambda i: bias[:, at[i]:at[i] + (i + 1) * P]
    QI, KB, KI = 4, 6, 7
    REPL = -3e38
    rounds = TOPK // 8
    chosen = [i for i in range(TL) if (i + 1) * P > TOPK]
    turns = [i for i in range(TL) if i not in chosen] + chosen[::-1]
    idx_tasks = [(i, c, h) for i in chosen[::-1] for c in range(0, (i + 1) * P, 512) for h in range(IH)]
    s_mm, s_rel, s_acc, s_own, s_m8, s_mr, s_bias = (e.sem(f"sp_{n}") for n in ("mm", "rel", "acc", "own", "m8", "mr", "bias"))
    s_lg, s_pm, s_ex, s_tr, s_pT, s_pv, s_on, s_ot, s_o = (e.sem(f"sp_{n}") for n in ("lg", "pm", "ex", "tr", "pT", "pv", "on", "ot", "o"))
    heads = [(a, i, h) for a, i in enumerate(turns) for h in range(HEADS)]
    s_gh, s_gmm, s_gev = (e.sem(f"sp_{n}") for n in ("gh", "gmm", "gev"))
    s_gw, s_gst = ([e.sem(f"sp_{n}{i}") for i in range(2)] for n in ("gw", "gst"))
    GN = 2 * 2 * KD
    assert 2 * GN == len(heads)
    with nc.Block() as block:
        @block.sync
        def _(sp):
            def load(c):
                at = 512 + RN + c * P
                sp.dma_start(wg[:, c % 2], w_in[:, :, at:at + P]).then_inc(s_gw[c % 2], 16)
            load(0)
            sp.dma_start(hT.rearrange("p a b -> p (a b)"), e.hT_dram).then_inc(s_gh, 16)
            load(1)
            for q in range(GN):
                sp.wait_ge(s_gev, q + 1)
                sp.dma_start(e.gates_dram[q // 2, :, (q % 2) * 512:(q % 2 + 1) * 512], go[:, q % 2]).then_inc(s_gst[q % 2], 16)
                if q % 2 == 1 and q // 2 + 2 < 2 * KD:
                    load(q // 2 + 2)
            for i in range(2):
                sp.wait_ge(s_gst[i], 16 * GN // 2)

        @block.tensor
        def _(pe):
            for n, (i, c, h) in enumerate(idx_tasks):
                w = min(512, (i + 1) * P - c)
                hh = slice(64 * (h % 2), 64 * (h % 2) + 64)
                if n >= 4:
                    pe.wait_ge(s_rel, n - 3)
                nc.tensor.matmul(ps[:, n % 4, 0:w], e.hd[hh, QI + h // 2, i * P:(i + 1) * P], e.hd[hh, KI, c:c + w], start=True, stop=True).then_inc(s_mm, 1)

            def logits(n):
                a, i, h = heads[n]
                hh = slice(64 * (h % 2), 64 * (h % 2) + 64)
                if n >= 2:
                    pe.wait_ge(s_pm, n - 1)
                for c in range(0, (i + 1) * P, 512):
                    w = min(512, (i + 1) * P - c)
                    ins = nc.tensor.matmul(ps[:, 2 * (n % 2) + c // 512, 0:w], e.hd[hh, h // 2, i * P:(i + 1) * P], e.hd[hh, KB, c:c + w], start=True, stop=True)
                ins.then_inc(s_lg, 1)

            def gates(q, half):
                c, n = divmod(q, 2)
                if q == 0 and half == 0:
                    pe.wait_ge(s_gh, 16)
                if n == 0 and half == 0:
                    pe.wait_ge(s_gw[c % 2], 16 * (c // 2 + 1))
                if q and half == 0:
                    pe.wait_ge(s_gev, q)
                for k in range(4 * half, 4 * half + 4):
                    ins = nc.tensor.matmul(ps[:, 7, :], wg[:, c % 2, k], hT[:, k, n * 512:(n + 1) * 512], start=(k == 0), stop=(k == KD - 1))
                if half == 1:
                    ins.then_inc(s_gmm, 1)

            def values(n):
                a, i, h = heads[n]
                pe.wait_ge(s_ex, n + 1)
                if n >= 1:
                    pe.wait_ge(s_pT, n)
                if h >= 2 and a >= 1:
                    pe.wait_ge(s_o, a)
                for b in range(i + 1):
                    ins = nc.tensor.transpose(ps[:, 4 + b // 4, (b % 4) * P:(b % 4 + 1) * P], pr[:, n % 2, b * P:(b + 1) * P], e.ident)
                ins.then_inc(s_tr, 1)
                if n + 2 < len(heads):
                    logits(n + 2)
                gates(n // 2, n % 2)
                pe.wait_ge(s_pT, n + 1)
                if h == 0 and a >= 1:
                    pe.wait_ge(s_on, a)
                for b in range(i + 1):
                    ins = nc.tensor.matmul(ps[:, 6, h * HD:(h + 1) * HD], pT[:, n % 2, b], e.r[:, b, RV:RV + HD], start=(b == 0), stop=(b == i))
                ins.then_inc(s_pv, 1)

            def output(a, n):
                pe.wait_ge(s_on, a + 1)
                pe.wait_ge(s_pT, n)
                for k in range(4):
                    ins = nc.tensor.transpose(ps[:, 4, k * P:(k + 1) * P], on[:, a % 2, k * P:(k + 1) * P], e.ident)
                ins.then_inc(s_ot, 1)

            pe.wait_ge(s_rel, len(idx_tasks))
            logits(0)
            logits(1)
            for n in range(len(heads)):
                values(n)
                if n > HEADS and n % HEADS == 1:
                    output(n // HEADS - 1, n + 1)
            output(TL - 1, len(heads))

        @block.scalar
        def _(act):
            for n, (i, c, h) in enumerate(idx_tasks):
                w = min(512, (i + 1) * P - c)
                act.wait_ge(s_mm, n + 1)
                if n >= 2:
                    act.wait_ge(s_acc, n - 1)
                nc.scalar.activation(rel[:, n % 2, 0:w], ps[:, n % 4, 0:w], ACT.Relu, scale=IH ** -0.5 * HD ** -0.5).then_inc(s_rel, 1)

            def softmax(n):
                a, i, h = heads[n]
                act.wait_ge(s_pm, n + 1)
                nc.scalar.activation(pr[:, n % 2, 0:(i + 1) * P], pr[:, n % 2, 0:(i + 1) * P], ACT.Exp, bias=sm[:, a % 2, 1, h:h + 1],
                                     scale=HD ** -0.5, accum_out=sm[:, a % 2, 2, h:h + 1]).then_inc(s_ex, 1)

            def turned(n):
                a, i, h = heads[n]
                act.wait_ge(s_tr, n + 1)
                if n >= 2:
                    act.wait_ge(s_pv, n - 1)
                nc.scalar.activation(pT[:, n % 2, 0:i + 1], ps[:, 4:6, :].rearrange("p a (b c) -> p (a b) c", c=P)[:, 0:i + 1], ACT.Copy).then_inc(s_pT, 1)

            def output(a):
                act.wait_ge(s_ot, a + 1)
                i = turns[a]
                nc.scalar.activation(e.yaT[:, :, i * P:(i + 1) * P], ps[:, 4, :].rearrange("p (a b) -> p a b", b=P), ACT.Copy).then_inc(s_o, 1)

            def gates(q):
                act.wait_ge(s_gmm, q + 1)
                if q >= 2:
                    act.wait_ge(s_gst[q % 2], 16 * (q // 2))
                nc.scalar.activation(go[:, q % 2], ps[:, 7, :], ACT.Copy).then_inc(s_gev, 1)

            for n in range(len(heads) + 1):
                if n < len(heads):
                    softmax(n)
                if n >= 3 and n % 2 == 1:
                    gates((n - 3) // 2)
                if n >= 1:
                    turned(n - 1)
                if n > HEADS and n % HEADS == 2:
                    output(n // HEADS - 1)
            gates(GN - 1)
            output(TL - 1)

        @block.vector
        def _(dve):
            step = Steps(dve, s_own)
            for i in range(TL):
                if i not in chosen:
                    if i:
                        nc.vector.memset(B(i)[:, 0:i * P], 0.0)
                    nc.vector.tensor_copy(B(i)[:, i * P:], e.const("causal")).then_inc(s_bias, 1)
            for n, (i, c, h) in enumerate(idx_tasks):
                w = min(512, (i + 1) * P - c)
                dst = B(i)[:, c:c + w]
                wi = e.r[:, i, RWI + h:RWI + h + 1]
                dve.wait_ge(s_rel, n + 1)
                if h == 0:
                    nc.vector.tensor_scalar(dst, rel[:, n % 2, 0:w], wi, None, ALU.mult).then_inc(s_acc, 1)
                else:
                    dve.wait_ge(s_acc, n)
                    nc.vector.scalar_tensor_tensor(out=dst, in0=rel[:, n % 2, 0:w], scalar=wi, in1=dst, op0=ALU.mult, op1=ALU.add).then_inc(s_acc, 1)
            dve.wait_ge(s_acc, len(idx_tasks))
            for i in chosen:
                step(nc.vector.tensor_tensor(B(i)[:, i * P:], B(i)[:, i * P:], e.const("causal"), ALU.add))

            def choose(r):
                b = B(chosen[::-1][r // rounds])
                nc.vector.max(m8, b).then_inc(s_m8, 1)
                dve.wait_ge(s_m8, r + 1)
                nc.vector.match_replace(b, m8, b, REPL).then_inc(s_mr, 1)
                dve.wait_ge(s_mr, r + 1)
                if r % rounds == rounds - 1:
                    nc.vector.tensor_scalar(b, b, 0.5 * REPL, -BIG, ALU.is_gt, ALU.mult).then_inc(s_bias, 1)

            def attend(n):
                a, i, h = heads[n]
                w = (i + 1) * P
                if h == 0:
                    dve.wait_ge(s_bias, max(a + 1, TL - len(chosen)))
                dve.wait_ge(s_lg, n + 1)
                if n >= 2:
                    dve.wait_ge(s_tr, n - 1)
                step(nc.vector.tensor_tensor_reduce(out=pr[:, n % 2, 0:w], in0=ps[:, 2 * (n % 2):2 * (n % 2) + 2, :].rearrange("p a b -> p (a b)")[:, 0:w],
                                                    in1=B(i), scale=1.0, scalar=REPL, op0=ALU.add, op1=ALU.max, accum_out=sm[:, a % 2, 0, h:h + 1]))
                nc.vector.tensor_scalar(sm[:, a % 2, 1, h:h + 1], sm[:, a % 2, 0, h:h + 1], -HD ** -0.5, None, ALU.mult).then_inc(s_pm, 1)

            def finish(a):
                dve.wait_ge(s_ex, 8 * a + 8)
                step(nc.vector.reciprocal(sm[:, a % 2, 0], sm[:, a % 2, 2]))
                dve.wait_ge(s_pv, 8 * a + 8)
                nc.vector.tensor_tensor(on[:, a % 2].rearrange("p (h c) -> p h c", h=HEADS), ps[:, 6, :].rearrange("p (h c) -> p h c", h=HEADS),
                                        sm[:, a % 2, 0].unsqueeze(2).broadcast_to([P, HEADS, HD]), ALU.mult).then_inc(s_on, 1)

            r = 0
            free = TL - len(chosen)
            for n, (a, i, h) in enumerate(heads):
                attend(n)
                if h == 0 and a >= 1:
                    finish(a - 1)
                upto = rounds * (n + 1) // (free * HEADS) if a < free else rounds * (a - free + 1) + rounds * (h + 1) // HEADS
                while r < min(upto, rounds * len(chosen)):
                    choose(r)
                    r += 1
            finish(TL - 1)
    A.give("hT2", "w_gates", "gate_out", "bias", "rel", "m8", "pr", "pT", "sm", "on", "hd", "r")


def stage_merge(e):
    nc, A, ps = e.nc, e.arena, e.ps
    e.merged = A.take("merged", KD, L)
    wp = A.take("w_proj", 2, 4, D)
    NG = 4
    gt = A.take("gates", NG, 2, 512)
    s_p = [e.sem(f"mg_p{i}") for i in range(2)]
    s_mm, s_sg, s_m1, s_out = (e.sem(f"mg_{n}") for n in ("mm", "sg", "m1", "out"))
    s_g = [e.sem(f"mg_g{i}") for i in range(NG)]
    steps = [(m, n) for m in range(KD) for n in range(2)]
    with nc.Block() as block:
        @block.sync
        def _(sp):
            def gates(i):
                m, n = steps[i]
                for g in range(2):
                    sp.dma_start(gt[:, i % NG, g], e.gates_dram[g * KD + m, :, n * 512:(n + 1) * 512]).then_inc(s_g[i % NG], 16)
            gates(0)
            for g, name in enumerate(("w_proj_ssm_2", "w_proj_attn_2")):
                sp.dma_start(wp[:, g], e.in_[name][0].rearrange("(k p) n -> p k n", p=P)).then_inc(s_p[g], 16)
            for i in range(1, len(steps)):
                if i >= NG:
                    sp.wait_ge(s_out, i - NG + 1)
                gates(i)

        @block.tensor
        def _(pe):
            for i, (m, n) in enumerate(steps):
                if i >= 4:
                    pe.wait_ge(s_m1, i - 3)
                for g, y in enumerate((e.yT, e.yaT)):
                    if i == 0:
                        pe.wait_ge(s_p[g], 16)
                    for k in range(4):
                        ins = nc.tensor.matmul(ps[:, 2 * (i % 4) + g, :], wp[:, g, k, m * P:(m + 1) * P], y[:, k, n * 512:(n + 1) * 512], start=(k == 0), stop=(k == 3))
                ins.then_inc(s_mm, 1)

        @block.scalar
        def _(act):
            for i in range(len(steps)):
                act.wait_ge(s_g[i % NG], 32 * (i // NG + 1))
                nc.scalar.activation(gt[:, i % NG], gt[:, i % NG], ACT.Sigmoid).then_inc(s_sg, 1)

        @block.vector
        def _(dve):
            for i, (m, n) in enumerate(steps):
                dve.wait_ge(s_sg, i + 1)
                dve.wait_ge(s_mm, i + 1)
                nc.vector.tensor_tensor(gt[:, i % NG], gt[:, i % NG], ps[:, 2 * (i % 4):2 * (i % 4) + 2, :], ALU.mult).then_inc(s_m1, 1)
                dve.wait_ge(s_m1, i + 1)
                nc.vector.tensor_tensor(e.merged[:, m, n * 512:(n + 1) * 512], gt[:, i % NG, 0], gt[:, i % NG, 1], ALU.add).then_inc(s_out, 1)
    A.give("w_proj", "gates", "yT", "yaT")


def stage_out2(e):
    nc, A, ps = e.nc, e.arena, e.ps
    e.x4 = A.take("x4", TL, D, high=True)
    e.hT3 = A.take("hT3", KD, L, high=True)
    w, s_w = A.take("w_o2", KD, D), e.sem("o2_w")
    e.w_ffn, e.s_wffn = A.take("w_ffn", 2, 2, KD, 256, high=True), [e.keep_sem(f"fu_w{i}") for i in range(2)]
    xr = A.take("x_ring", 2, D)
    g = A.take("gain", D)
    h = A.take("h", 2, D)
    junk = A.take("junk", D)
    ss = A.take("ss", TL)
    s_x = [e.sem(f"o2_xin{i}") for i in range(2)]
    s_g, s_mm, s_x4, s_sq, s_var, s_rt, s_own, s_h, s_tr, s_ev = (e.sem(f"o2_{n}") for n in ("g", "mm", "x4", "sq", "var", "rt", "own", "h", "tr", "ev"))
    two = lambda v: v.rearrange("p (a n) -> p a n", a=2)
    with nc.Block() as block:
        @block.sync
        def _(sp):
            sp.dma_start(w, e.in_["w_out_2"][0].rearrange("(k p) n -> p k n", p=P)).then_inc(s_w, 16)
            sp.dma_start(g, broadcast_rows(e.in_["norm2_g_2"][0])).then_inc(s_g, 16)
            for t in range(TL):
                if t >= 2:
                    sp.wait_ge(s_x4, t - 1)
                sp.dma_start(xr[:, t % 2], e.x3_dram[t * P:(t + 1) * P, :]).then_inc(s_x[t % 2], 16)
            for c in range(2):
                for i, name in enumerate(("w_ffn_gate_2", "w_ffn_up_2")):
                    src = e.in_[name][0].rearrange("(k p) n -> p k n", p=P)
                    sp.dma_start(e.w_ffn[:, c, i], src[:, :, c * 256:(c + 1) * 256]).then_inc(e.s_wffn[c], 16)

        @block.tensor
        def _(pe):
            pe.wait_ge(s_w, 16)
            for t in range(TL):
                if t >= 4:
                    pe.wait_ge(s_x4, t - 3)
                for j in range(2):
                    for k in range(KD):
                        ins = nc.tensor.matmul(ps[:, 2 * (t % 4) + j, :], e.merged[:, k, t * P:(t + 1) * P], w[:, k, j * 512:(j + 1) * 512], start=(k == 0), stop=(k == KD - 1))
                ins.then_inc(s_mm, 1)
            pe.wait_ge(s_x4, TL)
            for t in range(TL):
                pe.wait_ge(s_h, t + 1)
                if t >= 4:
                    pe.wait_ge(s_ev, 2 * (t - 3))
                for k in range(KD):
                    ins = nc.tensor.transpose(ps[:, (2 * t + k // 4) % 8, (k % 4) * P:(k % 4 + 1) * P], h[:, t % 2, k * P:(k + 1) * P], e.ident)
                    if k % 4 == 3:
                        ins.then_inc(s_tr, 1)

        @block.scalar
        def _(act):
            for t in range(TL):
                act.wait_ge(s_x4, t + 1)
                if t:
                    act.wait_ge(s_sq, t)
                nc.scalar.activation(junk, e.x4[:, t], ACT.Square, accum_out=ss[:, t:t + 1]).then_inc(s_sq, 1)
            act.wait_ge(s_var, 1)
            nc.scalar.activation(ss, ss, ACT.Sqrt).then_inc(s_rt, 1)
            for t in range(TL):
                for j in range(2):
                    act.wait_ge(s_tr, 2 * t + j + 1)
                    nc.scalar.activation(e.hT3[:, 4 * j:4 * j + 4, t * P:(t + 1) * P], ps[:, (2 * t + j) % 8, :].rearrange("p (a b) -> p a b", b=P), ACT.Copy).then_inc(s_ev, 1)

        @block.vector
        def _(dve):
            step = Steps(dve, s_own)
            for t in range(TL):
                dve.wait_ge(s_mm, t + 1)
                dve.wait_ge(s_x[t % 2], 16 * (t // 2 + 1))
                nc.vector.tensor_tensor(two(e.x4[:, t]), two(xr[:, t % 2]), ps[:, 2 * (t % 4):2 * (t % 4) + 2, :], ALU.add).then_inc(s_x4, 1)
            dve.wait_ge(s_sq, TL)
            step(nc.vector.tensor_scalar(ss, ss, 1.0 / D, EPS, ALU.mult, ALU.add))
            nc.vector.reciprocal(ss, ss).then_inc(s_var, 1)
            dve.wait_ge(s_rt, 1)
            dve.wait_ge(s_g, 16)
            for t in range(TL):
                if t >= 2:
                    dve.wait_ge(s_tr, 2 * (t - 1))
                nc.vector.scalar_tensor_tensor(out=h[:, t % 2], in0=e.x4[:, t], scalar=ss[:, t:t + 1], in1=g, op0=ALU.mult, op1=ALU.mult).then_inc(s_h, 1)
    A.give("merged", "w_o2", "x_ring", "gain", "h", "junk", "ss")


def stage_ffn_up(e):
    nc, A, ps = e.nc, e.arena, e.ps
    MB = DFF // P
    e.hid = A.take("hid", MB, L)
    w, s_w = e.w_ffn, e.s_wffn
    sg = A.take("sg", 2, 512)
    s_mm, s_sg, s_h = e.sem("fu_mm"), e.sem("fu_sg"), e.sem("fu_h")
    steps = [(m, n) for m in range(MB) for n in range(2)]
    src = [e.in_[n][0].rearrange("(k p) n -> p k n", p=P) for n in ("w_ffn_gate_2", "w_ffn_up_2")]
    with nc.Block() as block:
        @block.sync
        def _(sp):
            for c in range(2, MB // 2):
                sp.wait_ge(s_mm, 4 * (c - 1))
                for g in range(2):
                    sp.dma_start(w[:, c % 2, g], src[g][:, :, c * 256:(c + 1) * 256]).then_inc(s_w[c % 2], 16)

        @block.tensor
        def _(pe):
            for i, (m, n) in enumerate(steps):
                c = m // 2
                if i % 4 == 0:
                    pe.wait_ge(s_w[c % 2], 32 * (c // 2 + 1))
                if i >= 4:
                    pe.wait_ge(s_h, i - 3)
                for g in range(2):
                    for k in range(KD):
                        ins = nc.tensor.matmul(ps[:, 2 * (i % 4) + g, :], w[:, c % 2, g, k, (m % 2) * P:(m % 2 + 1) * P], e.hT3[:, k, n * 512:(n + 1) * 512],
                                               start=(k == 0), stop=(k == KD - 1))
                ins.then_inc(s_mm, 1)

        @block.scalar
        def _(act):
            for i in range(len(steps)):
                act.wait_ge(s_mm, i + 1)
                if i >= 2:
                    act.wait_ge(s_h, i - 1)
                nc.scalar.activation(sg[:, i % 2], ps[:, 2 * (i % 4), :], ACT.Silu).then_inc(s_sg, 1)

        @block.vector
        def _(dve):
            for i, (m, n) in enumerate(steps):
                dve.wait_ge(s_sg, i + 1)
                nc.vector.tensor_tensor(e.hid[:, m, n * 512:(n + 1) * 512], sg[:, i % 2], ps[:, 2 * (i % 4) + 1, :], ALU.mult).then_inc(s_h, 1)
    A.give("w_ffn", "sg", "hT3")


def stage_ffn_down(e):
    nc, A, ps = e.nc, e.arena, e.ps
    MB = DFF // P
    NW = 3
    w = A.take("w_ring", NW, 2, 512)
    o = A.take("o_ring", 4, 512)
    s_w = [e.sem(f"fd_w{i}") for i in range(NW)]
    s_o = [e.keep_sem(f"fd_o{i}") for i in range(4)]
    s_mm, s_acc, s_out = e.sem("fd_mm"), e.sem("fd_acc"), e.sem("fd_out")
    chunks = [(j, c) for j in range(2) for c in range(MB // 2)]
    src = e.in_["w_ffn_down_2"][0].rearrange("(k p) n -> p k n", p=P)
    with nc.Block() as block:
        @block.sync
        def _(sp):
            for i, (j, c) in enumerate(chunks):
                if i >= NW:
                    sp.wait_ge(s_mm, i - NW + 1)
                sp.dma_start(w[:, i % NW], src[:, 2 * c:2 * c + 2, j * 512:(j + 1) * 512]).then_inc(s_w[i % NW], 16)

        @block.gpsimd
        def _(pool):
            for i in range(2 * TL):
                j, t = divmod(i, TL)
                pool.wait_ge(s_out, i + 1)
                pool.dma_start(e.out[0, t * P:(t + 1) * P, j * 512:(j + 1) * 512], o[:, i % 4]).then_inc(s_o[i % 4], 16)
            for i in range(4):
                pool.wait_ge(s_o[i], 16 * 4)

        @block.tensor
        def _(pe):
            for i, (j, c) in enumerate(chunks):
                pe.wait_ge(s_w[i % NW], 16 * (i // NW + 1))
                for k in range(2):
                    for t in range(TL):
                        if j == 1 and c == 0 and k == 0:
                            pe.wait_ge(s_out, t + 1)
                        ins = nc.tensor.matmul(ps[:, t, :], e.hid[:, 2 * c + k, t * P:(t + 1) * P], w[:, i % NW, k], start=(c == 0 and k == 0), stop=(c == MB // 2 - 1 and k == 1))
                        if c == MB // 2 - 1 and k == 1:
                            ins.then_inc(s_acc, 1)
                        elif k == 1 and t == TL - 1:
                            ins.then_inc(s_mm, 1)
                if c == MB // 2 - 1 and j == 0:
                    pe.wait_ge(s_acc, TL)
                    pe.sem_inc(s_mm, 1)

        @block.vector
        def _(dve):
            for i in range(2 * TL):
                j, t = divmod(i, TL)
                dve.wait_ge(s_acc, i + 1)
                if i >= 4:
                    dve.wait_ge(s_o[i % 4], 16 * (i // 4))
                nc.vector.tensor_tensor(o[:, i % 4], e.x4[:, t, j * 512:(j + 1) * 512], ps[:, t, :], ALU.add).then_inc(s_out, 1)
    A.give("w_ring", "o_ring", "hid", "x4")


STAGES = [stage_modulation, stage_norm1, stage_da_project, stage_da, stage_gdn_project, stage_gdn, stage_gdn_out, stage_rows,
          stage_out_router, stage_choose, stage_experts, stage_between, stage_project2,
          stage_ssm, stage_glu, stage_heads, stage_sparse,
          stage_merge, stage_out2, stage_ffn_up, stage_ffn_down]


def build(nc, in_, out):
    e = Env()
    e.nc, e.in_, e.out = nc, in_, out
    with ExitStack() as ctx:
        words = 53000
        tensor = ctx.enter_context(nc.sbuf_tensor("arena", [P, words], F32))
        e.ps = ctx.enter_context(nc.psum_tensor("psum", [P, 8, 512], F32))
        e.arena = Arena(tensor, words)
        _, names, _ = constant_tables()
        width = sum(n for _, n in names.values())
        e.consts = e.arena.take("consts", width)
        e.const = lambda name: e.consts[:, names[name][0]:names[name][0] + names[name][1]]
        e.ident = e.const("ident")
        e.shift1 = e.arena.take("shift1", KD, 2)
        e.scale1 = e.arena.take("scale1", KD, 2)
        e.eps = e.const("eps")
        e.catA = e.arena.take("catA", 4, L)
        e.hT = e.arena.take("hT", KD, LA)
        e.keep_sem = nc.alloc_semaphore
        e.keep_sem = nc.alloc_semaphore
        for stage in STAGES:
            own = []
            e.sem = lambda name: own.append(nc.alloc_semaphore(name)) or own[-1]
            stage(e)
            for sem in own:
                nc.gpsimd.sem_clear(sem)
                nc.release_semaphore(sem)


def make_inputs(nc, inputs):
    tables, _, rope = constant_tables()
    arrays, aps = {}, {}
    for name, a in list(inputs.items()) + [("tables", tables), ("rope", rope)]:
        a = np.ascontiguousarray(a)
        arrays[f"in_{name}_dram"] = a
        aps[name] = nc.dram_tensor(f"in_{name}_dram", a.shape, mybir.dt.from_np(a.dtype), kind="ExternalInput").ap()
    return arrays, aps


def kernel(**inputs):
    import concourse.bacc as bacc
    from concourse.bass_utils import run_bass_kernel_spmd

    nc = bacc.Bacc("TRN2", target_bir_lowering=False, num_devices=1)
    arrays, aps = make_inputs(nc, inputs)
    out = nc.dram_tensor("out_0_dram", (1, L, D), F32, kind="ExternalOutput").ap()
    build(nc, aps, out)
    result = run_bass_kernel_spmd(nc, [arrays], core_ids=[0])
    return result.results[0]["out_0_dram"]
```
